# Optimizing a Trainium2 kernel written in Bass

```python
import jax
import jax.numpy as jnp
from jax import lax
import numpy as np
import jax, jax.numpy as jnp

D_MODEL = 2048
BATCH = 1
SEQ = 256
DEPTH = 1

HEAD_DIM = 128
SB_HEADS = 8
DSA_HEADS = 8
IDX_HEADS = 16
IDX_DIM = 64
TOPK_MAX = 256
D_FF = 5632
CONV_WIDTH = 3
Q_BLOCK = 128
ROPE_THETA = 10000.0
NORM_EPS = 1e-6
N_MOD = 6
SB_WIDTH = SB_HEADS * HEAD_DIM
DSA_WIDTH = DSA_HEADS * HEAD_DIM
IDX_Q_WIDTH = IDX_HEADS * IDX_DIM
IN_SPLIT_SIZES = (SB_WIDTH, SB_WIDTH, SB_WIDTH, DSA_WIDTH, DSA_WIDTH, DSA_WIDTH,
                  IDX_Q_WIDTH, IDX_DIM, IDX_HEADS, D_MODEL, D_MODEL)
IN_WIDTH = 3 * SB_WIDTH + 3 * DSA_WIDTH + IDX_Q_WIDTH + IDX_DIM + IDX_HEADS + 2 * D_MODEL


def rmsnorm(x, g):
    xf = x.astype(jnp.float32)
    r = xf * lax.rsqrt(jnp.mean(xf * xf, axis=-1, keepdims=True) + NORM_EPS)
    return (r * g.astype(jnp.float32)).astype(x.dtype)

def rope(t, pos):
    d = t.shape[-1]
    inv_freq = 1.0 / (ROPE_THETA ** (jnp.arange(0, d, 2, dtype=jnp.float32) / d))
    ang = pos.astype(jnp.float32)[..., None] * inv_freq
    cos = jnp.cos(ang)[:, :, None, :]
    sin = jnp.sin(ang)[:, :, None, :]
    tf = t.astype(jnp.float32)
    t1, t2 = tf[..., : d // 2], tf[..., d // 2:]
    return jnp.concatenate([t1 * cos - t2 * sin, t2 * cos + t1 * sin], axis=-1).astype(t.dtype)

def stick_breaking_attention(q, k, v):
    B, S, H, dh = q.shape
    nb = S // Q_BLOCK
    scale = dh ** -0.5
    kpos = jnp.arange(S)
    qb = q.reshape(B, nb, Q_BLOCK, H, dh).transpose(1, 0, 2, 3, 4)

    def block(args):
        q_blk, start = args
        z = jnp.einsum('bqhd,bkhd->bhqk', q_blk, k,
                       preferred_element_type=jnp.float32) * scale
        qpos = start + jnp.arange(Q_BLOCK)
        past = (kpos[None, :] < qpos[:, None])[None, None]
        log1m = jnp.where(past, -jax.nn.softplus(z), 0.0)
        after = lax.cumsum(log1m, axis=3, reverse=True) - log1m
        w = jnp.where(past, jnp.exp(jax.nn.log_sigmoid(z) + after), 0.0)
        return jnp.einsum('bhqk,bkhd->bqhd', w.astype(v.dtype), v)

    starts = jnp.arange(nb, dtype=jnp.int32) * Q_BLOCK
    out = lax.map(block, (qb, starts))
    return out.transpose(1, 0, 2, 3, 4).reshape(B, S, H, dh)

def dsa_attention(q, k, v, qi, ki, wi):
    B, S, H, dh = q.shape
    nb = S // Q_BLOCK
    topk = min(TOPK_MAX, S // 4)
    kpos = jnp.arange(S)
    starts = jnp.arange(nb, dtype=jnp.int32) * Q_BLOCK

    def per_seq(args):
        q_s, k_s, v_s, qi_s, ki_s, wi_s = args
        q_blocks = q_s.reshape(nb, Q_BLOCK, H, dh)
        qi_blocks = qi_s.reshape(nb, Q_BLOCK, IDX_HEADS, IDX_DIM)
        wi_blocks = wi_s.reshape(nb, Q_BLOCK, IDX_HEADS)

        def block(bargs):
            q_b, qi_b, wi_b, start = bargs
            qpos = start + jnp.arange(Q_BLOCK)
            dots = jnp.einsum('qhi,ki->qhk', qi_b, ki_s,
                              preferred_element_type=jnp.float32) * (IDX_DIM ** -0.5)
            score = jnp.einsum('qh,qhk->qk', wi_b.astype(jnp.float32),
                               jax.nn.relu(dots)) * (IDX_HEADS ** -0.5)
            visible = kpos[None, :] <= qpos[:, None]
            score = jnp.where(visible, score, -jnp.inf)
            _, idx = lax.top_k(score, topk)
            k_sel = k_s[idx]
            v_sel = v_s[idx]
            logits = jnp.einsum('qhd,qkhd->qhk', q_b, k_sel,
                                preferred_element_type=jnp.float32) * (dh ** -0.5)
            valid = (idx <= qpos[:, None])[:, None, :]
            p = jax.nn.softmax(jnp.where(valid, logits, -jnp.inf), axis=-1)
            return jnp.einsum('qhk,qkhd->qhd', p.astype(v_s.dtype), v_sel)

        out = lax.map(block, (q_blocks, qi_blocks, wi_blocks, starts))
        return out.reshape(S, H, dh)

    return lax.map(per_seq, (q, k, v, qi, ki, wi))

def mixer(h, pos, w_in, w_a, w_b, w_o):
    B, S, _ = h.shape
    proj = h @ w_in
    offsets = [int(o) for o in np.cumsum(IN_SPLIT_SIZES)[:-1]]
    q_a, k_a, v_a, q_b, k_b, v_b, qi, ki, wi, g_a, g_b = jnp.split(proj, offsets, axis=-1)
    y_a = stick_breaking_attention(q_a.reshape(B, S, SB_HEADS, HEAD_DIM),
                                   k_a.reshape(B, S, SB_HEADS, HEAD_DIM),
                                   v_a.reshape(B, S, SB_HEADS, HEAD_DIM))
    y_a = y_a.reshape(B, S, SB_WIDTH) @ w_a
    y_b = dsa_attention(rope(q_b.reshape(B, S, DSA_HEADS, HEAD_DIM), pos),
                        rope(k_b.reshape(B, S, DSA_HEADS, HEAD_DIM), pos),
                        v_b.reshape(B, S, DSA_HEADS, HEAD_DIM),
                        rope(qi.reshape(B, S, IDX_HEADS, IDX_DIM), pos),
                        rope(ki[:, :, None, :], pos)[:, :, 0, :],
                        wi)
    y_b = y_b.reshape(B, S, DSA_WIDTH) @ w_b
    merged = jax.nn.sigmoid(g_a) * y_a + jax.nn.sigmoid(g_b) * y_b
    return merged @ w_o

def conv_ffn(h, w_up, conv_w, conv_b, w_down):
    u = h @ w_up
    S = u.shape[1]
    up = jnp.pad(u, ((0, 0), (CONV_WIDTH - 1, 0), (0, 0)))
    u = conv_b + sum(conv_w[i] * up[:, i:i + S] for i in range(CONV_WIDTH))
    a, b = jnp.split(u, 2, axis=-1)
    return (jax.nn.silu(a) * b) @ w_down

def first_inputs(seed: int = 0) -> dict:
    key = jax.random.key(seed)
    ks = jax.random.split(key, 16)
    f32 = jnp.float32

    def nrm(k, shape, scale):
        return jax.random.normal(k, shape, f32) * scale

    x = nrm(ks[0], (BATCH, SEQ, D_MODEL), 1.0)
    c = nrm(ks[1], (BATCH, D_MODEL), 1.0)
    offset = jax.random.randint(ks[2], (BATCH, 1), 0, 4096, dtype=jnp.int32)
    positions = offset + jnp.arange(SEQ, dtype=jnp.int32)[None, :]
    w_in = nrm(ks[3], (DEPTH, D_MODEL, IN_WIDTH), D_MODEL ** -0.5)
    w_a = nrm(ks[4], (DEPTH, SB_WIDTH, D_MODEL), SB_WIDTH ** -0.5)
    w_b = nrm(ks[5], (DEPTH, DSA_WIDTH, D_MODEL), DSA_WIDTH ** -0.5)
    w_o = nrm(ks[6], (DEPTH, D_MODEL, D_MODEL), D_MODEL ** -0.5)
    w_ada = nrm(ks[7], (DEPTH, D_MODEL, N_MOD * D_MODEL), 0.1 * D_MODEL ** -0.5)
    b_ada = nrm(ks[8], (DEPTH, N_MOD * D_MODEL), 0.01)
    g_mix = 1.0 + nrm(ks[9], (DEPTH, D_MODEL), 0.02)
    g_ffn = 1.0 + nrm(ks[10], (DEPTH, D_MODEL), 0.02)
    w_up = nrm(ks[11], (DEPTH, D_MODEL, 2 * D_FF), D_MODEL ** -0.5)
    conv_w = nrm(ks[12], (DEPTH, CONV_WIDTH, 2 * D_FF), CONV_WIDTH ** -0.5)
    conv_b = nrm(ks[13], (DEPTH, 2 * D_FF), 0.01)
    w_down = nrm(ks[14], (DEPTH, D_FF, D_MODEL), D_FF ** -0.5)
    g_final = 1.0 + nrm(ks[15], (D_MODEL,), 0.02)
    return {"x": x, "c": c, "positions": positions, "w_in": w_in, "w_a": w_a, "w_b": w_b,
            "w_o": w_o, "w_ada": w_ada, "b_ada": b_ada, "g_mix": g_mix, "g_ffn": g_ffn,
            "w_up": w_up, "conv_w": conv_w, "conv_b": conv_b, "w_down": w_down,
            "g_final": g_final}

def first_block(x, c, positions, w_in, w_a, w_b, w_o, w_ada, b_ada, g_mix, g_ffn,
              w_up, conv_w, conv_b, w_down, g_final):
    c_act = jax.nn.silu(c)
    for layer in range(DEPTH):
        mod = c_act @ w_ada[layer] + b_ada[layer]
        sh1, sc1, gt1, sh2, sc2, gt2 = jnp.split(mod[:, None, :], N_MOD, axis=-1)
        h = rmsnorm(x, g_mix[layer]) * (1 + sc1) + sh1
        x = x + (1 + gt1) * mixer(h, positions, w_in[layer], w_a[layer], w_b[layer], w_o[layer])
        h = rmsnorm(x, g_ffn[layer]) * (1 + sc2) + sh2
        x = x + (1 + gt2) * conv_ffn(h, w_up[layer], conv_w[layer], conv_b[layer], w_down[layer])
    return rmsnorm(x, g_final)


N_MIXERS = 2
GRID_W = 64
N_HEADS = 16
HEAD_DIM_2 = D_MODEL // N_HEADS
WIN_H_MAX = 8
WIN_W = 16
CONV_WIDTH_2 = 31
D_FF_2 = 4 * D_MODEL
N_CONV_LAYERS = (DEPTH + N_MIXERS - 1) // N_MIXERS
N_NA_LAYERS = DEPTH // N_MIXERS
NORM_EPS_2 = 1e-5


def rms_norm(x, g):
    xf = x.astype(jnp.float32)
    y = xf * lax.rsqrt(jnp.mean(xf * xf, axis=-1, keepdims=True) + NORM_EPS_2)
    return (y * g.astype(jnp.float32)).astype(x.dtype)

def layer_norm(x, g, b):
    xf = x.astype(jnp.float32)
    mu = jnp.mean(xf, axis=-1, keepdims=True)
    xc = xf - mu
    y = xc * lax.rsqrt(jnp.mean(xc * xc, axis=-1, keepdims=True) + NORM_EPS_2)
    return (y * g.astype(jnp.float32) + b.astype(jnp.float32)).astype(x.dtype)

def conformer_conv(h, w_pw1, b_pw1, w_dw, b_dw, ln_g, ln_b, w_pw2, b_pw2):
    u = h @ w_pw1 + b_pw1
    a, gate = jnp.split(u, 2, axis=-1)
    u = a * jax.nn.sigmoid(gate)
    u = lax.conv_general_dilated(
        u, w_dw[:, None, :], window_strides=(1,),
        padding=[(CONV_WIDTH_2 // 2, CONV_WIDTH_2 // 2)],
        dimension_numbers=("NWC", "WIO", "NWC"),
        feature_group_count=D_MODEL) + b_dw
    u = jax.nn.silu(layer_norm(u, ln_g, ln_b))
    return u @ w_pw2 + b_pw2

def neighbourhood_attention(h, w_qkv, b_qkv, rpb, w_o, b_o):
    bsz, t, _ = h.shape
    rows = t // GRID_W
    kh = min(WIN_H_MAX, rows)
    qkv = (h @ w_qkv + b_qkv).reshape(bsz, rows, GRID_W, 3, N_HEADS, HEAD_DIM_2)
    q = qkv[:, :, :, 0] * (HEAD_DIM_2 ** -0.5)
    k = qkv[:, :, :, 1]
    v = qkv[:, :, :, 2]
    row_ids = jnp.arange(rows, dtype=jnp.int32)
    row_start = jnp.clip(row_ids - kh // 2, 0, rows - kh)
    col_ids = jnp.arange(GRID_W, dtype=jnp.int32)
    col_start = jnp.clip(col_ids - WIN_W // 2, 0, GRID_W - WIN_W)
    col_idx = col_start[:, None] + jnp.arange(WIN_W, dtype=jnp.int32)[None, :]
    col_bias_idx = col_idx - col_ids[:, None] + (WIN_W - 1)
    rpb_cols = rpb[:, :, col_bias_idx]

    def row_block(r):
        rs = row_start[r]
        q_r = lax.dynamic_index_in_dim(q, r, axis=1, keepdims=False)
        k_band = lax.dynamic_slice_in_dim(k, rs, kh, axis=1)
        v_band = lax.dynamic_slice_in_dim(v, rs, kh, axis=1)
        k_win = k_band[:, :, col_idx]
        v_win = v_band[:, :, col_idx]
        row_bias_idx = rs + jnp.arange(kh, dtype=jnp.int32) - r + (WIN_H_MAX - 1)
        bias = jnp.transpose(rpb_cols[:, row_bias_idx], (0, 2, 1, 3))
        s = jnp.einsum("bqhd,biqjhd->bhqij", q_r, k_win) + bias[None]
        p = jax.nn.softmax(
            s.astype(jnp.float32).reshape(bsz, N_HEADS, GRID_W, kh * WIN_W), axis=-1)
        p = p.reshape(s.shape).astype(v.dtype)
        return jnp.einsum("bhqij,biqjhd->bqhd", p, v_win)

    o = lax.map(row_block, row_ids)
    o = jnp.moveaxis(o, 0, 1).reshape(bsz, t, D_MODEL)
    return o @ w_o + b_o

def sq_relu_mlp(h, w_up, w_down):
    return jnp.square(jax.nn.relu(h @ w_up)) @ w_down

def second_inputs(seed: int = 0) -> dict:
    key = jax.random.key(seed)
    ks = jax.random.split(key, 24)

    def nrm(k, shape, scale):
        return jax.random.normal(k, shape, jnp.float32) * scale

    d = D_MODEL
    return {
        "x": nrm(ks[0], (BATCH, SEQ, d), 1.0),
        "norm_mix_g": 1.0 + nrm(ks[1], (DEPTH, d), 0.02),
        "norm_ffn_g": 1.0 + nrm(ks[2], (DEPTH, d), 0.02),
        "final_norm_g": 1.0 + nrm(ks[3], (d,), 0.02),
        "conv_w_pw1": nrm(ks[4], (N_CONV_LAYERS, d, 2 * d), d ** -0.5),
        "conv_b_pw1": nrm(ks[5], (N_CONV_LAYERS, 2 * d), 0.02),
        "conv_w_dw": nrm(ks[6], (N_CONV_LAYERS, CONV_WIDTH_2, d), CONV_WIDTH_2 ** -0.5),
        "conv_b_dw": nrm(ks[7], (N_CONV_LAYERS, d), 0.02),
        "conv_ln_g": 1.0 + nrm(ks[8], (N_CONV_LAYERS, d), 0.02),
        "conv_ln_b": nrm(ks[9], (N_CONV_LAYERS, d), 0.02),
        "conv_w_pw2": nrm(ks[10], (N_CONV_LAYERS, d, d), d ** -0.5),
        "conv_b_pw2": nrm(ks[11], (N_CONV_LAYERS, d), 0.02),
        "na_w_qkv": nrm(ks[12], (N_NA_LAYERS, d, 3 * d), d ** -0.5),
        "na_b_qkv": nrm(ks[13], (N_NA_LAYERS, 3 * d), 0.02),
        "na_rpb": nrm(ks[14], (N_NA_LAYERS, N_HEADS, 2 * WIN_H_MAX - 1, 2 * WIN_W - 1), 0.1),
        "na_w_o": nrm(ks[15], (N_NA_LAYERS, d, d), d ** -0.5),
        "na_b_o": nrm(ks[16], (N_NA_LAYERS, d), 0.02),
        "ffn_w_up": nrm(ks[17], (DEPTH, d, D_FF_2), d ** -0.5),
        "ffn_w_down": nrm(ks[18], (DEPTH, D_FF_2, d), D_FF_2 ** -0.5),
    }

def second_block(x, norm_mix_g, norm_ffn_g, final_norm_g,
              conv_w_pw1, conv_b_pw1, conv_w_dw, conv_b_dw, conv_ln_g, conv_ln_b,
              conv_w_pw2, conv_b_pw2,
              na_w_qkv, na_b_qkv, na_rpb, na_w_o, na_b_o,
              ffn_w_up, ffn_w_down):
    h = x
    for i in range(DEPTH):
        j = i // N_MIXERS
        hn = rms_norm(h, norm_mix_g[i])
        if i % N_MIXERS == 0:
            h = h + conformer_conv(hn, conv_w_pw1[j], conv_b_pw1[j], conv_w_dw[j],
                                   conv_b_dw[j], conv_ln_g[j], conv_ln_b[j],
                                   conv_w_pw2[j], conv_b_pw2[j])
        else:
            h = h + neighbourhood_attention(hn, na_w_qkv[j], na_b_qkv[j], na_rpb[j],
                                            na_w_o[j], na_b_o[j])
        h = h + sq_relu_mlp(rms_norm(h, norm_ffn_g[i]), ffn_w_up[i], ffn_w_down[i])
    return rms_norm(h, final_norm_g)


def setup_inputs(seed=0):
    out = dict(first_inputs(seed))
    for name, value in second_inputs(seed + 1).items():
        if name != "x":
            out[name + "_2"] = value
    return out


def reference(
    x, c, positions, w_in, w_a, w_b, w_o, w_ada, b_ada, g_mix, g_ffn, w_up, conv_w, conv_b,
    w_down, g_final, norm_mix_g_2, norm_ffn_g_2, final_norm_g_2, conv_w_pw1_2, conv_b_pw1_2,
    conv_w_dw_2, conv_b_dw_2, conv_ln_g_2, conv_ln_b_2, conv_w_pw2_2, conv_b_pw2_2, na_w_qkv_2,
    na_b_qkv_2, na_rpb_2, na_w_o_2, na_b_o_2, ffn_w_up_2, ffn_w_down_2,
):
    x = first_block(
        x, c, positions, w_in, w_a, w_b, w_o, w_ada, b_ada, g_mix, g_ffn, w_up, conv_w, conv_b,
        w_down, g_final,
    )
    return second_block(
        x, norm_mix_g_2, norm_ffn_g_2, final_norm_g_2, conv_w_pw1_2, conv_b_pw1_2, conv_w_dw_2,
        conv_b_dw_2, conv_ln_g_2, conv_ln_b_2, conv_w_pw2_2, conv_b_pw2_2, na_w_qkv_2,
        na_b_qkv_2, na_rpb_2, na_w_o_2, na_b_o_2, ffn_w_up_2, ffn_w_down_2,
    )


_drawn_inputs = setup_inputs


def setup_inputs(seed=0):
    import zlib

    import numpy as np

    out = dict(_drawn_inputs(seed))
    spreads = {}
    factors = {'g_mix': 2.685,
     'g_ffn': 3.572,
     'conv_b': 7.154,
     'norm_mix_g_2': 4.53,
     'norm_ffn_g_2': 3.438,
     'final_norm_g_2': 7.808,
     'conv_b_pw1_2': 4.585,
     'conv_ln_g_2': 4.127,
     'conv_ln_b_2': 4.917,
     'conv_b_pw2_2': 3.034,
     'conv_b_dw_2': 7.401}
    for name, (base, spread) in spreads.items():
        noise = np.random.default_rng([zlib.crc32(name.encode()), seed]).standard_normal(out[name].shape)
        drawn = base * np.exp(spread * noise) if base else spread * noise
        out[name] = jnp.asarray(drawn.astype(out[name].dtype))
    for name, factor in factors.items():
        out[name] = (out[name] * factor).astype(out[name].dtype)
    return out
```

```python
from contextlib import ExitStack

import numpy as np
import concourse.bass as bass
from concourse import mybir

F32 = mybir.dt.float32
F32R = mybir.dt.float32r
I32 = mybir.dt.int32
ALU = mybir.AluOpType
ACT = mybir.ActivationFunctionType
AX_X = mybir.AxisListType.X

P = 128
T = 256
D = 2048
DC = D // P
HEADS = 8
IDX_HEADS = 16
TOPK = 64
TOP_ROUNDS = TOPK // 8
FF = 5632
FC = FF // P
FF2 = 8192
TAPS = 31
PAD = TAPS // 2
TP = T + 2 * PAD
SCALE = float(P) ** -0.5
EPS1, EPS2 = 1e-6, 1e-5
BIG = 1.0e30

KC = 4
NCOL = 512
RAW = 4
SPL = 2
ADA_START = 8
ADA_GROUPS = 6 * D // NCOL
ADA_RING = 4
ATT = 3 * HEADS * 2

QKV_LOOP = 6
T_SMALL = 14 * KC
T_GATE = T_SMALL + 1
T_WAB = T_GATE + 8 * KC
T_WO = T_WAB + 4 * KC
T_UP = T_WO + 4 * KC
UPN = [6, 5]
T_UP, T_DOWN = [T_WO + 4 * KC, 0], [T_WO + 4 * KC + 8 * UPN[0], 0]
T_UP[1] = T_DOWN[0] + 4 * UPN[0]
T_DOWN[1] = T_UP[1] + 8 * UPN[1]
T_PW1 = T_DOWN[1] + 4 * UPN[1]
T_PW2 = T_PW1 + 8 * KC
T_UP2 = [T_PW2 + 4 * KC, 0]
T_DN2 = [T_UP2[0] + 8 * KC, 0]
T_UP2[1] = T_DN2[0] + 4 * 8
T_DN2[1] = T_UP2[1] + 8 * KC
T_END = T_DN2[1] + 4 * 8
G_SMALL = 14
G_GATE = 15
G_WAB = 23
G_WO = 31
G_UP, G_DOWN = [35, 49], [47, 59]
G_PW1 = 61
G_PW2 = 69
G_UP2 = [73, 85]
G_DN2 = [81, 93]
NPROD = 4
COL_KI, COL_GATE = 7168, 7248
NSMALL = COL_GATE - COL_KI
IDX_SCALE = 0.125 * 0.25
ROUND = 1.5 * 2.0 ** 23
TWO_PI = 6.283185307179586
TWO_PI_PARTS = (6.28125, 0.0019340515136718750, 1.2556659146e-06)
PI_IN, HALF_PI = 3.1415925, 1.5707963267948966


def free_at(group):
    return group // 2 + 2


B_VTA = 24
B_STICK = 24
B_ROPE = 44
B_VTB = 52
B_ROPEI = 59
B_IDX = 64
B_DSA = 77

VECS = [("b_ada", 96), ("g_mix", 16), ("g_ffn", 16), ("conv_b", 88), ("conv_w", 264), ("g_final", 16),
        ("norm_mix_g_2", 16), ("norm_ffn_g_2", 16), ("final_norm_g_2", 16), ("conv_b_pw1_2", 32),
        ("conv_w_dw_2", 16 * TAPS), ("conv_b_dw_2", 16), ("conv_ln_g_2", 16), ("conv_ln_b_2", 16),
        ("conv_b_pw2_2", 16), ("c", 16)]
AT, _n = {}, 0
for _name, _rows in VECS:
    AT[_name] = _n
    _n += _rows
NV = _n
VB = NV // P
assert NV % P == 0

C_ID, C_SW128, C_SW64, C_TRI, C_PAST, C_NEG, C_FREQ, C_SIGN = 0, 128, 256, 384, 512, 896, 1280, 1282
NCONST = 1284


def shape_constants():
    c = np.zeros((P, NCONST), np.float32)
    i = np.arange(P)
    c[i, C_ID + i] = 1
    c[i, C_SW128 + (i + 64) % 128] = 1
    c[i, C_SW64 + (i // 64) * 64 + (i % 64 + 32) % 64] = 1
    c[:, C_TRI:C_TRI + P] = i[:, None] > i[None, :]
    past = (i[:, None] < i[None, :]).astype(np.float32)
    c[:, C_PAST:C_PAST + 384] = np.concatenate([past, np.ones_like(past), past], 1)
    ahead = np.where(i[None, :] <= i[:, None], 0, -BIG).astype(np.float32)
    c[:, C_NEG:C_NEG + 384] = np.concatenate([ahead, np.zeros_like(ahead), ahead], 1)
    for n, d in enumerate((128, 64)):
        f = 1.0 / (np.float32(10000.0) ** (np.arange(0, d, 2, dtype=np.float32) / np.float32(d)))
        c[:, C_FREQ + n] = f.astype(np.float32)[i % (d // 2)]
        c[:, C_SIGN + n] = np.where(i % d < d // 2, -1, 1)
    return c


def build(nc, A, out):
    ctx = ExitStack()
    with ctx:
        def sem(name):
            return ctx.enter_context(nc.semaphore(name))

        def sb(name, shape, dt=F32, scope=ctx):
            return scope.enter_context(nc.sbuf_tensor(name, shape, dt))

        raw = [sb(f"raw{s}", [P, KC, NCOL]) for s in range(RAW)]
        whi = [sb(f"whi{s}", [P, KC, NCOL], F32R) for s in range(SPL)]
        wlo = [sb(f"wlo{s}", [P, KC, NCOL], F32R) for s in range(SPL)]
        res = sb("res", [P, DC, T])
        xh = sb("xh", [P, DC, T], F32R)
        xl = sb("xl", [P, DC, T], F32R)
        cons = sb("cons", [P, NCONST])
        cols = sb("cols", [P, NV])
        ones = sb("ones", [P, P])
        mean_w = sb("mean_w", [P, P])
        mod = sb("mod", [P, ADA_GROUPS * 4])
        gmod = sb("gmod", [P, 2, DC])
        one_c = sb("one_c", [P, 1])
        zero_c = sb("zero_c", [P, 1])
        varr = sb("varr", [P, T])
        rstd = sb("rstd", [P, T])
        nsq = sb("nsq", [P, T])
        nwt = sb("nwt", [P, T])
        cact = sb("cact", [P, DC])
        gate = sb("gate", [P, 2, DC])
        sq = sb("sq", [P, 4, T])
        mixer = ExitStack()
        att = sb("att", [P, 64, T], F32, mixer)
        def ch(a, b=None):
            b = a + 1 if b is None else b
            return att[:, a:b, :].rearrange("p c t -> p (c t)")

        ada = [att[:, 56 + 4 * s:60 + 4 * s, :].rearrange("p (c m) t -> p c (m t)", c=2) for s in range(2)]
        rope = sb("rope", [P, 4, T], F32, mixer)
        kidx = sb("kidx", [P, T], F32, mixer)
        wi = sb("wi", [P, 2, IDX_HEADS], F32, mixer)
        tA3, tB3 = sq[:, 0:2, :], sq[:, 2:4, :]
        tA, tB = (x.rearrange("p a t -> p (a t)") for x in (tA3, tB3))
        tC = sb("tC", [P, 384], F32, mixer)
        tD = sb("tD", [P, 384], F32, mixer)
        tE = sb("tE", [P, 384], F32, mixer)
        small = sb("small", [P, 32], F32, mixer)
        wi_t = tC[0:16, 0:T]
        rA, rB = ch(26, 28), ch(28, 30)
        posi, posf = att[0:1, 30, :].bitcast(I32), att[0:1, 31, :]
        mixer.close()
        ffn = ExitStack()
        fh = sb("fh", [P, 4 * UPN[0], T], F32R, ffn)
        fl = sb("fl", [P, 4 * UPN[0], T], F32R, ffn)
        ca = sb("ca", [P, 4, T], F32, ffn)
        cb = sb("cb", [P, 4, T], F32, ffn)
        ffn.close()
        blk2 = ExitStack()
        gh = sb("gh", [P, 32, T], F32R, blk2)
        gl = sb("gl", [P, 32, T], F32R, blk2)
        tmp = sb("tmp", [P, 4, T], F32, blk2)
        tmp2 = sb("tmp2", [P, 4, T], F32, blk2)
        blk2.close()
        conv = ExitStack()
        upad = sb("upad", [P, DC, TP], F32, conv)
        ucv = sb("ucv", [P, DC, T], F32, conv)
        pa = sb("pa", [P, 4, T], F32, conv)
        pg = sb("pg", [P, 4, T], F32, conv)
        prod = sb("prod", [P, NPROD, T], F32, conv)
        conv.close()

        ps = [ctx.enter_context(nc.psum_tensor(f"ps{i}", [P, 4, T], F32)) for i in range(2)]
        ms = [ctx.enter_context(nc.psum_tensor(f"ms{i}", [P, 4, T], F32)) for i in range(2)]
        bank_z, bank_f = ms[0][:, 0:2, :].rearrange("p a t -> p (a t)"), ms[0][:, 2:4, :].rearrange("p a t -> p (a t)")
        bank_o, bank_m = ms[1][:, 0:2, :].rearrange("p a t -> p (a t)"), ms[1][:, 2:4, :].rearrange("p a t -> p (a t)")

        down_psum = [ps[G_DOWN[0] % 2], ps[1 - G_DOWN[0] % 2], ms[0], ms[1]]
        tri = cons[:, C_TRI:C_TRI + P]
        ident = cons[:, C_ID:C_ID + P]
        past = cons[:, C_PAST:C_PAST + 384]
        ahead = cons[:, C_NEG:C_NEG + 384]

        def col(name, i):
            return cols[:, AT[name] + i:AT[name] + i + 1]

        def dcol(name, reg, i):
            return cols[:, bass.ds(reg + (AT[name] + i), 1)]

        s_in = [sem(f"input_landed{i}") for i in range(3)]
        s_vin = sem("vectors_landed")
        s_const = sem("constants_made")
        s_land = [sem(f"weights_landed{s}") for s in range(RAW)]
        s_hi = sem("piece_hi_made")
        s_lo = sem("piece_lo_made")
        s_used = sem("piece_multiplied")
        s_free = [sem(f"psum{s}_read_out") for s in range(2)]
        s_tr = sem("input_transposed")
        s_trc = sem("transposes_copied")
        s_cact = sem("c_activated")
        s_adaring = [sem(f"first_modulation_landed{s}") for s in range(ADA_RING)]
        s_adaland = [sem(f"modulation_landed{s}") for s in range(2)]
        s_ada1 = sem("first_modulation_used")
        s_ada = sem("modulation_used")
        s_mod = sem("modulation_read_out")
        s_res = sem("residual_updated")
        s_sq = sem("squares_made")
        s_acc = sem("squares_added")
        s_stat = sem("statistic_multiplied")
        s_var = sem("variance_read")
        s_std = sem("root_made")
        s_nt = sem("normed_chunk_scaled")
        s_nh = sem("normed_chunk_hi")
        s_h = sem("input_chunk_split")
        s_v = sem("vector_step")
        s_a = sem("scalar_step")
        s_posf = sem("positions_converted")
        s_posb = sem("positions_spread")
        s_ang = sem("angles_reduced")
        s_sin = sem("sines_made")
        s_vt = sem("v_transposed")
        s_vtc = sem("v_copied")
        s_z = sem("stick_logits")
        s_soft = sem("stick_softplus_tail")
        s_lm = sem("stick_log_left")
        s_af = sem("stick_suffix_sum")
        s_w = sem("stick_exponent")
        s_we = sem("stick_weights")
        s_wm = sem("stick_weights_masked")
        s_o = sem("stick_output")
        s_oc = sem("stick_output_copied")
        s_rp = sem("rotary_swapped")
        s_rd = sem("rotary_done")
        s_ki = sem("index_key_copied")
        s_wt = sem("head_weights_turned")
        s_wtc = sem("head_weights_copied")
        s_dots = sem("index_dots")
        s_relu = sem("index_relu")
        s_score = sem("index_scored")
        s_L = sem("logits")
        s_lg = sem("logits_shifted")
        s_e = sem("exponentials")
        s_p = sem("probabilities")
        s_pt = sem("probabilities_turned")
        s_ptc = sem("probabilities_copied")
        s_ob = sem("selected_output")
        s_obc = sem("selected_output_copied")
        s_cathi = sem("attention_output_hi")
        s_sig = sem("gate_sigmoid")
        s_mrg = sem("branches_merged")
        s_cA = sem("conv_scaled")
        s_cS = sem("conv_summed")
        s_silu = sem("conv_gate")
        s_hid = sem("hidden_made")
        s_hidh = sem("hidden_hi")
        s_hidl = sem("hidden_split")
        s_u = sem("glu_chunk")
        s_prod = sem("tap_product")
        s_padd = sem("tap_added")
        s_dwd = sem("depthwise_chunk_by_vector")
        s_edge = sem("padding_cleared")
        s_xc = sem("centred")
        s_y = sem("layer_norm_silu")
        s_yh = sem("layer_norm_hi")
        s_dn = sem("down_read_out")
        s_fin = sem("final_scaled")
        s_ft = sem("final_transposed")
        s_fc = sem("final_copied")
        s_out = sem("output_stored")

        H_QKV, H_CAT, H_MRG, H_UP, H_PW1, H_PW2, H_UP2 = (DC * i for i in range(7))

        class Steps:

            def __init__(self, eng, sem_steps):
                self.eng, self.sem_steps, self.n = eng, sem_steps, 0

            def did(self, ins):
                ins.then_inc(self.sem_steps, 1)
                self.n += 1

            def wait(self, back=0):
                self.eng.wait_ge(self.sem_steps, self.n - back)

        vec_parts = []
        for name, rows in VECS:
            done = 0
            while done < rows:
                at = AT[name] + done
                n = min(rows - done, P - at % P)
                vec_parts.append((name, done, n, at))
                done += n

        block = ctx.enter_context(nc.Block())

        @block.sync
        def _(sp):
            for name, done, n, at in vec_parts:
                v = A[name]
                letters = "abc"[:len(v.shape)]
                flat = v.rearrange(f"{' '.join(letters)} -> ({' '.join(letters)})") if len(v.shape) > 1 else v
                sp.dma_start(att[at % P:at % P + n, 16 + at // P, 0:P],
                             flat.rearrange("(r p) -> r p", p=P)[done:done + n, :]).then_inc(s_vin, 16)
            sp.dma_start(cons[:, :], A["consts"]).then_inc(s_in[0], 16)
            sp.dma_start(posi, A["positions"]).then_inc(s_in[1], 16)
            x_in = A["x"].rearrange("b (c p) (h t) -> p (b c) h t", p=P, t=T)
            for c in range(2):
                sp.dma_start(att[:, 8 * c:8 * c + 8, :], x_in[:, c]).then_inc(s_in[2], 16)

            def blocks(name, parts=KC):
                return A[name].rearrange("a (q c p) n -> (a q) p c n", p=P, c=parts)

            w_ada = blocks("w_ada")
            with sp.Fori(0, ADA_START) as g:
                for q in range(KC):
                    sp.wait_ge(s_ada1, g * KC + (q + 1))
                    sp.dma_start(att[:, 32 + 8 * q:40 + 8 * q, :].rearrange("p (c m) t -> p c (m t)", c=KC),
                                 w_ada[q][:, :, bass.ds(g * NCOL, NCOL)]).then_inc(s_adaring[q], 16)

            def load(g, t, src):
                sp.wait_ge(s_lo, g + (t + 1))
                sp.dma_start(raw[t % RAW][:, :, :], src).then_inc(s_land[t % RAW], 16)

            def columns(base, n, w, first_col, nq, k0=0):
                with sp.Fori(0, n) as g:
                    for q in range(nq):
                        load(g * nq, base + q, w[k0 + q][:, :, bass.ds(g * NCOL + first_col, NCOL)])

            def pairs(base, n, w, half, col0=0):
                with sp.Fori(0, n) as g:
                    for k in range(2):
                        for q in range(KC):
                            load(g * (2 * KC), base + KC * k + q, w[q][:, :, bass.ds(g * NCOL + (half * k + col0), NCOL)])

            w_in = blocks("w_in")
            columns(0, 14, w_in, 0, KC)
            sp.wait_ge(s_lo, T_SMALL + 1)
            sp.dma_start(raw[T_SMALL % RAW][:, :, :].rearrange("p c n -> p (c n)")[:, 0:DC * NSMALL].rearrange("p (c n) -> p c n", c=DC),
                         A["w_in"].rearrange("a (c p) n -> p (a c) n", p=P)[:, :, COL_KI:COL_GATE]).then_inc(s_land[T_SMALL % RAW], 16)
            columns(T_GATE, 8, w_in, COL_GATE, KC)
            w_a, w_b = blocks("w_a"), blocks("w_b")
            with sp.Fori(0, 4) as g:
                for q in range(4):
                    load(g * 4, T_WAB + q, (w_a, w_b)[q // 2][q % 2][:, :, bass.ds(g * NCOL, NCOL)])
            columns(T_WO, 4, blocks("w_o"), 0, KC)
            w_dn = A["w_down"].rearrange("a (c p) n -> p (a c) n", p=P)
            for u in range(2):
                pairs(T_UP[u], UPN[u], blocks("w_up"), FF, NCOL * UPN[0] * u)
                with sp.Fori(0, UPN[u]) as r:
                    for q in range(4):
                        load(r * 4, T_DOWN[u] + q, w_dn[:, bass.ds(r * KC + KC * UPN[0] * u, KC), NCOL * q:NCOL * (q + 1)])
            pairs(T_PW1, 4, blocks("conv_w_pw1_2"), D)
            columns(T_PW2, 4, blocks("conv_w_pw2_2"), 0, KC)
            for half in range(2):
                columns(T_UP2[half], 8, blocks("ffn_w_up_2"), half * FF2 // 2, KC)
                columns(T_DN2[half], 4, blocks("ffn_w_down_2"), 0, 8, k0=8 * half)

            o2 = out.rearrange("b (c p) d -> (b c) p d", p=P)
            for c in range(2):
                for j in range(4):
                    sp.wait_ge(s_fc, 4 * c + j + 1)
                    sp.dma_start(o2[c][:, NCOL * j:NCOL * (j + 1)],
                                 ucv[:, 8 * c + 2 * j:8 * c + 2 * j + 2, :].rearrange("p a t -> p (a t)")).then_inc(s_out, 16)
            sp.wait_ge(s_out, 8 * 16)

        @block.gpsimd
        def _(pool):
            nc.gpsimd.memset(ones[:, :], 1.0).then_inc(s_const, 1)
            nc.gpsimd.memset(mean_w[:, :], 1.0 / D).then_inc(s_const, 1)
            nc.gpsimd.memset(one_c[:, :], 1.0).then_inc(s_const, 1)
            nc.gpsimd.memset(zero_c[:, :], 0.0).then_inc(s_const, 1)

            w_ada = A["w_ada"].rearrange("a (q c p) n -> (a q) p c n", p=P, c=2)

            def modulation(g8, m, group):
                for k in range(2):
                    pool.wait_ge(s_ada, g8 + (2 * m + k + 1))
                    pool.dma_start(ada[k][:, :, :], w_ada[2 * m + k][:, :, bass.ds(group * NCOL, NCOL)]).then_inc(s_adaland[k], 16)

            def add_chunk(s, c, src):
                if c:
                    pool.wait_ge(s_acc, DC * s + c)
                    nc.gpsimd.tensor_tensor(nsq[:, :], nsq[:, :], src, ALU.add).then_inc(s_acc, 1)
                else:
                    if s:
                        pool.wait_ge(s_stat, s)
                    nc.gpsimd.tensor_copy(nsq[:, :], src).then_inc(s_acc, 1)

            def add_squares(s, k):
                for j in range(4):
                    pool.wait_ge(s_sq, 4 * k + j + 1)
                    for m in range(4):
                        add_chunk(s, 4 * j + m, sq[:, m, :])

            add_squares(0, 0)
            pool.wait_ge(s_ada1, ADA_RING + KC * ADA_START)
            with pool.Fori(0, QKV_LOOP) as g:
                for m in range(4):
                    modulation(g * 8, m, g + ADA_START)
            for t in range(4 * QKV_LOOP, B_STICK + 2 * HEADS + 2):
                if t < 64:
                    modulation(8 * (t // 4), t % 4, t // 4 + ADA_START)
                h = (t - B_STICK) // 2 - 1
                if (t - B_STICK) % 2 == 0 and 0 <= h < HEADS:
                    pool.wait_ge(s_we, h + 1)
                    if h:
                        pool.wait_ge(s_o, h)
                    nc.gpsimd.tensor_tensor(tC[:, :], tE[:, :], past, ALU.mult).then_inc(s_wm, 1)
            for t in range(B_STICK + 2 * HEADS + 2, 64):
                modulation(8 * (t // 4), t % 4, t // 4 + ADA_START)
            for s in (1, 2, 3):
                add_squares(s, s)

            pool.wait_ge(s_used, SPL + T_PW1)
            nc.gpsimd.memset(upad[:, :, 0:PAD], 0.0).then_inc(s_edge, 1)
            nc.gpsimd.memset(upad[:, :, PAD + T:TP], 0.0).then_inc(s_edge, 1)
            for j in range(4):
                for n in range(2 * TAPS):
                    dst, src = ucv[:, 4 * j + 2 * (n % 2) + 1, :], prod[:, n % NPROD, :]
                    pool.wait_ge(s_prod, 2 * TAPS * j + n + 1)
                    if n < 2:
                        nc.gpsimd.tensor_copy(dst, src).then_inc(s_padd, 1)
                    else:
                        pool.wait_ge(s_padd, 2 * TAPS * j + n - 1)
                        nc.gpsimd.tensor_tensor(dst, dst, src, ALU.add).then_inc(s_padd, 1)
            for c in range(DC):
                if c % 4 == 0:
                    pool.wait_ge(s_dwd, 2 * TAPS * (c // 4 + 1))
                    pool.wait_ge(s_padd, 2 * TAPS * (c // 4 + 1))
                add_chunk(4, c, ucv[:, c, :])
            for s in (5, 6, 7):
                add_squares(s, s - 1)

        @block.scalar
        def _(act):
            st = Steps(act, s_a)

            def split_hi(g, t):
                act.wait_ge(s_land[t % RAW], g * 4 + 16 * (t // RAW + 1))
                act.wait_ge(s_used, g + (t + 1))
                nc.scalar.copy(whi[t % SPL][:, :, :], raw[t % RAW][:, :, :]).then_inc(s_hi, 1)

            def done(g, t):
                act.wait_ge(s_used, g + (SPL + t))

            def squares(k, ready, src=res):
                for j in range(4):
                    ready(j)
                    if k or j:
                        act.wait_ge(s_acc, sum_at(k, j))
                    nc.scalar.activation(sq[:, :, :], src[:, 4 * j:4 * j + 4, :], ACT.Square).then_inc(s_sq, 1)

            def sum_at(k, j):
                s = k + (k > 3)
                return DC * s + 4 * j if j else DC * (s - (s == 5))

            def root(n):
                act.wait_ge(s_var, n + 1)
                nc.scalar.activation(rstd[:, :], varr[:, :], ACT.Sqrt).then_inc(s_std, 1)

            def norm_hi(k, shift):
                for c in range(DC):
                    act.wait_ge(s_nt, DC * k + c + 1)
                    nc.scalar.activation(xh[:, c, :], sq[:, c % 4, :], ACT.Identity, bias=shift(c)).then_inc(s_nh, 1)

            act.wait_ge(s_trc, 3)
            nc.scalar.activation(cact[:, :], cols[:, AT["c"]:AT["c"] + DC], ACT.Silu).then_inc(s_cact, 1)
            squares(0, lambda j: act.wait_ge(s_trc, 3 + 2 * (j + 1)))
            act.wait_ge(s_ang, 1)
            for n in range(2):
                nc.scalar.activation(rope[:, 2 * n, :], rB[:, T * n:T * (n + 1)], ACT.Sin).then_inc(s_sin, 1)
                nc.scalar.activation(rope[:, 2 * n + 1, :], rA[:, T * n:T * (n + 1)], ACT.Sin).then_inc(s_sin, 1)
            split_hi(0, 0)
            split_hi(0, 1)
            root(0)
            norm_hi(0, lambda c: mod[:, c:c + 1])

            def read_out(g, group, t, dst):
                done(g, t)
                nc.scalar.copy(dst, ps[group % 2][:, :, :]).then_inc(s_free[group % 2], 1)

            with act.Fori(0, QKV_LOOP // 2) as g:
                for k in range(2):
                    for q in range(2, 6):
                        split_hi(g * 8, 4 * k + q)
                    read_out(g * 8, k, 4 * (k + 1), att[:, bass.ds(g * 8 + 4 * k, 4), :])

            def background(t):
                if B_VTA <= t < B_VTA + 4 or B_VTB <= t < B_VTB + 4:
                    j = t - B_VTA if t < B_VTB else t - B_VTB + 4
                    first = 16 + 2 * j if j < 4 else 40 + 2 * (j - 4)
                    act.wait_ge(s_vt, j + 1)
                    nc.scalar.copy(ch(first, first + 2), bank_o).then_inc(s_vtc, 1)
                h = (t - B_STICK) // 2
                if (t - B_STICK) % 2 == 0 and 1 <= h <= HEADS:
                    act.wait_ge(s_w, h)
                    if h > 1:
                        act.wait_ge(s_wm, h - 1)
                    nc.scalar.activation(tE[:, :], tD[:, :], ACT.Exp).then_inc(s_we, 1)
                if (t - B_STICK) % 2 == 0 and 0 <= h < HEADS:
                    act.wait_ge(s_z, h + 1)
                    if h:
                        act.wait_ge(s_lm, h)
                    st.did(nc.scalar.activation(tA[:, 0:384], bank_z[:, 0:384], ACT.Abs, scale=SCALE))
                    st.wait()
                    st.did(nc.scalar.activation(tA[:, 0:384], tA[:, 0:384], ACT.Exp, scale=-1.0))
                    st.wait()
                    nc.scalar.activation(tA[:, 0:384], tA[:, 0:384], ACT.Ln, bias=one_c[:, 0:1]).then_inc(s_soft, 1)
                if (t - B_STICK) % 2 == 0 and 2 <= h < HEADS + 2:
                    act.wait_ge(s_o, h - 1)
                    nc.scalar.copy(att[:, h - 2, :], bank_o[:, 0:T]).then_inc(s_oc, 1)
                if t == T_SMALL + 1:
                    done(0, T_SMALL + 1)
                    nc.scalar.copy(kidx[0:64, :], ps[0][0:64, 0, :]).then_inc(s_ki, 1)
                    nc.scalar.copy(kidx[64:128, :], ps[0][0:64, 0, :]).then_inc(s_ki, 1)
                    nc.scalar.copy(wi_t[:, :], ps[0][64:80, 0, :]).then_inc(s_free[0], 1)
                c = t - B_IDX
                if 0 <= c < 8:
                    act.wait_ge(s_dots, c + 1)
                    if c:
                        act.wait_ge(s_score, 4 * c)
                    nc.scalar.activation(tA[:, 0:384], bank_z[:, 0:384], ACT.Relu, scale=IDX_SCALE).then_inc(s_relu, 1)
                    nc.scalar.activation(tB[:, 0:384], bank_f[:, 0:384], ACT.Relu, scale=IDX_SCALE).then_inc(s_relu, 1)
                h = t - B_DSA
                if 0 <= h < HEADS:
                    act.wait_ge(s_lg, 2 * h + 2)
                    if h:
                        act.wait_ge(s_pt, h)
                    for b, (lo, hi) in enumerate(((0, P), (P, 384))):
                        nc.scalar.activation(tE[:, lo:hi], tD[:, lo:hi], ACT.Exp, bias=small[:, b:b + 1],
                                             accum_out=small[:, 4 + b:5 + b]).then_inc(s_e, 1)
                if 2 <= h < HEADS + 2:
                    act.wait_ge(s_ob, h - 1)
                    nc.scalar.copy(att[:, 24 + h - 2, :], bank_o[:, 0:T]).then_inc(s_obc, 1)

            background(4 * QKV_LOOP)
            for t in range(4 * QKV_LOOP + 1, T_WAB + 1):
                split_hi(0, t + 1)
                if t <= T_SMALL and t % 4 == 0:
                    g = t // 4 - 1
                    read_out(0, g, t, att[:, 4 * g:4 * g + 4, :])
                if t > T_GATE and (t - T_GATE) % 4 == 0:
                    g = (t - T_GATE) // 4 - 1
                    first = 8 + 4 * g if g < 4 else 48 + 4 * (g - 4)
                    read_out(0, G_GATE + g, t, att[:, first:first + 4, :])
                background(t)
            done(0, T_WAB)
            for c, first in enumerate((0, 24)):
                act.wait_ge((s_oc, s_obc)[c], HEADS)
                nc.scalar.copy(xh[:, 8 * c:8 * c + 8, :], att[:, first:first + 8, :]).then_inc(s_cathi, 1)
            with act.Fori(0, 4) as g:
                for k in range(2):
                    gk = att[:, bass.ds(g * 4 + (8 + 40 * k), 4), :]
                    nc.scalar.activation(gk, gk, ACT.Sigmoid).then_inc(s_sig, 1)
                for q in range(2, 6):
                    split_hi(g * 4, T_WAB + q)
            done(0, T_WO)
            for j in range(4):
                act.wait_ge(s_mrg, j + 1)
                nc.scalar.copy(xh[:, 4 * j:4 * j + 4, :], att[:, 8 + 4 * j:12 + 4 * j, :]).then_inc(s_cathi, 1)
            for j in range(4):
                for q in range(2, 6):
                    split_hi(0, T_WO + 4 * j + q)
                act.wait_ge(s_free[(G_WO + j) % 2], free_at(G_WO + j))
                act.wait_ge(s_acc, sum_at(1, j))
                nc.scalar.activation(sq[:, :, :], res[:, 4 * j:4 * j + 4, :], ACT.Square).then_inc(s_sq, 1)
            root(1)

            norm_hi(1, lambda c: mod[:, 3 * DC + c:3 * DC + c + 1])

            for u in range(2):
                b0 = UPN[0] * u
                with act.Fori(0, UPN[u]) as i:
                    for k in range(2):
                        for q in range(2, 6):
                            split_hi(i * 8, T_UP[u] + 4 * k + q)
                            if k == 1 and q == 2:
                                act.wait_ge(s_free[G_UP[u] % 2], i + free_at(G_UP[u]))
                                nc.scalar.activation(ca[:, :, :], ca[:, :, :], ACT.Silu).then_inc(s_silu, 1)
                        done(i * 8, T_UP[u] + 4 * (k + 1))
                        if k == 0:
                            act.wait_ge(s_hidl, i + (b0 + 1))
                        for m in range(4):
                            nc.scalar.activation((ca, cb)[k][:, m, :], ps[(G_UP[u] + k) % 2][:, m, :], ACT.Identity,
                                                 scale=dcol("conv_w", i * 4, (4 + k) * FC + 4 * b0 + m),
                                                 bias=dcol("conv_b", i * 4, k * FC + 4 * b0 + m)).then_inc(s_cA, 1)
                    act.wait_ge(s_hid, i + (b0 + 1))
                    nc.scalar.copy(fh[:, bass.ds(i * 4, 4), :], ca[:, :, :]).then_inc(s_hidh, 1)
                with act.Fori(0, UPN[u]) as r:
                    for q in range(2, 6):
                        split_hi(r * 4, T_DOWN[u] + q)
            squares(2, lambda j: act.wait_ge(s_free[(G_DOWN[1] + j) % 2], free_at(G_DOWN[1] + j)) if j < 2 else act.wait_ge(s_dn, j + 1))
            root(2)
            squares(3, lambda j: act.wait_ge(s_res, 4 * (j + 1)))
            root(3)
            norm_hi(2, lambda c: zero_c[:, 0:1])

            def products(j, lo, hi):
                for n in range(lo, hi):
                    tap, k = n // 2, n % 2
                    c = 4 * j + 2 * k + 1
                    if n == 0:
                        act.wait_ge(s_u, 4 * j + 4)
                        act.wait_ge(s_edge, 2)
                    if j or n >= NPROD:
                        act.wait_ge(s_padd, 2 * TAPS * j + max(0, n - NPROD + 1))
                    dst, src, w = prod[:, n % NPROD, :], upad[:, c, tap:tap + T], col("conv_w_dw_2", DC * tap + c)
                    if tap == 0:
                        nc.scalar.activation(dst, src, ACT.Identity, scale=w, bias=col("conv_b_dw_2", c)).then_inc(s_prod, 1)
                    else:
                        nc.scalar.activation(dst, src, ACT.Copy, scale=w).then_inc(s_prod, 1)

            per = -(-2 * TAPS // 8)
            for j in range(5):
                for q in range(2, 10):
                    if j < 4:
                        split_hi(0, T_PW1 + 8 * j + q)
                    if j:
                        products(j - 1, min(2 * TAPS, (q - 2) * per), min(2 * TAPS, (q - 1) * per))
                if j < 4:
                    done(0, T_PW1 + 8 * (j + 1))
                    for m in range(4):
                        ins = nc.scalar.activation(pg[:, m, :], ps[(G_PW1 + 1) % 2][:, m, :], ACT.Sigmoid,
                                                   bias=col("conv_b_pw1_2", DC + 4 * j + m))
                    ins.then_inc(s_free[(G_PW1 + 1) % 2], 1)
            squares(4, lambda j: act.wait_ge(s_xc, j + 1), ucv)
            root(4)
            for c in range(DC):
                act.wait_ge(s_nt, DC * 3 + c + 1)
                nc.scalar.activation(ucv[:, c, :], sq[:, c % 4, :], ACT.Silu, bias=col("conv_ln_b_2", c)).then_inc(s_y, 1)
            for j in range(4):
                for q in range(2, 6):
                    split_hi(0, T_PW2 + 4 * j + q)
                act.wait_ge(s_free[(G_PW2 + j) % 2], free_at(G_PW2 + j))
                act.wait_ge(s_acc, sum_at(5, j))
                nc.scalar.activation(sq[:, :, :], res[:, 4 * j:4 * j + 4, :], ACT.Square).then_inc(s_sq, 1)
            root(5)
            norm_hi(4, lambda c: zero_c[:, 0:1])
            for half in range(2):
                with act.Fori(0, 4) as i:
                    for k in range(2):
                        for q in range(2, 6):
                            split_hi(i * 8, T_UP2[half] + 4 * k + q)
                        done(i * 8, T_UP2[half] + 4 * (k + 1))
                        nc.scalar.activation(tmp[:, :, :], ps[(G_UP2[half] + k) % 2][:, :, :], ACT.Relu).then_inc(s_free[(G_UP2[half] + k) % 2], 1)
                        act.wait_ge(s_hid, i * 2 + (FC // 4 + 8 * half + k + 1))
                        nc.scalar.copy(gh[:, bass.ds(i * 8 + 4 * k, 4), :], tmp2[:, :, :]).then_inc(s_hidh, 1)
                for j in range(4):
                    for q in range(2, 10):
                        t = T_DN2[half] + 8 * j + q
                        if t < T_END:
                            split_hi(0, t)
                    if half == 1:
                        act.wait_ge(s_free[(G_DN2[1] + j) % 2], free_at(G_DN2[1] + j))
                        act.wait_ge(s_acc, sum_at(6, j))
                        nc.scalar.activation(sq[:, :, :], res[:, 4 * j:4 * j + 4, :], ACT.Square).then_inc(s_sq, 1)
            root(6)
            for b in range(8):
                act.wait_ge(s_ft, b + 1)
                nc.scalar.copy(ucv[:, 2 * b:2 * b + 2, :].rearrange("p a t -> p (a t)"), (bank_z, bank_f)[b % 2]).then_inc(s_fc, 1)

        @block.vector
        def _(dve):
            sv = Steps(dve, s_v)
            dve.sem_inc(s_lo, RAW)
            for s in (s_mod, s_hidl, *s_free):
                dve.sem_inc(s, 1)

            def split_lo(g, t):
                dve.wait_ge(s_hi, g + (t + 1))
                nc.vector.tensor_tensor(wlo[t % SPL][:, :, :], raw[t % RAW][:, :, :], whi[t % SPL][:, :, :].bitcast(F32),
                                        ALU.subtract).then_inc(s_lo, 1)

            def done(g, t):
                dve.wait_ge(s_used, g + (SPL + t))

            def root(n, s, eps):
                dve.wait_ge(s_stat, s + 1)
                nc.vector.tensor_scalar(varr[:, :], bank_o[:, 0:T], eps, None, ALU.add).then_inc(s_var, 1)
                dve.wait_ge(s_std, n + 1)
                sv.did(nc.vector.reciprocal(rstd[:, :], rstd[:, :]))
                sv.wait()
                sv.did(nc.vector.tensor_tensor(nwt[:, :], rstd[:, :], rstd[:, :], ALU.mult))
                sv.wait()
                sv.did(nc.vector.scalar_tensor_tensor(nwt[:, :], nwt[:, :], -0.5, varr[:, :], ALU.mult, ALU.mult))
                sv.wait()
                sv.did(nc.vector.scalar_tensor_tensor(rstd[:, :], nwt[:, :], 1.5, rstd[:, :], ALU.add, ALU.mult))
                sv.wait()

            def norm_split(k, k_hi, h0, gain, shift, src=res):
                def scaled(c):
                    nc.vector.scalar_tensor_tensor(sq[:, c % 4, :], src[:, c, :], gain(c), rstd[:, :], ALU.mult, ALU.mult).then_inc(s_nt, 1)
                for c in range(2):
                    scaled(c)
                for c in range(DC):
                    if c + 2 < DC:
                        if c >= 2:
                            dve.wait_ge(s_h, h0 + c - 1)
                        scaled(c + 2)
                    dve.wait_ge(s_nt, DC * k + c + 1)
                    dve.wait_ge(s_nh, DC * k_hi + c + 1)
                    nc.vector.scalar_tensor_tensor(xl[:, c, :], sq[:, c % 4, :], shift(c), xh[:, c, :].bitcast(F32),
                                                   ALU.add, ALU.subtract).then_inc(s_h, 1)

            for b in range(3 + DC // 2):
                dve.wait_ge(s_tr, b + 1)
                bank = (bank_z, bank_f)[b % 2]
                if b < 3:
                    n = min(4, VB - 4 * b) * P
                    nc.vector.tensor_copy(cols[:, 4 * P * b:4 * P * b + n], bank[:, 0:n]).then_inc(s_trc, 1)
                else:
                    nc.vector.tensor_copy(res[:, 2 * (b - 3):2 * (b - 3) + 2, :].rearrange("p c t -> p (c t)"), bank).then_inc(s_trc, 1)
            dve.wait_ge(s_in[1], 16)
            nc.vector.tensor_copy(posf, posi).then_inc(s_posf, 1)
            dve.wait_ge(s_posb, 1)
            dve.wait_ge(s_in[0], 16)
            for n in range(2):
                sv.did(nc.vector.tensor_scalar(rA[:, T * n:T * (n + 1)], bank_o[:, 0:T], cons[:, C_FREQ + n:C_FREQ + n + 1], None, ALU.mult))
            sv.wait()
            sv.did(nc.vector.tensor_scalar(rB, rA, 1.0 / TWO_PI, ROUND, ALU.mult, ALU.add))
            sv.wait()
            sv.did(nc.vector.tensor_scalar(rB, rB, ROUND, None, ALU.subtract))
            for part in TWO_PI_PARTS:
                sv.wait()
                sv.did(nc.vector.scalar_tensor_tensor(rA, rB, -part, rA, ALU.mult, ALU.add))
            sv.wait()
            sv.did(nc.vector.tensor_scalar(rA, rA, PI_IN, -PI_IN, ALU.min, ALU.max))
            sv.wait()
            sv.did(nc.vector.scalar_tensor_tensor(rB, rA, -1.0, rA, ALU.mult, ALU.min))
            sv.wait()
            nc.vector.tensor_scalar(rB, rB, HALF_PI, None, ALU.add).then_inc(s_ang, 1)
            dve.wait_ge(s_sin, 4)
            for n in range(2):
                sv.did(nc.vector.tensor_scalar(rope[:, 2 * n + 1, :], rope[:, 2 * n + 1, :], cons[:, C_SIGN + n:C_SIGN + n + 1], None, ALU.mult))

            def read_modulation(g, group_bias, n_used, dst):
                dve.wait_ge(s_ada, n_used)
                nc.vector.tensor_tensor(dst, bank_m[:, 0:4], group_bias, ALU.add).then_inc(s_mod, 1)

            with dve.Fori(0, ADA_START) as g:
                dve.wait_ge(s_ada1, g * KC + (ADA_RING + KC))
                nc.vector.tensor_tensor(mod[:, bass.ds(g * 4, 4)], bank_m[:, 0:4], cols[:, bass.ds(g * 4 + AT["b_ada"], 4)],
                                        ALU.add).then_inc(s_mod, 1)
            dve.wait_ge(s_mod, ADA_START + 1)
            sv.did(nc.vector.scalar_tensor_tensor(gmod[:, 0, :], mod[:, DC:2 * DC], 1.0, cols[:, AT["g_mix"]:AT["g_mix"] + DC],
                                                  ALU.add, ALU.mult))
            split_lo(0, 0)
            split_lo(0, 1)
            root(0, 0, EPS1)
            norm_split(0, 0, H_QKV, lambda c: gmod[:, 0, c:c + 1], lambda c: mod[:, c:c + 1])

            with dve.Fori(0, QKV_LOOP) as g:
                for q in range(2, 6):
                    dve.wait_ge(s_hi, g * 4 + (q + 1))
                    nc.vector.tensor_tensor(wlo[q % SPL][:, :, :], raw[q % RAW][:, :, :], whi[q % SPL][:, :, :].bitcast(F32),
                                            ALU.subtract).then_inc(s_lo, 1)
                dve.wait_ge(s_ada, g * 8 + 10)
                nc.vector.tensor_tensor(mod[:, bass.ds(g * 4 + 4 * ADA_START, 4)], bank_m[:, 0:4],
                                        cols[:, bass.ds(g * 4 + (AT["b_ada"] + 4 * ADA_START), 4)], ALU.add).then_inc(s_mod, 1)

            def rotate(r):
                key = r == 12
                n = 1 if key else 2
                x = kidx[:, :].unsqueeze(1) if key else (att[:, 24 + 2 * r:26 + 2 * r, :] if r < 8 else att[:, 48 + 2 * (r - 8):50 + 2 * (r - 8), :])
                k = 0 if r < 8 else 2
                cos = rope[:, k:k + 1, :].to_broadcast([P, n, T])
                sin = rope[:, k + 1:k + 2, :].to_broadcast([P, n, T])
                dve.wait_ge(s_rp, r + 1)
                sv.did(nc.vector.tensor_tensor(tA3[:, 0:n, :], x, cos, ALU.mult))
                sv.did(nc.vector.tensor_tensor(tB3[:, 0:n, :], ms[0][:, 0:n, :], sin, ALU.mult))
                sv.wait()
                nc.vector.tensor_tensor(x, tA3[:, 0:n, :], tB3[:, 0:n, :], ALU.add).then_inc(s_rd, 1)

            BLK = ((0, P), (P, 384))

            def background_first(t):
                h = t - B_DSA
                if 0 <= h < HEADS:
                    dve.wait_ge(s_L, h + 1)
                    if h:
                        dve.wait_ge(s_e, 2 * h)
                    sv.did(nc.vector.scalar_tensor_tensor(tD[:, :], bank_z[:, 0:384], SCALE, tC[:, :], ALU.mult, ALU.add))
                    sv.wait()
                    for b, (lo, hi) in enumerate(BLK):
                        nc.vector.tensor_reduce(small[:, b:b + 1], tD[:, lo:hi], AX_X, ALU.max, negate=True).then_inc(s_lg, 1)

            def background(t):
                h = (t - B_STICK) // 2
                if (t - B_STICK) % 2 == 0 and 1 <= h <= HEADS:
                    dve.wait_ge(s_af, h)
                    nc.vector.tensor_tensor(tD[:, :], tD[:, :], bank_f[:, 0:384], ALU.add).then_inc(s_w, 1)
                if (t - B_STICK) % 2 == 0 and 0 <= h < HEADS:
                    dve.wait_ge(s_soft, h + 1)
                    sv.did(nc.vector.tensor_scalar(tB[:, 0:384], bank_z[:, 0:384], SCALE, 0.0, ALU.mult, ALU.max))
                    sv.wait()
                    sv.did(nc.vector.tensor_tensor(tB[:, 0:384], tB[:, 0:384], tA[:, 0:384], ALU.add))
                    if h:
                        dve.wait_ge(s_we, h)
                    sv.wait()
                    sv.did(nc.vector.scalar_tensor_tensor(tD[:, :], bank_z[:, 0:384], SCALE, tB[:, 0:384], ALU.mult, ALU.subtract))
                    sv.wait()
                    nc.vector.scalar_tensor_tensor(tB[:, 0:384], tB[:, 0:384], -1.0, past, ALU.mult, ALU.mult).then_inc(s_lm, 1)
                if t % 4 == 0 and 4 * QKV_LOOP < t <= 64:
                    g = t // 4 - 1
                    a = 4 * (ADA_START + g)
                    read_modulation(0, cols[:, AT["b_ada"] + a:AT["b_ada"] + a + 4], 2 + 8 * (g + 1), mod[:, a:a + 4])
                if t == 66:
                    dve.wait_ge(s_mod, ADA_GROUPS + 1)
                    sv.did(nc.vector.scalar_tensor_tensor(gmod[:, 1, :], mod[:, 4 * DC:5 * DC], 1.0, cols[:, AT["g_ffn"]:AT["g_ffn"] + DC],
                                                          ALU.add, ALU.mult))
                    sv.did(nc.vector.tensor_scalar(gate[:, 0, :], mod[:, 2 * DC:3 * DC], 1.0, None, ALU.add))
                    sv.did(nc.vector.tensor_scalar(gate[:, 1, :], mod[:, 5 * DC:6 * DC], 1.0, None, ALU.add))
                if B_ROPE <= t < B_ROPE + 8:
                    rotate(t - B_ROPE)
                if B_ROPEI <= t < B_ROPEI + 5:
                    rotate(t - B_ROPEI + 8)
                if t == B_ROPEI + 4:
                    dve.wait_ge(s_wt, 1)
                    nc.vector.tensor_copy(wi[:, :, :].rearrange("p a h -> p (a h)"), bank_f[:, 0:2 * IDX_HEADS]).then_inc(s_wtc, 1)
                c = t - B_IDX
                if 0 <= c < 8:
                    dve.wait_ge(s_relu, 2 * c + 2)
                    if c == 0:
                        dve.wait_ge(s_wtc, 1)
                    for k in range(2):
                        i = 2 * c + k
                        for b, (lo, hi) in enumerate(BLK):
                            src = (tA, tB)[k][:, lo:hi]
                            if i == 0:
                                nc.vector.tensor_scalar(tD[:, lo:hi], src, wi[:, b, i:i + 1], None, ALU.mult).then_inc(s_score, 1)
                            else:
                                dve.wait_ge(s_score, 2 * i + b - 1)
                                nc.vector.scalar_tensor_tensor(tD[:, lo:hi], src, wi[:, b, i:i + 1], tD[:, lo:hi],
                                                               ALU.mult, ALU.add).then_inc(s_score, 1)
                r = t - (B_IDX + 8)
                if r == 0:
                    dve.wait_ge(s_score, 2 * IDX_HEADS)
                    sv.did(nc.vector.tensor_tensor(tE[:, :], tD[:, :], ahead, ALU.add))
                    sv.wait()
                    sv.did(nc.vector.tensor_copy(tC[:, :], tE[:, :]))
                if 0 <= r < 4:
                    for last in range(2 * r, 2 * r + 2):
                        sv.wait()
                        for b, (lo, hi) in enumerate(BLK):
                            sv.did(nc.vector.max(small[:, 8 + 8 * b:16 + 8 * b], tC[:, lo:hi]))
                        if last < TOP_ROUNDS - 1:
                            for b, (lo, hi) in enumerate(BLK):
                                sv.wait(1)
                                sv.did(nc.vector.match_replace(tC[:, lo:hi], small[:, 8 + 8 * b:16 + 8 * b], tC[:, lo:hi], -3.0e38))
                if r == 4:
                    for b, (lo, hi) in enumerate(BLK):
                        thr, cnt = small[:, 15 + 8 * b:16 + 8 * b], small[:, 24 + b:25 + b]
                        sv.wait()
                        sv.did(nc.vector.tensor_scalar(tC[:, lo:hi], tE[:, lo:hi], thr, 0.0, ALU.is_gt, ALU.add, accum_out=cnt))
                        sv.did(nc.vector.tensor_scalar(tA[:, lo:hi], tE[:, lo:hi], thr, None, ALU.is_equal))
                        sv.wait()
                        sv.did(nc.vector.tensor_scalar(cnt, cnt, -1.0, float(TOPK), ALU.mult, ALU.add))
                        sv.did(nc.vector.tensor_tensor_scan(tB[:, lo:hi], tA[:, lo:hi], tA[:, lo:hi], 0.0, ALU.add, ALU.max))
                        sv.wait()
                        sv.did(nc.vector.scalar_tensor_tensor(tB[:, lo:hi], tB[:, lo:hi], cnt, tA[:, lo:hi], ALU.is_le, ALU.mult))
                        sv.wait()
                        sv.did(nc.vector.tensor_tensor(tC[:, lo:hi], tC[:, lo:hi], tB[:, lo:hi], ALU.add))
                        sv.wait()
                        sv.did(nc.vector.tensor_scalar(tC[:, lo:hi], tC[:, lo:hi], 1.0, BIG, ALU.subtract, ALU.mult))
                    sv.wait()
                    sv.did(nc.vector.tensor_tensor(tC[:, :], tC[:, :], ahead, ALU.add))
                    sv.wait()
                h = t - B_DSA
                if 0 <= h < HEADS:
                    dve.wait_ge(s_e, 2 * h + 2)
                    sv.did(nc.vector.reciprocal(small[:, 6:8], small[:, 4:6]))
                    sv.wait()
                    for b, (lo, hi) in enumerate(BLK):
                        ins = nc.vector.tensor_scalar(tE[:, lo:hi], tE[:, lo:hi], small[:, 6 + b:7 + b], None, ALU.mult)
                        ins.then_inc(s_p, 1)
                if 1 <= h <= HEADS:
                    dve.wait_ge(s_pt, h)
                    if h > 1:
                        dve.wait_ge(s_ob, h - 1)
                    nc.vector.tensor_copy(tA[:, 0:384], bank_f[:, 0:384]).then_inc(s_ptc, 1)

            background(4 * QKV_LOOP)
            for t in range(4 * QKV_LOOP + 1, T_WAB + 1):
                background_first(t)
                split_lo(0, t + 1)
                background(t)
            done(0, T_WAB)
            for c, first in enumerate((0, 24)):
                dve.wait_ge(s_cathi, c + 1)
                ins = nc.vector.tensor_tensor(xl[:, 8 * c:8 * c + 8, :], att[:, first:first + 8, :], xh[:, 8 * c:8 * c + 8, :].bitcast(F32), ALU.subtract)
                ins.then_inc(s_h, 8)
            with dve.Fori(0, 4) as g:
                for q in range(2, 6):
                    split_lo(g * 4, T_WAB + q)
                    if q % 2:
                        k = q // 2 - 1
                        gk = att[:, bass.ds(g * 4 + (8 + 40 * k), 4), :]
                        par = (G_WAB + k) % 2
                        done(g * 4, T_WAB + 2 * (k + 1))
                        dve.wait_ge(s_sig, g * 2 + (k + 1))
                        nc.vector.tensor_tensor(gk, gk, ps[par][:, :, :], ALU.mult).then_inc(s_free[par], 1)
                ga = att[:, bass.ds(g * 4 + 8, 4), :]
                for k in range(2):
                    dve.wait_ge(s_free[(G_WAB + k) % 2], g + free_at(G_WAB + k))
                nc.vector.tensor_tensor(ga, ga, gk, ALU.add).then_inc(s_mrg, 1)
            done(0, T_WO)
            for j in range(4):
                dve.wait_ge(s_cathi, 2 + j + 1)
                nc.vector.tensor_tensor(xl[:, 4 * j:4 * j + 4, :], att[:, 8 + 4 * j:12 + 4 * j, :], xh[:, 4 * j:4 * j + 4, :].bitcast(F32),
                                        ALU.subtract).then_inc(s_h, 4)

            for j in range(4):
                for q in range(2, 6):
                    split_lo(0, T_WO + 4 * j + q)
                done(0, T_WO + 4 * (j + 1))
                for m in range(4):
                    c = 4 * j + m
                    ins = nc.vector.scalar_tensor_tensor(res[:, c, :], ps[(G_WO + j) % 2][:, m, :], gate[:, 0, c:c + 1], res[:, c, :], ALU.mult, ALU.add)
                ins.then_inc(s_free[(G_WO + j) % 2], 1)
            root(1, 1, EPS1)
            norm_split(1, 1, H_UP, lambda c: gmod[:, 1, c:c + 1], lambda c: mod[:, 3 * DC + c:3 * DC + c + 1])

            for u in range(2):
                b0 = UPN[0] * u
                with dve.Fori(0, UPN[u]) as i:
                    for k in range(2):
                        for q in range(2, 6):
                            split_lo(i * 8, T_UP[u] + 4 * k + q)
                        cx, par = (ca, cb)[k], (G_UP[u] + k) % 2
                        for m in range(4):
                            dve.wait_ge(s_cA, i * 8 + (8 * b0 + 4 * k + m - m % 2 + 2))
                            nc.vector.scalar_tensor_tensor(cx[:, m, 1:T], ps[par][:, m, 0:T - 1], dcol("conv_w", i * 4, 2 * FC + k * FC + 4 * b0 + m),
                                                           cx[:, m, 1:T], ALU.mult, ALU.add).then_inc(s_cS, 1)
                        for m in range(4):
                            dve.wait_ge(s_cS, i * 8 + (8 * b0 + 4 * k + m + 1))
                            ins = nc.vector.scalar_tensor_tensor(cx[:, m, 2:T], ps[par][:, m, 0:T - 2], dcol("conv_w", i * 4, k * FC + 4 * b0 + m),
                                                                 cx[:, m, 2:T], ALU.mult, ALU.add)
                        ins.then_inc(s_free[par], 1)
                    dve.wait_ge(s_silu, i + (b0 + 1))
                    dve.wait_ge(s_free[(G_UP[u] + 1) % 2], i + free_at(G_UP[u] + 1))
                    nc.vector.tensor_tensor(ca[:, :, :], ca[:, :, :], cb[:, :, :], ALU.mult).then_inc(s_hid, 1)
                    dve.wait_ge(s_hidh, i + (b0 + 1))
                    nc.vector.tensor_tensor(fl[:, bass.ds(i * 4, 4), :], ca[:, :, :], fh[:, bass.ds(i * 4, 4), :].bitcast(F32),
                                            ALU.subtract).then_inc(s_hidl, 1)
                with dve.Fori(0, UPN[u]) as r:
                    for q in range(2, 6):
                        split_lo(r * 4, T_DOWN[u] + q)
                done(0, T_DOWN[u] + 4 * UPN[u])
                for j in range(4):
                    for m in range(4):
                        c = 4 * j + m
                        ins = nc.vector.scalar_tensor_tensor(res[:, c, :], down_psum[j][:, m, :], gate[:, 1, c:c + 1], res[:, c, :], ALU.mult, ALU.add)
                    ins.then_inc(s_free[(G_DOWN[u] + j) % 2] if j < 2 else s_dn, 1)
            root(2, 2, EPS1)
            for c in range(DC):
                nc.vector.scalar_tensor_tensor(res[:, c, :], res[:, c, :], col("g_final", c), rstd[:, :], ALU.mult, ALU.mult).then_inc(s_res, 1)
            root(3, 3, EPS2)
            norm_split(2, 2, H_PW1, lambda c: col("norm_mix_g_2", c), lambda c: zero_c[:, 0:1])

            def glu(j):
                par = (G_PW1 + 1) % 2
                dve.wait_ge(s_free[par], free_at(G_PW1 + 1 + 2 * j))
                dve.wait_ge(s_free[1 - par], free_at(G_PW1 + 2 * j))
                for m in range(4):
                    c = 4 * j + m
                    nc.vector.scalar_tensor_tensor(upad[:, c, PAD:PAD + T], pa[:, m, :], col("conv_b_pw1_2", c), pg[:, m, :],
                                                   ALU.add, ALU.mult).then_inc(s_u, 1)

            def taps(j, lo, hi):
                for n in range(lo, hi):
                    tap, k = n // 2, n % 2
                    c = 4 * j + 2 * k
                    src = upad[:, c, tap:tap + T]
                    w = col("conv_w_dw_2", DC * tap + c)
                    if tap == 0:
                        dve.wait_ge(s_u, 4 * j + 4)
                        dve.wait_ge(s_edge, 2)
                        nc.vector.tensor_scalar(ucv[:, c, :], src, w, col("conv_b_dw_2", c), ALU.mult, ALU.add).then_inc(s_dwd, 1)
                    else:
                        dve.wait_ge(s_dwd, 2 * TAPS * j + n - 1)
                        nc.vector.scalar_tensor_tensor(ucv[:, c, :], src, w, ucv[:, c, :], ALU.mult, ALU.add).then_inc(s_dwd, 1)

            per = -(-2 * TAPS // 8)
            for j in range(5):
                for q in range(2, 10):
                    if j < 4:
                        split_lo(0, T_PW1 + 8 * j + q)
                    if j:
                        taps(j - 1, min(2 * TAPS, (q - 2) * per), min(2 * TAPS, (q - 1) * per))
                    if q == 5 and j < 4:
                        done(0, T_PW1 + 8 * j + 4)
                        nc.vector.tensor_copy(pa[:, :, :], ps[G_PW1 % 2][:, :, :]).then_inc(s_free[G_PW1 % 2], 1)
                if j < 4:
                    glu(j)
            dve.wait_ge(s_stat, 5)
            sv.did(nc.vector.tensor_copy(nwt[:, :], bank_o[:, 0:T]))
            sv.wait()
            for j in range(4):
                nc.vector.tensor_tensor(ucv[:, 4 * j:4 * j + 4, :], ucv[:, 4 * j:4 * j + 4, :], nwt[:, :].unsqueeze(1).to_broadcast([P, 4, T]),
                                        ALU.subtract).then_inc(s_xc, 1)
            root(4, 5, EPS2)

            def scaled(c):
                nc.vector.scalar_tensor_tensor(sq[:, c % 4, :], ucv[:, c, :], col("conv_ln_g_2", c), rstd[:, :], ALU.mult, ALU.mult).then_inc(s_nt, 1)
            for c in range(3):
                scaled(c)
            for c in range(DC):
                dve.wait_ge(s_y, c + 1)
                if c + 3 < DC:
                    scaled(c + 3)
                nc.vector.tensor_copy(xh[:, c, :], ucv[:, c, :]).then_inc(s_yh, 1)
                dve.wait_ge(s_yh, c + 1)
                nc.vector.tensor_tensor(xl[:, c, :], ucv[:, c, :], xh[:, c, :].bitcast(F32), ALU.subtract).then_inc(s_h, 1)
            for j in range(4):
                for q in range(2, 6):
                    split_lo(0, T_PW2 + 4 * j + q)
                done(0, T_PW2 + 4 * (j + 1))
                for m in range(4):
                    c = 4 * j + m
                    ins = nc.vector.scalar_tensor_tensor(res[:, c, :], ps[(G_PW2 + j) % 2][:, m, :], col("conv_b_pw2_2", c), res[:, c, :], ALU.add, ALU.add)
                ins.then_inc(s_free[(G_PW2 + j) % 2], 1)
            root(5, 6, EPS2)
            norm_split(4, 3, H_UP2, lambda c: col("norm_ffn_g_2", c), lambda c: zero_c[:, 0:1])
            for half in range(2):
                h0 = FC // 4 + 8 * half
                with dve.Fori(0, 4) as i:
                    for k in range(2):
                        for q in range(2, 6):
                            split_lo(i * 8, T_UP2[half] + 4 * k + q)
                        par = (G_UP2[half] + k) % 2
                        dve.wait_ge(s_free[par], i + free_at(G_UP2[half] + k))
                        nc.vector.tensor_tensor(tmp2[:, :, :], tmp[:, :, :], tmp[:, :, :], ALU.mult).then_inc(s_hid, 1)
                        dve.wait_ge(s_hidh, i * 2 + (h0 + k + 1))
                        nc.vector.tensor_tensor(gl[:, bass.ds(i * 8 + 4 * k, 4), :], tmp2[:, :, :], gh[:, bass.ds(i * 8 + 4 * k, 4), :].bitcast(F32),
                                                ALU.subtract).then_inc(s_hidl, 1)
                for j in range(4):
                    for q in range(2, 10):
                        if T_DN2[half] + 8 * j + q < T_END:
                            split_lo(0, T_DN2[half] + 8 * j + q)
                    par = (G_DN2[half] + j) % 2
                    done(0, T_DN2[half] + 8 * (j + 1))
                    nc.vector.tensor_tensor(res[:, 4 * j:4 * j + 4, :], res[:, 4 * j:4 * j + 4, :], ps[par][:, :, :], ALU.add).then_inc(s_free[par], 1)
            root(6, 7, EPS2)
            for c in range(DC):
                nc.vector.scalar_tensor_tensor(res[:, c, :], res[:, c, :], col("final_norm_g_2", c), rstd[:, :], ALU.mult, ALU.mult).then_inc(s_fin, 1)

        @block.tensor
        def _(pe):
            mm = nc.tensor.matmul
            pe.sem_inc(s_used, SPL)
            pe.sem_inc(s_ada1, ADA_RING)
            pe.sem_inc(s_ada, 2)

            def three(o, h, l, rh, rl, start, stop):
                mm(o, h, rh, start=start, stop=False, skip_group_check=True)
                mm(o, h, rl, start=False, stop=False, skip_group_check=True)
                return mm(o, l, rh, start=False, stop=stop, skip_group_check=True)

            def piece(g, t, o, rhs, first, last):
                pe.wait_ge(s_lo, g + (RAW + t + 1))
                for c in range(KC):
                    rh, rl = rhs(c)
                    for m in range(4):
                        w = slice(m * P, (m + 1) * P)
                        ins = three(o[:, m, :], whi[t % SPL][:, c, w], wlo[t % SPL][:, c, w], rh, rl,
                                    first and c == 0 and m % 2 == 0, last and c == KC - 1)
                ins.then_inc(s_used, 1)

            def from_x(k):
                return xh[:, k, :], xl[:, k, :]

            def group(g, i, t, G, H, n=4, k0=0, rhs=from_x, each=None):
                pe.wait_ge(s_free[G % 2], i + (G // 2 + 1))
                for q in range(n):
                    if H is not None:
                        pe.wait_ge(s_h, H + k0 + 4 * (q + 1))
                    piece(g, t + q, ps[G % 2], lambda c: rhs(k0 + 4 * q + c), q == 0, q == n - 1)
                    if each:
                        each(q)

            def statistic(s):
                pe.wait_ge(s_acc, DC * (s + 1))
                mm(bank_o[:, 0:T], mean_w[:, :], nsq[:, :], start=True, stop=True).then_inc(s_stat, 1)

            pe.wait_ge(s_in[0], 16)
            pe.wait_ge(s_vin, 16 * len(vec_parts))
            for b in range(3 + DC // 2):
                bank = (bank_z, bank_f)[b % 2]
                if b == 3:
                    pe.wait_ge(s_in[2], 32)
                if b >= 2:
                    pe.wait_ge(s_trc, b - 1)
                for i in range(min(4, VB - 4 * b) if b < 3 else 4):
                    if b < 3:
                        src = att[:, 16 + 4 * b + i, 0:P]
                    else:
                        m, c = 2 * (b - 3) + i // 2, i % 2
                        src = att[:, 8 * c + m // 2, (m % 2) * P:(m % 2 + 1) * P]
                    ins = nc.tensor.transpose(bank[:, P * i:P * (i + 1)], src, ident)
                ins.then_inc(s_tr, 1)
            pe.wait_ge(s_const, 4)
            pe.wait_ge(s_posf, 1)
            mm(bank_o[:, 0:T], ones[0:1, :], posf, start=True, stop=True).then_inc(s_posb, 1)
            pe.wait_ge(s_cact, 1)
            with pe.Fori(0, ADA_START) as g:
                pe.wait_ge(s_mod, g + 1)
                for q in range(KC):
                    pe.wait_ge(s_adaring[q], g * 16 + 16)
                    slot = att[:, 32 + 8 * q:40 + 8 * q, :].rearrange("p (c m) t -> p c (m t)", c=KC)
                    for c in range(KC):
                        for m in range(4):
                            ins = mm(bank_m[:, m:m + 1], slot[:, c, P * m:P * (m + 1)], cact[:, KC * q + c:KC * q + c + 1],
                                     start=q == 0 and c == 0 and m == 0, stop=q == KC - 1 and c == KC - 1, skip_group_check=True)
                    ins.then_inc(s_ada1, 1)
            pe.wait_ge(s_ang, 1)
            statistic(0)

            def modulation(g16, gm, m4):
                if m4 == 0:
                    pe.wait_ge(s_mod, gm + 1)
                for k in range(2):
                    pe.wait_ge(s_adaland[k], g16 + 16 * (m4 + 1))
                    for c in range(2):
                        kc = 4 * m4 + 2 * k + c
                        for m in range(4):
                            ins = mm(bank_m[:, m:m + 1], ada[k][:, c, P * m:P * (m + 1)], cact[:, kc:kc + 1],
                                     start=kc == 0 and m == 0, stop=kc == DC - 1, skip_group_check=True)
                    ins.then_inc(s_ada, 1)

            with pe.Fori(0, QKV_LOOP // 2) as i:
                for k in range(2):
                    group(i * 8, i, 4 * k, k, H_QKV,
                          each=lambda q: modulation(i * 128 + 64 * k, i * 2 + (ADA_START + k), q))

            BLK = ((0, P), (P, 384))

            def background(t):
                if B_VTA <= t < B_VTA + 4 or B_VTB <= t < B_VTB + 4:
                    j = t - B_VTA if t < B_VTB else t - B_VTB + 4
                    first = 16 + 2 * j if j < 4 else 40 + 2 * (j - 4)
                    G = first // 4
                    pe.wait_ge(s_free[G % 2], free_at(G))
                    if j == 4:
                        pe.wait_ge(s_oc, HEADS)
                    elif j:
                        pe.wait_ge(s_vtc, j)
                    for i in range(4):
                        ins = nc.tensor.transpose(bank_o[:, P * i:P * (i + 1)], att[:, first + i // 2, (i % 2) * P:(i % 2 + 1) * P], ident)
                    ins.then_inc(s_vt, 1)
                h = (t - B_STICK) // 2
                if (t - B_STICK) % 2 == 0 and 0 <= h < HEADS:
                    if h:
                        pe.wait_ge(s_lm, h)
                    mm(bank_z[:, 0:T], att[:, 8 + h, 0:P], att[:, h, :], start=True, stop=True)
                    mm(bank_z[:, T:384], att[:, 8 + h, P:T], att[:, h, P:T], start=True, stop=True).then_inc(s_z, 1)
                if (t - B_STICK) % 2 == 0 and 1 <= h <= HEADS:
                    pe.wait_ge(s_lm, h)
                    if h > 1:
                        pe.wait_ge(s_w, h - 1)
                    mm(bank_f[:, 0:P], tri, tB[:, 0:P], start=True, stop=True)
                    mm(bank_f[:, P:T], tri, tB[:, P:T], start=True, stop=False)
                    mm(bank_f[:, P:T], ones[:, :], tB[:, T:384], start=False, stop=True)
                    mm(bank_f[:, T:384], tri, tB[:, T:384], start=True, stop=True).then_inc(s_af, 1)
                if (t - B_STICK) % 2 == 0 and 2 <= h < HEADS + 2:
                    n = h - 2
                    pe.wait_ge(s_wm, n + 1)
                    pe.wait_ge(s_vtc, 4)
                    if n:
                        pe.wait_ge(s_oc, n)
                    attend(16 + n, tC)
                    last_mm[0].then_inc(s_o, 1)
                if B_ROPE <= t < B_ROPE + 8 or B_ROPEI <= t < B_ROPEI + 5:
                    r = t - B_ROPE if t < B_ROPE + 8 else t - B_ROPEI + 8
                    if r == 0:
                        pe.wait_ge(s_lm, HEADS)
                        pe.wait_ge(s_free[0], free_at(8))
                        pe.wait_ge(s_free[1], free_at(9))
                    else:
                        pe.wait_ge(s_rd, r)
                    if r == 8:
                        pe.wait_ge(s_free[0], free_at(12))
                        pe.wait_ge(s_free[1], free_at(13))
                    if r == 12:
                        pe.wait_ge(s_ki, 2)
                        mm(bank_z[:, 0:T], cons[:, C_SW64:C_SW64 + P], kidx[:, :], start=True, stop=True).then_inc(s_rp, 1)
                    else:
                        first = 24 + 2 * r if r < 8 else 48 + 2 * (r - 8)
                        at = C_SW128 if r < 8 else C_SW64
                        mm(bank_z[:, :], cons[:, at:at + P], ch(first, first + 2), start=True, stop=True).then_inc(s_rp, 1)
                if t == B_ROPEI + 4:
                    pe.wait_ge(s_free[0], free_at(G_SMALL))
                    pe.wait_ge(s_w, HEADS)
                    for b in range(2):
                        ins = nc.tensor.transpose(bank_f[:, IDX_HEADS * b:IDX_HEADS * (b + 1)], wi_t[:, P * b:P * (b + 1)], cons[0:16, C_ID:C_ID + 16])
                    ins.then_inc(s_wt, 1)
                c = t - B_IDX
                if 0 <= c < 8:
                    if c == 0:
                        pe.wait_ge(s_rd, 13)
                        pe.wait_ge(s_wtc, 1)
                    else:
                        pe.wait_ge(s_relu, 2 * c)
                    for k in range(2):
                        half = slice(64 * k, 64 * k + 64)
                        bank = (bank_z, bank_f)[k]
                        mm(bank[:, 0:P], att[half, 48 + c, 0:P], kidx[half, 0:P], start=True, stop=True)
                        ins = mm(bank[:, P:384], att[half, 48 + c, P:T], kidx[half, :], start=True, stop=True)
                    ins.then_inc(s_dots, 1)
                h = t - B_DSA
                if 0 <= h < HEADS:
                    if h:
                        pe.wait_ge(s_lg, 2 * h)
                    else:
                        pe.wait_ge(s_relu, 16)
                    mm(bank_z[:, 0:P], att[:, 24 + h, 0:P], att[:, 32 + h, 0:P], start=True, stop=True)
                    mm(bank_z[:, P:384], att[:, 24 + h, P:T], att[:, 32 + h, :], start=True, stop=True).then_inc(s_L, 1)
                if 1 <= h <= HEADS:
                    pe.wait_ge(s_p, 2 * h)
                    if h > 1:
                        pe.wait_ge(s_ptc, h - 1)
                    for i in range(3):
                        ins = nc.tensor.transpose(bank_f[:, P * i:P * (i + 1)], tE[:, P * i:P * (i + 1)], ident)
                    ins.then_inc(s_pt, 1)
                if 2 <= h < HEADS + 2:
                    n = h - 2
                    pe.wait_ge(s_ptc, n + 1)
                    if n:
                        pe.wait_ge(s_obc, n)
                    else:
                        pe.wait_ge(s_vtc, 8)
                    attend(40 + n, tA)
                    last_mm[0].then_inc(s_ob, 1)

            last_mm = [None]

            def attend(v, w):
                mm(bank_o[:, 0:P], att[:, v, 0:P], w[:, 0:P], start=True, stop=True)
                mm(bank_o[:, P:T], att[:, v, 0:P], w[:, P:T], start=True, stop=False)
                last_mm[0] = mm(bank_o[:, P:T], att[:, v, P:T], w[:, T:384], start=False, stop=True)

            for t in range(4 * QKV_LOOP, T_WAB):
                if t == 4 * QKV_LOOP:
                    for par in range(2):
                        pe.wait_ge(s_free[par], QKV_LOOP // 2 + 1)
                background(t)
                if t == T_SMALL:
                    pe.wait_ge(s_free[G_SMALL % 2], G_SMALL // 2 + 1)
                    pe.wait_ge(s_lo, RAW + t + 1)
                    wh, wl = (x[t % SPL][:, :, :].rearrange("p c n -> p (c n)") for x in (whi, wlo))
                    for c in range(DC):
                        w = slice(NSMALL * c, NSMALL * (c + 1))
                        ins = three(ps[G_SMALL % 2][0:NSMALL, 0, :], wh[:, w], wl[:, w], xh[:, c, :], xl[:, c, :], c == 0, c == DC - 1)
                    ins.then_inc(s_used, 1)
                else:
                    G, q = (t // 4, t % 4) if t < T_SMALL else (G_GATE + (t - T_GATE) // 4, (t - T_GATE) % 4)
                    if q == 0:
                        pe.wait_ge(s_free[G % 2], G // 2 + 1)
                    piece(0, t, ps[G % 2], lambda c: from_x(4 * q + c), q == 0, q == 3)
                if t < 64:
                    modulation(64 * (t // 4), ADA_START + t // 4, t % 4)
            with pe.Fori(0, 4) as g:
                for k in range(2):
                    group(g * 4, g, T_WAB + 2 * k, G_WAB + k, H_CAT, n=2, k0=8 * k)
            for j in range(4):
                group(0, 0, T_WO + 4 * j, G_WO + j, H_MRG)
            statistic(1)
            for u in range(2):
                with pe.Fori(0, UPN[u]) as i:
                    for k in range(2):
                        group(i * 8, i, T_UP[u] + 4 * k, G_UP[u] + k, H_UP)

                for j in range(2):
                    pe.wait_ge(s_free[(G_DOWN[u] + j) % 2], (G_DOWN[u] + j) // 2 + 1)
                if u:
                    pe.wait_ge(s_dn, 2)

                def hidden(r, first):
                    pe.wait_ge(s_hidl, r + (UPN[0] * u + 2))
                    for q in range(4):
                        piece(r * 4, T_DOWN[u] + q, down_psum[q],
                              lambda c: (fh[:, bass.ds(r * 4 + c, 1), :], fl[:, bass.ds(r * 4 + c, 1), :]), first, True)

                hidden(0, True)
                with pe.Fori(1, UPN[u]) as r:
                    hidden(r, False)
            statistic(2)
            statistic(3)
            for j in range(4):
                for k in range(2):
                    group(0, 0, T_PW1 + 8 * j + 4 * k, G_PW1 + 2 * j + k, H_PW1)
            statistic(4)
            statistic(5)
            for j in range(4):
                group(0, 0, T_PW2 + 4 * j, G_PW2 + j, H_PW2)
            statistic(6)
            for half in range(2):
                with pe.Fori(0, 4) as i:
                    for k in range(2):
                        group(i * 8, i, T_UP2[half] + 4 * k, G_UP2[half] + k, H_UP2)
                pe.wait_ge(s_hidl, FC // 4 + 8 * (half + 1) + 1)
                with pe.Fori(0, 2) as i:
                    for k in range(2):
                        group(i * 16, i, T_DN2[half] + 8 * k, G_DN2[half] + k, None, n=8, rhs=lambda c: (gh[:, c, :], gl[:, c, :]))
            statistic(7)
            for b in range(8):
                c, j = b // 4, b % 4
                pe.wait_ge(s_fin, DC if c else 4 * (j + 1))
                if b >= 2:
                    pe.wait_ge(s_fc, b - 1)
                for m in range(4):
                    ins = nc.tensor.transpose((bank_z, bank_f)[b % 2][:, P * m:P * (m + 1)], res[:, 4 * j + m, P * c:P * (c + 1)], ident)
                ins.then_inc(s_ft, 1)
    return nc


INPUTS = ["x", "c", "positions", "w_in", "w_a", "w_b", "w_o", "w_ada", "b_ada", "g_mix", "g_ffn", "w_up", "conv_w", "conv_b",
          "w_down", "g_final", "norm_mix_g_2", "norm_ffn_g_2", "final_norm_g_2", "conv_w_pw1_2", "conv_b_pw1_2", "conv_w_dw_2",
          "conv_b_dw_2", "conv_ln_g_2", "conv_ln_b_2", "conv_w_pw2_2", "conv_b_pw2_2", "ffn_w_up_2", "ffn_w_down_2"]


def kernel(**inputs):
    import concourse.bacc as bacc
    from concourse.bass_utils import run_bass_kernel_spmd

    nc = bacc.Bacc("TRN2", target_bir_lowering=False, num_devices=1)
    arrays = {name: np.ascontiguousarray(inputs[name]) for name in INPUTS}
    arrays["consts"] = shape_constants()
    aps = {name: nc.dram_tensor(f"in_{name}", a.shape, mybir.dt.from_np(a.dtype), kind="ExternalInput").ap() for name, a in arrays.items()}
    out = nc.dram_tensor("out", (1, T, D), F32, kind="ExternalOutput").ap()
    build(nc, aps, out)
    r = run_bass_kernel_spmd(nc, [{f"in_{name}": a for name, a in arrays.items()}], core_ids=[0])
    return r.results[0]["out"]
```

```python
from contextlib import ExitStack

import numpy as np
import concourse.bass as bass
from concourse import mybir

F32 = mybir.dt.float32
F32R = mybir.dt.float32r
I32 = mybir.dt.int32
ALU = mybir.AluOpType
ACT = mybir.ActivationFunctionType
AX_X = mybir.AxisListType.X

P = 128
T = 256
D = 2048
DC = D // P
HEADS = 8
IDX_HEADS = 16
TOPK = 64
TOP_ROUNDS = TOPK // 8
FF = 5632
FC = FF // P
FF2 = 8192
TAPS = 31
PAD = TAPS // 2
TP = T + 2 * PAD
SCALE = float(P) ** -0.5
EPS1, EPS2 = 1e-6, 1e-5
BIG = 1.0e30

KC = 4
NCOL = 512
RAW = 4
SPL = 2
ADA_START = 8
ADA_GROUPS = 6 * D // NCOL
ATT = 3 * HEADS * 2

QKV_LOOP = 6
T_SMALL = 14 * KC
T_GATE = T_SMALL + 1
T_WAB = T_GATE + 8 * KC
T_WO = T_WAB + 4 * KC
T_UP = T_WO + 4 * KC
UPN = [6, 5]
T_UP, T_DOWN = [T_WO + 4 * KC, 0], [T_WO + 4 * KC + 8 * UPN[0], 0]
T_UP[1] = T_DOWN[0] + 4 * UPN[0]
T_DOWN[1] = T_UP[1] + 8 * UPN[1]
T_PW1 = T_DOWN[1] + 4 * UPN[1]
T_PW2 = T_PW1 + 8 * KC
T_UP2 = [T_PW2 + 4 * KC, 0]
T_DN2 = [T_UP2[0] + 8 * KC, 0]
T_UP2[1] = T_DN2[0] + 4 * 8
T_DN2[1] = T_UP2[1] + 8 * KC
T_END = T_DN2[1] + 4 * 8
G_SMALL = 14
G_GATE = 15
G_WAB = 23
G_WO = 31
G_UP, G_DOWN = [35, 49], [47, 59]
G_PW1 = 61
G_PW2 = 69
G_UP2 = [73, 85]
G_DN2 = [81, 93]
NPROD = 4
COL_KI, COL_GATE = 7168, 7248
NSMALL = COL_GATE - COL_KI
IDX_SCALE = 0.125 * 0.25
ROUND = 1.5 * 2.0 ** 23
TWO_PI = 6.283185307179586
TWO_PI_PARTS = (6.28125, 0.0019340515136718750, 1.2556659146e-06)
PI_IN, HALF_PI = 3.1415925, 1.5707963267948966


def free_at(group):
    return group // 2 + 2


B_VTA = 24
B_STICK = 24
B_ROPE = 44
B_VTB = 52
B_ROPEI = 59
B_IDX = 64
B_DSA = 77
M_LATE = B_IDX + 8 + 4 * QKV_LOOP

VECS = [("b_ada", 96), ("g_mix", 16), ("g_ffn", 16), ("conv_b", 88), ("conv_w", 264), ("g_final", 16),
        ("norm_mix_g_2", 16), ("norm_ffn_g_2", 16), ("final_norm_g_2", 16), ("conv_b_pw1_2", 32),
        ("conv_w_dw_2", 16 * TAPS), ("conv_b_dw_2", 16), ("conv_ln_g_2", 16), ("conv_ln_b_2", 16),
        ("conv_b_pw2_2", 16), ("c", 16)]
AT, _n = {}, 0
for _name, _rows in VECS:
    AT[_name] = _n
    _n += _rows
NV = _n
VB = NV // P
assert NV % P == 0

C_ID, C_SW128, C_SW64, C_TRI, C_PAST, C_NEG, C_FREQ, C_SIGN = 0, 128, 256, 384, 512, 896, 1280, 1282
NCONST = 1284


def shape_constants():
    c = np.zeros((P, NCONST), np.float32)
    i = np.arange(P)
    c[i, C_ID + i] = 1
    c[i, C_SW128 + (i + 64) % 128] = 1
    c[i, C_SW64 + (i // 64) * 64 + (i % 64 + 32) % 64] = 1
    c[:, C_TRI:C_TRI + P] = i[:, None] > i[None, :]
    past = (i[:, None] < i[None, :]).astype(np.float32)
    c[:, C_PAST:C_PAST + 384] = np.concatenate([past, np.ones_like(past), past], 1)
    ahead = np.where(i[None, :] <= i[:, None], 0, -BIG).astype(np.float32)
    c[:, C_NEG:C_NEG + 384] = np.concatenate([ahead, np.zeros_like(ahead), ahead], 1)
    for n, d in enumerate((128, 64)):
        f = 1.0 / (np.float32(10000.0) ** (np.arange(0, d, 2, dtype=np.float32) / np.float32(d)))
        c[:, C_FREQ + n] = f.astype(np.float32)[i % (d // 2)]
        c[:, C_SIGN + n] = np.where(i % d < d // 2, -1, 1)
    return c


def build(nc, A, out):
    ctx = ExitStack()
    with ctx:
        def sem(name):
            return ctx.enter_context(nc.semaphore(name))

        def sb(name, shape, dt=F32, scope=ctx):
            return scope.enter_context(nc.sbuf_tensor(name, shape, dt))

        raw = [sb(f"raw{s}", [P, KC, NCOL]) for s in range(RAW)]
        whi = [sb(f"whi{s}", [P, KC, NCOL], F32R) for s in range(SPL)]
        wlo = [sb(f"wlo{s}", [P, KC, NCOL], F32R) for s in range(SPL)]
        res = sb("res", [P, DC, T])
        xh = sb("xh", [P, DC, T], F32R)
        xl = sb("xl", [P, DC, T], F32R)
        cons = sb("cons", [P, NCONST])
        cols = sb("cols", [P, NV])
        ones = sb("ones", [P, P])
        mean_w = sb("mean_w", [P, P])
        mod = sb("mod", [P, ADA_GROUPS * 4])
        gmod = sb("gmod", [P, 2, DC])
        one_c = sb("one_c", [P, 1])
        zero_c = sb("zero_c", [P, 1])
        norm_rows = sb("norm_rows", [P, 4, T])
        varr, rstd, nwt = (norm_rows[:, i, :] for i in range(3))
        mod_sum = [norm_rows[:, 2 * i:2 * i + 2, :].rearrange("p a t -> p (a t)") for i in range(2)]
        warm = sb("warm", [P, 8])
        cact = sb("cact", [P, DC])
        gate = sb("gate", [P, 2, DC])
        sq = sb("sq", [P, 4, T])
        mixer = ExitStack()
        att = sb("att", [P, 64, T], F32, mixer)
        def ch(a, b=None):
            b = a + 1 if b is None else b
            return att[:, a:b, :].rearrange("p c t -> p (c t)")

        ada_first = [att[:, 32 + 8 * q:40 + 8 * q, :].rearrange("p (c m) t -> p c (m t)", c=KC) for q in range(KC)]
        ada, ada_late = ([att[:, a + 4 * s:a + 4 * s + 4, :].rearrange("p (c m) t -> p c (m t)", c=2) for s in range(2)]
                         for a in (56, 32))
        rope = sb("rope", [P, 4, T], F32, mixer)
        kidx = sb("kidx", [P, T], F32, mixer)
        wi = sb("wi", [P, 2, IDX_HEADS], F32, mixer)
        tA3, tB3 = sq[:, 0:2, :], sq[:, 2:4, :]
        tA, tB = (x.rearrange("p a t -> p (a t)") for x in (tA3, tB3))
        tC = sb("tC", [P, 384], F32, mixer)
        tD = sb("tD", [P, 384], F32, mixer)
        tE = sb("tE", [P, 384], F32, mixer)
        small = sb("small", [P, 32], F32, mixer)
        wi_t = tC[0:16, 0:T]
        rA, rB = ch(26, 28), ch(28, 30)
        posi, posf = att[0:1, 30, :].bitcast(I32), att[0:1, 31, :]
        mixer.close()
        ffn = ExitStack()
        fh = sb("fh", [P, 4 * UPN[0], T], F32R, ffn)
        fl = sb("fl", [P, 4 * UPN[0], T], F32R, ffn)
        ca = sb("ca", [P, 4, T], F32, ffn)
        cb = sb("cb", [P, 4, T], F32, ffn)
        ffn.close()
        blk2 = ExitStack()
        gh = sb("gh", [P, 32, T], F32R, blk2)
        gl = sb("gl", [P, 32, T], F32R, blk2)
        tmp = sb("tmp", [P, 4, T], F32, blk2)
        tmp2 = sb("tmp2", [P, 4, T], F32, blk2)
        blk2.close()
        conv = ExitStack()
        upad = sb("upad", [P, DC, TP], F32, conv)
        ucv = sb("ucv", [P, DC, T], F32, conv)
        pa = sb("pa", [P, 4, T], F32, conv)
        pg = sb("pg", [P, 4, T], F32, conv)
        prod = sb("prod", [P, NPROD, T], F32, conv)
        conv.close()

        ps = [ctx.enter_context(nc.psum_tensor(f"ps{i}", [P, 4, T], F32)) for i in range(2)]
        ms = [ctx.enter_context(nc.psum_tensor(f"ms{i}", [P, 4, T], F32)) for i in range(2)]
        bank_z, bank_f = ms[0][:, 0:2, :].rearrange("p a t -> p (a t)"), ms[0][:, 2:4, :].rearrange("p a t -> p (a t)")
        bank_o, bank_m = ms[1][:, 0:2, :].rearrange("p a t -> p (a t)"), ms[1][:, 2:4, :].rearrange("p a t -> p (a t)")

        down_psum = [ps[G_DOWN[0] % 2], ps[1 - G_DOWN[0] % 2], ms[0], ms[1]]
        bank_d = down_psum[0][:, 0, :]
        tri = cons[:, C_TRI:C_TRI + P]
        ident = cons[:, C_ID:C_ID + P]
        past = cons[:, C_PAST:C_PAST + 384]
        ahead = cons[:, C_NEG:C_NEG + 384]

        def col(name, i):
            return cols[:, AT[name] + i:AT[name] + i + 1]

        def dcol(name, reg, i):
            return cols[:, bass.ds(reg + (AT[name] + i), 1)]

        s_in = [sem(f"input_landed{i}") for i in range(3)]
        s_vin = sem("vectors_landed")
        s_const = sem("constants_made")
        s_land = [sem(f"weights_landed{s}") for s in range(RAW)]
        s_hi = sem("piece_hi_made")
        s_lo = sem("piece_lo_made")
        s_used = sem("piece_multiplied")
        s_free = [sem(f"psum{s}_read_out") for s in range(2)]
        s_tr = sem("input_transposed")
        s_trc = sem("transposes_copied")
        s_cact = sem("c_activated")
        s_adaring = [sem(f"first_modulation_landed{s}") for s in range(KC)]
        s_adaland = [sem(f"modulation_landed{s}") for s in range(2)]
        s_chain = sem("modulation_chunk_added")
        s_gemv = sem("modulation_group_summed")
        s_mod = sem("modulation_read_out")
        s_res = sem("residual_updated")
        s_sq = sem("squares_made")
        s_acc = sem("squares_summed")
        s_mean = sem("layer_norm_mean")
        s_var = sem("variance_read")
        s_std = sem("root_made")
        s_nt = sem("normed_chunk_scaled")
        s_nh = sem("normed_chunk_hi")
        s_h = sem("input_chunk_split")
        s_v = sem("vector_step")
        s_a = sem("scalar_step")
        s_posf = sem("positions_converted")
        s_posb = sem("positions_spread")
        s_ang = sem("angles_reduced")
        s_sin = sem("sines_made")
        s_vt = sem("v_transposed")
        s_vtc = sem("v_copied")
        s_z = sem("stick_logits")
        s_soft = sem("stick_softplus_tail")
        s_lm = sem("stick_log_left")
        s_af = sem("stick_suffix_sum")
        s_w = sem("stick_exponent")
        s_we = sem("stick_weights")
        s_wm = sem("stick_weights_masked")
        s_o = sem("stick_output")
        s_oc = sem("stick_output_copied")
        s_rp = sem("rotary_swapped")
        s_rd = sem("rotary_done")
        s_ki = sem("index_key_copied")
        s_wt = sem("head_weights_turned")
        s_wtc = sem("head_weights_copied")
        s_dots = sem("index_dots")
        s_relu = sem("index_relu")
        s_score = sem("index_scored")
        s_L = sem("logits")
        s_lg = sem("logits_shifted")
        s_e = sem("exponentials")
        s_p = sem("probabilities")
        s_pt = sem("probabilities_turned")
        s_ptc = sem("probabilities_copied")
        s_ob = sem("selected_output")
        s_obc = sem("selected_output_copied")
        s_cathi = sem("attention_output_hi")
        s_sig = sem("gate_sigmoid")
        s_mrg = sem("branches_merged")
        s_cA = sem("conv_scaled")
        s_cS = sem("conv_summed")
        s_silu = sem("conv_gate")
        s_hid = sem("hidden_made")
        s_hidh = sem("hidden_hi")
        s_hidl = sem("hidden_split")
        s_u = sem("glu_chunk")
        s_prod = sem("tap_product")
        s_padd = sem("tap_added")
        s_dwd = sem("depthwise_chunk_by_vector")
        s_edge = sem("padding_cleared")
        s_xc = sem("centred")
        s_y = sem("layer_norm_silu")
        s_yh = sem("layer_norm_hi")
        s_dn = sem("down_read_out")
        s_fin = sem("final_scaled")
        s_ft = sem("final_transposed")
        s_fc = sem("final_copied")
        s_out = sem("output_stored")

        H_QKV, H_CAT, H_MRG, H_UP, H_PW1, H_PW2, H_UP2 = (DC * i for i in range(7))

        class Steps:

            def __init__(self, eng, sem_steps):
                self.eng, self.sem_steps, self.n = eng, sem_steps, 0

            def did(self, ins):
                ins.then_inc(self.sem_steps, 1)
                self.n += 1

            def wait(self, back=0):
                self.eng.wait_ge(self.sem_steps, self.n - back)

        vec_parts = []
        for name, rows in VECS:
            done = 0
            while done < rows:
                at = AT[name] + done
                n = min(rows - done, P - at % P)
                vec_parts.append((name, done, n, at))
                done += n

        block = ctx.enter_context(nc.Block())

        @block.sync
        def _(sp):
            for name, done, n, at in vec_parts:
                v = A[name]
                letters = "abc"[:len(v.shape)]
                flat = v.rearrange(f"{' '.join(letters)} -> ({' '.join(letters)})") if len(v.shape) > 1 else v
                sp.dma_start(att[at % P:at % P + n, 16 + at // P, 0:P],
                             flat.rearrange("(r p) -> r p", p=P)[done:done + n, :]).then_inc(s_vin, 16)
            sp.dma_start(cons[:, :], A["consts"]).then_inc(s_in[0], 16)
            sp.dma_start(posi, A["positions"]).then_inc(s_in[1], 16)
            x_in = A["x"].rearrange("b (c p) (h t) -> p (b c) h t", p=P, t=T)
            for c in range(2):
                sp.dma_start(att[:, 8 * c:8 * c + 8, :], x_in[:, c]).then_inc(s_in[2], 16)

            def blocks(name, parts=KC):
                return A[name].rearrange("a (q c p) n -> (a q) p c n", p=P, c=parts)

            w_ada = blocks("w_ada")
            with sp.Fori(0, ADA_START) as g:
                for q in range(KC):
                    sp.wait_ge(s_chain, g * DC + KC * (q + 1))
                    sp.dma_start(ada_first[q][:, :, :],
                                 w_ada[q][:, :, bass.ds(g * NCOL, NCOL)]).then_inc(s_adaring[q], 16)

            def load(g, t, src):
                sp.wait_ge(s_lo, g + (t + 1))
                sp.dma_start(raw[t % RAW][:, :, :], src).then_inc(s_land[t % RAW], 16)

            def columns(base, n, w, first_col, nq, k0=0):
                with sp.Fori(0, n) as g:
                    for q in range(nq):
                        load(g * nq, base + q, w[k0 + q][:, :, bass.ds(g * NCOL + first_col, NCOL)])

            def pairs(base, n, w, half, col0=0):
                with sp.Fori(0, n) as g:
                    for k in range(2):
                        for q in range(KC):
                            load(g * (2 * KC), base + KC * k + q, w[q][:, :, bass.ds(g * NCOL + (half * k + col0), NCOL)])

            w_in = blocks("w_in")
            columns(0, 14, w_in, 0, KC)
            sp.wait_ge(s_lo, T_SMALL + 1)
            sp.dma_start(raw[T_SMALL % RAW][:, :, :].rearrange("p c n -> p (c n)")[:, 0:DC * NSMALL].rearrange("p (c n) -> p c n", c=DC),
                         A["w_in"].rearrange("a (c p) n -> p (a c) n", p=P)[:, :, COL_KI:COL_GATE]).then_inc(s_land[T_SMALL % RAW], 16)
            columns(T_GATE, 8, w_in, COL_GATE, KC)
            w_a, w_b = blocks("w_a"), blocks("w_b")
            with sp.Fori(0, 4) as g:
                for q in range(4):
                    load(g * 4, T_WAB + q, (w_a, w_b)[q // 2][q % 2][:, :, bass.ds(g * NCOL, NCOL)])
            columns(T_WO, 4, blocks("w_o"), 0, KC)
            w_dn = A["w_down"].rearrange("a (c p) n -> p (a c) n", p=P)
            for u in range(2):
                pairs(T_UP[u], UPN[u], blocks("w_up"), FF, NCOL * UPN[0] * u)
                with sp.Fori(0, UPN[u]) as r:
                    for q in range(4):
                        load(r * 4, T_DOWN[u] + q, w_dn[:, bass.ds(r * KC + KC * UPN[0] * u, KC), NCOL * q:NCOL * (q + 1)])
            pairs(T_PW1, 4, blocks("conv_w_pw1_2"), D)
            columns(T_PW2, 4, blocks("conv_w_pw2_2"), 0, KC)
            for half in range(2):
                columns(T_UP2[half], 8, blocks("ffn_w_up_2"), half * FF2 // 2, KC)
                columns(T_DN2[half], 4, blocks("ffn_w_down_2"), 0, 8, k0=8 * half)

            o2 = out.rearrange("b (c p) d -> (b c) p d", p=P)
            for c in range(2):
                for j in range(4):
                    sp.wait_ge(s_fc, 4 * c + j + 1)
                    sp.dma_start(o2[c][:, NCOL * j:NCOL * (j + 1)],
                                 ucv[:, 8 * c + 2 * j:8 * c + 2 * j + 2, :].rearrange("p a t -> p (a t)")).then_inc(s_out, 16)
            sp.wait_ge(s_out, 8 * 16)

        @block.gpsimd
        def _(pool):
            nc.gpsimd.memset(ones[:, :], 1.0).then_inc(s_const, 1)
            nc.gpsimd.memset(mean_w[:, :], 1.0 / D).then_inc(s_const, 1)
            nc.gpsimd.memset(one_c[:, :], 1.0).then_inc(s_const, 1)
            nc.gpsimd.memset(zero_c[:, :], 0.0).then_inc(s_const, 1)

            w_ada = A["w_ada"].rearrange("a (q c p) n -> (a q) p c n", p=P, c=2)

            def modulation(g, m, src, slots=ada):
                pool.wait_ge(s_chain, g * 2 + (DC * (1 + ADA_START) + 2 * (m - 1)))
                pool.dma_start(slots[m % 2][:, :, :], src).then_inc(s_adaland[m % 2], 16)

            pool.wait_ge(s_chain, DC * (1 + ADA_START))
            with pool.Fori(0, QKV_LOOP) as g:
                for m in range(8):
                    modulation(g * 8, m, w_ada[m][:, :, bass.ds((g + ADA_START) * NCOL, NCOL)])

            def half_piece(m, slots=ada):
                n = (m // 8 + ADA_START) * NCOL
                modulation(0, m, w_ada[m % 8][:, :, n:n + NCOL], slots)

            for t in range(4 * QKV_LOOP, B_IDX + 8):
                half_piece(t + 4 * QKV_LOOP)
                h = (t - B_STICK) // 2 - 1
                if (t - B_STICK) % 2 == 0 and 0 <= h < HEADS:
                    pool.wait_ge(s_we, h + 1)
                    if h:
                        pool.wait_ge(s_o, h)
                    nc.gpsimd.tensor_tensor(tC[:, :], tE[:, :], past, ALU.mult).then_inc(s_wm, 1)
            pool.wait_ge(s_L, HEADS)
            for m in range(M_LATE, 8 * (ADA_GROUPS - ADA_START)):
                half_piece(m, ada_late)

            pool.wait_ge(s_used, SPL + T_PW1)
            nc.gpsimd.memset(upad[:, :, 0:PAD], 0.0).then_inc(s_edge, 1)
            nc.gpsimd.memset(upad[:, :, PAD + T:TP], 0.0).then_inc(s_edge, 1)
            for j in range(4):
                for n in range(2 * TAPS):
                    dst, src = ucv[:, 4 * j + 2 * (n % 2) + 1, :], prod[:, n % NPROD, :]
                    pool.wait_ge(s_prod, 2 * TAPS * j + n + 1)
                    if n < 2:
                        nc.gpsimd.tensor_copy(dst, src).then_inc(s_padd, 1)
                    else:
                        pool.wait_ge(s_padd, 2 * TAPS * j + n - 1)
                        nc.gpsimd.tensor_tensor(dst, dst, src, ALU.add).then_inc(s_padd, 1)

        @block.scalar
        def _(act):
            st = Steps(act, s_a)

            def split_hi(g, t):
                act.wait_ge(s_land[t % RAW], g * 4 + 16 * (t // RAW + 1))
                act.wait_ge(s_used, g + (t + 1))
                nc.scalar.copy(whi[t % SPL][:, :, :], raw[t % RAW][:, :, :]).then_inc(s_hi, 1)

            def done(g, t):
                act.wait_ge(s_used, g + (SPL + t))

            def square(k, i, src=res):
                n = 8 * k + i
                if n >= 2:
                    act.wait_ge(s_acc, n - 1)
                nc.scalar.activation(sq[:, 2 * (i % 2):2 * (i % 2) + 2, :], src[:, 2 * i:2 * i + 2, :], ACT.Square).then_inc(s_sq, 1)

            def squares(k, ready, src=res):
                for i in range(DC // 2):
                    ready(i)
                    square(k, i, src)

            def root(n):
                nc.scalar.activation(warm[:, n:n + 1], one_c[:, 0:1], ACT.Sqrt)
                act.wait_ge(s_var, n + 1)
                nc.scalar.activation(rstd[:, :], varr[:, :], ACT.Sqrt).then_inc(s_std, 1)

            def norm_hi(k, shift):
                for c in range(DC):
                    act.wait_ge(s_nt, DC * k + c + 1)
                    nc.scalar.activation(xh[:, c, :], sq[:, c % 4, :], ACT.Identity, bias=shift(c)).then_inc(s_nh, 1)

            act.wait_ge(s_trc, 3)
            nc.scalar.activation(cact[:, :], cols[:, AT["c"]:AT["c"] + DC], ACT.Silu).then_inc(s_cact, 1)
            squares(0, lambda i: act.wait_ge(s_trc, 3 + (i + 1)))
            act.wait_ge(s_ang, 1)
            for n in range(2):
                nc.scalar.activation(rope[:, 2 * n, :], rB[:, T * n:T * (n + 1)], ACT.Sin).then_inc(s_sin, 1)
                nc.scalar.activation(rope[:, 2 * n + 1, :], rA[:, T * n:T * (n + 1)], ACT.Sin).then_inc(s_sin, 1)
            split_hi(0, 0)
            split_hi(0, 1)
            root(0)
            norm_hi(0, lambda c: mod[:, c:c + 1])

            def read_out(g, group, t, dst):
                done(g, t)
                nc.scalar.copy(dst, ps[group % 2][:, :, :]).then_inc(s_free[group % 2], 1)

            with act.Fori(0, QKV_LOOP // 2) as g:
                for k in range(2):
                    for q in range(2, 6):
                        split_hi(g * 8, 4 * k + q)
                    read_out(g * 8, k, 4 * (k + 1), att[:, bass.ds(g * 8 + 4 * k, 4), :])

            def background(t):
                if B_VTA <= t < B_VTA + 4 or B_VTB <= t < B_VTB + 4:
                    j = t - B_VTA if t < B_VTB else t - B_VTB + 4
                    first = 16 + 2 * j if j < 4 else 40 + 2 * (j - 4)
                    act.wait_ge(s_vt, j + 1)
                    nc.scalar.copy(ch(first, first + 2), bank_o).then_inc(s_vtc, 1)
                h = (t - B_STICK) // 2
                if (t - B_STICK) % 2 == 0 and 1 <= h <= HEADS:
                    act.wait_ge(s_w, h)
                    if h > 1:
                        act.wait_ge(s_wm, h - 1)
                    nc.scalar.activation(tE[:, :], tD[:, :], ACT.Exp).then_inc(s_we, 1)
                if (t - B_STICK) % 2 == 0 and 0 <= h < HEADS:
                    act.wait_ge(s_z, h + 1)
                    if h:
                        act.wait_ge(s_lm, h)
                    st.did(nc.scalar.activation(tA[:, 0:384], bank_z[:, 0:384], ACT.Abs, scale=SCALE))
                    st.wait()
                    st.did(nc.scalar.activation(tA[:, 0:384], tA[:, 0:384], ACT.Exp, scale=-1.0))
                    st.wait()
                    nc.scalar.activation(tA[:, 0:384], tA[:, 0:384], ACT.Ln, bias=one_c[:, 0:1]).then_inc(s_soft, 1)
                if (t - B_STICK) % 2 == 0 and 2 <= h < HEADS + 2:
                    act.wait_ge(s_o, h - 1)
                    nc.scalar.copy(att[:, h - 2, :], bank_o[:, 0:T]).then_inc(s_oc, 1)
                if t == T_SMALL + 1:
                    done(0, T_SMALL + 1)
                    nc.scalar.copy(kidx[0:64, :], ps[0][0:64, 0, :]).then_inc(s_ki, 1)
                    nc.scalar.copy(kidx[64:128, :], ps[0][0:64, 0, :]).then_inc(s_ki, 1)
                    nc.scalar.copy(wi_t[:, :], ps[0][64:80, 0, :]).then_inc(s_free[0], 1)
                c = t - B_IDX
                if 0 <= c < 8:
                    act.wait_ge(s_dots, c + 1)
                    if c:
                        act.wait_ge(s_score, 4 * c)
                    nc.scalar.activation(tA[:, 0:384], bank_z[:, 0:384], ACT.Relu, scale=IDX_SCALE).then_inc(s_relu, 1)
                    nc.scalar.activation(tB[:, 0:384], bank_f[:, 0:384], ACT.Relu, scale=IDX_SCALE).then_inc(s_relu, 1)
                h = t - B_DSA
                if 0 <= h < HEADS:
                    act.wait_ge(s_lg, 2 * h + 2)
                    if h:
                        act.wait_ge(s_pt, h)
                    for b, (lo, hi) in enumerate(((0, P), (P, 384))):
                        nc.scalar.activation(tE[:, lo:hi], tD[:, lo:hi], ACT.Exp, bias=small[:, b:b + 1],
                                             accum_out=small[:, 4 + b:5 + b]).then_inc(s_e, 1)
                if 2 <= h < HEADS + 2:
                    act.wait_ge(s_ob, h - 1)
                    nc.scalar.copy(att[:, 24 + h - 2, :], bank_o[:, 0:T]).then_inc(s_obc, 1)

            background(4 * QKV_LOOP)
            for t in range(4 * QKV_LOOP + 1, T_WAB + 1):
                split_hi(0, t + 1)
                if t <= T_SMALL and t % 4 == 0:
                    g = t // 4 - 1
                    read_out(0, g, t, att[:, 4 * g:4 * g + 4, :])
                if t > T_GATE and (t - T_GATE) % 4 == 0:
                    g = (t - T_GATE) // 4 - 1
                    first = 8 + 4 * g if g < 4 else 48 + 4 * (g - 4)
                    read_out(0, G_GATE + g, t, att[:, first:first + 4, :])
                background(t)
            done(0, T_WAB)
            for c, first in enumerate((0, 24)):
                act.wait_ge((s_oc, s_obc)[c], HEADS)
                nc.scalar.copy(xh[:, 8 * c:8 * c + 8, :], att[:, first:first + 8, :]).then_inc(s_cathi, 1)
            with act.Fori(0, 4) as g:
                for k in range(2):
                    gk = att[:, bass.ds(g * 4 + (8 + 40 * k), 4), :]
                    nc.scalar.activation(gk, gk, ACT.Sigmoid).then_inc(s_sig, 1)
                for q in range(2, 6):
                    split_hi(g * 4, T_WAB + q)
            done(0, T_WO)
            for j in range(4):
                act.wait_ge(s_mrg, j + 1)
                nc.scalar.copy(xh[:, 4 * j:4 * j + 4, :], att[:, 8 + 4 * j:12 + 4 * j, :]).then_inc(s_cathi, 1)
            for j in range(4):
                for q in range(2, 6):
                    split_hi(0, T_WO + 4 * j + q)
                act.wait_ge(s_free[(G_WO + j) % 2], free_at(G_WO + j))
                for i in range(2):
                    square(1, 2 * j + i)
            root(1)

            norm_hi(1, lambda c: mod[:, 3 * DC + c:3 * DC + c + 1])

            for u in range(2):
                b0 = UPN[0] * u
                with act.Fori(0, UPN[u]) as i:
                    for k in range(2):
                        for q in range(2, 6):
                            split_hi(i * 8, T_UP[u] + 4 * k + q)
                            if k == 1 and q == 2:
                                act.wait_ge(s_free[G_UP[u] % 2], i + free_at(G_UP[u]))
                                nc.scalar.activation(ca[:, :, :], ca[:, :, :], ACT.Silu).then_inc(s_silu, 1)
                        done(i * 8, T_UP[u] + 4 * (k + 1))
                        if k == 0:
                            act.wait_ge(s_hidl, i + (b0 + 1))
                        for m in range(4):
                            nc.scalar.activation((ca, cb)[k][:, m, :], ps[(G_UP[u] + k) % 2][:, m, :], ACT.Identity,
                                                 scale=dcol("conv_w", i * 4, (4 + k) * FC + 4 * b0 + m),
                                                 bias=dcol("conv_b", i * 4, k * FC + 4 * b0 + m)).then_inc(s_cA, 1)
                    act.wait_ge(s_hid, i + (b0 + 1))
                    nc.scalar.copy(fh[:, bass.ds(i * 4, 4), :], ca[:, :, :]).then_inc(s_hidh, 1)
                with act.Fori(0, UPN[u]) as r:
                    for q in range(2, 6):
                        split_hi(r * 4, T_DOWN[u] + q)
            squares(2, lambda i: act.wait_ge(s_free[(G_DOWN[1] + i // 2) % 2], free_at(G_DOWN[1] + i // 2)) if i < 4 else act.wait_ge(s_dn, i // 2 + 1))
            root(2)
            squares(3, lambda i: act.wait_ge(s_res, 2 * (i + 1)))
            root(3)
            norm_hi(2, lambda c: zero_c[:, 0:1])

            def products(j, lo, hi):
                for n in range(lo, hi):
                    tap, k = n // 2, n % 2
                    c = 4 * j + 2 * k + 1
                    if n == 0:
                        act.wait_ge(s_u, 4 * j + 4)
                        act.wait_ge(s_edge, 2)
                    if j or n >= NPROD:
                        act.wait_ge(s_padd, 2 * TAPS * j + max(0, n - NPROD + 1))
                    dst, src, w = prod[:, n % NPROD, :], upad[:, c, tap:tap + T], col("conv_w_dw_2", DC * tap + c)
                    if tap == 0:
                        nc.scalar.activation(dst, src, ACT.Identity, scale=w, bias=col("conv_b_dw_2", c)).then_inc(s_prod, 1)
                    else:
                        nc.scalar.activation(dst, src, ACT.Copy, scale=w).then_inc(s_prod, 1)

            per = -(-2 * TAPS // 8)
            for j in range(5):
                for q in range(2, 10):
                    if j < 4:
                        split_hi(0, T_PW1 + 8 * j + q)
                    if j:
                        products(j - 1, min(2 * TAPS, (q - 2) * per), min(2 * TAPS, (q - 1) * per))
                if j < 4:
                    done(0, T_PW1 + 8 * (j + 1))
                    for m in range(4):
                        ins = nc.scalar.activation(pg[:, m, :], ps[(G_PW1 + 1) % 2][:, m, :], ACT.Sigmoid,
                                                   bias=col("conv_b_pw1_2", DC + 4 * j + m))
                    ins.then_inc(s_free[(G_PW1 + 1) % 2], 1)
            squares(4, lambda i: act.wait_ge(s_xc, i // 2 + 1), ucv)
            root(4)
            for c in range(DC):
                act.wait_ge(s_nt, DC * 3 + c + 1)
                nc.scalar.activation(ucv[:, c, :], sq[:, c % 4, :], ACT.Silu, bias=col("conv_ln_b_2", c)).then_inc(s_y, 1)
            for j in range(4):
                for q in range(2, 6):
                    split_hi(0, T_PW2 + 4 * j + q)
                act.wait_ge(s_free[(G_PW2 + j) % 2], free_at(G_PW2 + j))
                for i in range(2):
                    square(5, 2 * j + i)
            root(5)
            norm_hi(4, lambda c: zero_c[:, 0:1])
            for half in range(2):
                with act.Fori(0, 4) as i:
                    for k in range(2):
                        for q in range(2, 6):
                            split_hi(i * 8, T_UP2[half] + 4 * k + q)
                        done(i * 8, T_UP2[half] + 4 * (k + 1))
                        nc.scalar.activation(tmp[:, :, :], ps[(G_UP2[half] + k) % 2][:, :, :], ACT.Relu).then_inc(s_free[(G_UP2[half] + k) % 2], 1)
                        act.wait_ge(s_hid, i * 2 + (FC // 4 + 8 * half + k + 1))
                        nc.scalar.copy(gh[:, bass.ds(i * 8 + 4 * k, 4), :], tmp2[:, :, :]).then_inc(s_hidh, 1)
                for j in range(4):
                    for q in range(2, 10):
                        t = T_DN2[half] + 8 * j + q
                        if t < T_END:
                            split_hi(0, t)
                    if half == 1:
                        act.wait_ge(s_free[(G_DN2[1] + j) % 2], free_at(G_DN2[1] + j))
                        for i in range(2):
                            square(6, 2 * j + i)
            root(6)
            for b in range(8):
                act.wait_ge(s_ft, b + 1)
                nc.scalar.copy(ucv[:, 2 * b:2 * b + 2, :].rearrange("p a t -> p (a t)"), (bank_z, bank_f)[b % 2]).then_inc(s_fc, 1)

        @block.vector
        def _(dve):
            sv = Steps(dve, s_v)
            dve.sem_inc(s_lo, RAW)
            dve.sem_inc(s_chain, DC)
            for s in (s_hidl, *s_free):
                dve.sem_inc(s, 1)

            def split_lo(g, t):
                dve.wait_ge(s_hi, g + (t + 1))
                nc.vector.tensor_tensor(wlo[t % SPL][:, :, :], raw[t % RAW][:, :, :], whi[t % SPL][:, :, :].bitcast(F32),
                                        ALU.subtract).then_inc(s_lo, 1)

            def done(g, t):
                dve.wait_ge(s_used, g + (SPL + t))

            def root(n, eps, o=bank_o[:, 0:T]):
                dve.wait_ge(s_acc, 8 * (n + 1))
                nc.vector.tensor_scalar(varr[:, :], o, eps, None, ALU.add).then_inc(s_var, 1)
                dve.wait_ge(s_std, n + 1)
                sv.did(nc.vector.reciprocal(rstd[:, :], rstd[:, :]))
                sv.wait()
                sv.did(nc.vector.tensor_tensor(nwt[:, :], rstd[:, :], rstd[:, :], ALU.mult))
                sv.wait()
                sv.did(nc.vector.scalar_tensor_tensor(nwt[:, :], nwt[:, :], -0.5, varr[:, :], ALU.mult, ALU.mult))
                sv.wait()
                sv.did(nc.vector.scalar_tensor_tensor(rstd[:, :], nwt[:, :], 1.5, rstd[:, :], ALU.add, ALU.mult))
                sv.wait()

            def norm_split(k, k_hi, h0, gain, shift, src=res):
                def scaled(c):
                    nc.vector.scalar_tensor_tensor(sq[:, c % 4, :], src[:, c, :], gain(c), rstd[:, :], ALU.mult, ALU.mult).then_inc(s_nt, 1)
                for c in range(2):
                    scaled(c)
                for c in range(DC):
                    if c + 2 < DC:
                        if c >= 2:
                            dve.wait_ge(s_h, h0 + c - 1)
                        scaled(c + 2)
                    dve.wait_ge(s_nt, DC * k + c + 1)
                    dve.wait_ge(s_nh, DC * k_hi + c + 1)
                    nc.vector.scalar_tensor_tensor(xl[:, c, :], sq[:, c % 4, :], shift(c), xh[:, c, :].bitcast(F32),
                                                   ALU.add, ALU.subtract).then_inc(s_h, 1)

            for b in range(3 + DC // 2):
                dve.wait_ge(s_tr, b + 1)
                bank = (bank_z, bank_f)[b % 2]
                if b < 3:
                    n = min(4, VB - 4 * b) * P
                    nc.vector.tensor_copy(cols[:, 4 * P * b:4 * P * b + n], bank[:, 0:n]).then_inc(s_trc, 1)
                else:
                    nc.vector.tensor_copy(res[:, 2 * (b - 3):2 * (b - 3) + 2, :].rearrange("p c t -> p (c t)"), bank).then_inc(s_trc, 1)
            dve.wait_ge(s_in[1], 16)
            nc.vector.tensor_copy(posf, posi).then_inc(s_posf, 1)
            dve.wait_ge(s_posb, 1)
            dve.wait_ge(s_in[0], 16)
            for n in range(2):
                sv.did(nc.vector.tensor_scalar(rA[:, T * n:T * (n + 1)], bank_o[:, 0:T], cons[:, C_FREQ + n:C_FREQ + n + 1], None, ALU.mult))
            sv.wait()
            sv.did(nc.vector.tensor_scalar(rB, rA, 1.0 / TWO_PI, ROUND, ALU.mult, ALU.add))
            sv.wait()
            sv.did(nc.vector.tensor_scalar(rB, rB, ROUND, None, ALU.subtract))
            for part in TWO_PI_PARTS:
                sv.wait()
                sv.did(nc.vector.scalar_tensor_tensor(rA, rB, -part, rA, ALU.mult, ALU.add))
            sv.wait()
            sv.did(nc.vector.tensor_scalar(rA, rA, PI_IN, -PI_IN, ALU.min, ALU.max))
            sv.wait()
            sv.did(nc.vector.scalar_tensor_tensor(rB, rA, -1.0, rA, ALU.mult, ALU.min))
            sv.wait()
            nc.vector.tensor_scalar(rB, rB, HALF_PI, None, ALU.add).then_inc(s_ang, 1)
            dve.wait_ge(s_sin, 4)
            for n in range(2):
                sv.did(nc.vector.tensor_scalar(rope[:, 2 * n + 1, :], rope[:, 2 * n + 1, :], cons[:, C_SIGN + n:C_SIGN + n + 1], None, ALU.mult))

            def add_product(par, w, kc, g, n):
                cx = cact[:, kc:kc + 1]
                if kc == 0:
                    ins = nc.vector.tensor_scalar(mod_sum[par], w, cx, None, ALU.mult)
                else:
                    dve.wait_ge(s_chain, g + n)
                    ins = nc.vector.scalar_tensor_tensor(mod_sum[par], w, cx, mod_sum[par], ALU.mult, ALU.add)
                ins.then_inc(s_chain, 1)

            def half_piece(g, m, slots=ada):
                if m % 8 == 0:
                    dve.wait_ge(s_gemv, g + (ADA_START + m // 8 + 1))
                dve.wait_ge(s_adaland[m % 2], g * 64 + 16 * (m // 2 + 1))
                for c in range(2):
                    add_product(m // 8 % 2, slots[m % 2][:, c, :], 2 * (m % 8) + c, g * DC, DC * (1 + ADA_START) + 2 * m + c)

            def read_modulation(a, b):
                dve.wait_ge(s_gemv, 2 + b)
                c = slice(4 * a, 4 * b)
                nc.vector.tensor_tensor(mod[:, c], bank_m[:, c], cols[:, AT["b_ada"] + 4 * a:AT["b_ada"] + 4 * b], ALU.add).then_inc(s_mod, 1)

            dve.wait_ge(s_cact, 1)
            with dve.Fori(0, ADA_START // 2) as i:
                for par in range(2):
                    dve.wait_ge(s_gemv, i * 2 + (par + 1))
                    for q in range(KC):
                        dve.wait_ge(s_adaring[q], i * 32 + (16 * par + 16))
                        for c in range(KC):
                            kc = KC * q + c
                            add_product(par, ada_first[q][:, c, :], kc, i * 32, DC * (1 + par) + kc)
            read_modulation(0, ADA_START)
            dve.wait_ge(s_mod, 1)
            sv.did(nc.vector.scalar_tensor_tensor(gmod[:, 0, :], mod[:, DC:2 * DC], 1.0, cols[:, AT["g_mix"]:AT["g_mix"] + DC],
                                                  ALU.add, ALU.mult))
            split_lo(0, 0)
            split_lo(0, 1)
            root(0, EPS1)
            norm_split(0, 0, H_QKV, lambda c: gmod[:, 0, c:c + 1], lambda c: mod[:, c:c + 1])

            with dve.Fori(0, QKV_LOOP // 2) as g:
                for k in range(2):
                    for q in range(2, 6):
                        for i in range(2):
                            half_piece(g * 2, 8 * k + 2 * (q - 2) + i)
                        split_lo(g * 8, 4 * k + q)

            def rotate(r):
                key = r == 12
                n = 1 if key else 2
                x = kidx[:, :].unsqueeze(1) if key else (att[:, 24 + 2 * r:26 + 2 * r, :] if r < 8 else att[:, 48 + 2 * (r - 8):50 + 2 * (r - 8), :])
                k = 0 if r < 8 else 2
                cos = rope[:, k:k + 1, :].to_broadcast([P, n, T])
                sin = rope[:, k + 1:k + 2, :].to_broadcast([P, n, T])
                dve.wait_ge(s_rp, r + 1)
                sv.did(nc.vector.tensor_tensor(tA3[:, 0:n, :], x, cos, ALU.mult))
                sv.did(nc.vector.tensor_tensor(tB3[:, 0:n, :], ms[0][:, 0:n, :], sin, ALU.mult))
                sv.wait()
                nc.vector.tensor_tensor(x, tA3[:, 0:n, :], tB3[:, 0:n, :], ALU.add).then_inc(s_rd, 1)

            BLK = ((0, P), (P, 384))

            def background_first(t):
                h = t - B_DSA
                if 0 <= h < HEADS:
                    dve.wait_ge(s_L, h + 1)
                    if h:
                        dve.wait_ge(s_e, 2 * h)
                    sv.did(nc.vector.scalar_tensor_tensor(tD[:, :], bank_z[:, 0:384], SCALE, tC[:, :], ALU.mult, ALU.add))
                    sv.wait()
                    for b, (lo, hi) in enumerate(BLK):
                        nc.vector.tensor_reduce(small[:, b:b + 1], tD[:, lo:hi], AX_X, ALU.max, negate=True).then_inc(s_lg, 1)

            def background(t):
                h = (t - B_STICK) // 2
                if (t - B_STICK) % 2 == 0 and 1 <= h <= HEADS:
                    dve.wait_ge(s_af, h)
                    nc.vector.tensor_tensor(tD[:, :], tD[:, :], bank_f[:, 0:384], ALU.add).then_inc(s_w, 1)
                if (t - B_STICK) % 2 == 0 and 0 <= h < HEADS:
                    dve.wait_ge(s_soft, h + 1)
                    sv.did(nc.vector.tensor_scalar(tB[:, 0:384], bank_z[:, 0:384], SCALE, 0.0, ALU.mult, ALU.max))
                    sv.wait()
                    sv.did(nc.vector.tensor_tensor(tB[:, 0:384], tB[:, 0:384], tA[:, 0:384], ALU.add))
                    if h:
                        dve.wait_ge(s_we, h)
                    sv.wait()
                    sv.did(nc.vector.scalar_tensor_tensor(tD[:, :], bank_z[:, 0:384], SCALE, tB[:, 0:384], ALU.mult, ALU.subtract))
                    sv.wait()
                    nc.vector.scalar_tensor_tensor(tB[:, 0:384], tB[:, 0:384], -1.0, past, ALU.mult, ALU.mult).then_inc(s_lm, 1)
                if t == 4 * QKV_LOOP + 2:
                    read_modulation(ADA_START, ADA_START + QKV_LOOP)
                if t == B_DSA + 1:
                    read_modulation(ADA_START + QKV_LOOP, ADA_START + M_LATE // 8)
                    dve.wait_ge(s_mod, 3)
                    sv.did(nc.vector.scalar_tensor_tensor(gmod[:, 1, :], mod[:, 4 * DC:5 * DC], 1.0, cols[:, AT["g_ffn"]:AT["g_ffn"] + DC],
                                                          ALU.add, ALU.mult))
                    sv.did(nc.vector.tensor_scalar(gate[:, 0, :], mod[:, 2 * DC:3 * DC], 1.0, None, ALU.add))
                if B_ROPE <= t < B_ROPE + 8:
                    rotate(t - B_ROPE)
                if B_ROPEI <= t < B_ROPEI + 5:
                    rotate(t - B_ROPEI + 8)
                if t == B_ROPEI + 4:
                    dve.wait_ge(s_wt, 1)
                    nc.vector.tensor_copy(wi[:, :, :].rearrange("p a h -> p (a h)"), bank_f[:, 0:2 * IDX_HEADS]).then_inc(s_wtc, 1)
                c = t - B_IDX
                if 0 <= c < 8:
                    dve.wait_ge(s_relu, 2 * c + 2)
                    if c == 0:
                        dve.wait_ge(s_wtc, 1)
                    for k in range(2):
                        i = 2 * c + k
                        for b, (lo, hi) in enumerate(BLK):
                            src = (tA, tB)[k][:, lo:hi]
                            if i == 0:
                                nc.vector.tensor_scalar(tD[:, lo:hi], src, wi[:, b, i:i + 1], None, ALU.mult).then_inc(s_score, 1)
                            else:
                                dve.wait_ge(s_score, 2 * i + b - 1)
                                nc.vector.scalar_tensor_tensor(tD[:, lo:hi], src, wi[:, b, i:i + 1], tD[:, lo:hi],
                                                               ALU.mult, ALU.add).then_inc(s_score, 1)
                r = t - (B_IDX + 8)
                if r == 0:
                    dve.wait_ge(s_score, 2 * IDX_HEADS)
                    sv.did(nc.vector.tensor_tensor(tE[:, :], tD[:, :], ahead, ALU.add))
                    sv.wait()
                    sv.did(nc.vector.tensor_copy(tC[:, :], tE[:, :]))
                if 0 <= r < 4:
                    for last in range(2 * r, 2 * r + 2):
                        sv.wait()
                        for b, (lo, hi) in enumerate(BLK):
                            sv.did(nc.vector.max(small[:, 8 + 8 * b:16 + 8 * b], tC[:, lo:hi]))
                        if last < TOP_ROUNDS - 1:
                            for b, (lo, hi) in enumerate(BLK):
                                sv.wait(1)
                                sv.did(nc.vector.match_replace(tC[:, lo:hi], small[:, 8 + 8 * b:16 + 8 * b], tC[:, lo:hi], -3.0e38))
                if r == 4:
                    for b, (lo, hi) in enumerate(BLK):
                        thr, cnt = small[:, 15 + 8 * b:16 + 8 * b], small[:, 24 + b:25 + b]
                        sv.wait()
                        sv.did(nc.vector.tensor_scalar(tC[:, lo:hi], tE[:, lo:hi], thr, 0.0, ALU.is_gt, ALU.add, accum_out=cnt))
                        sv.did(nc.vector.tensor_scalar(tA[:, lo:hi], tE[:, lo:hi], thr, None, ALU.is_equal))
                        sv.wait()
                        sv.did(nc.vector.tensor_scalar(cnt, cnt, -1.0, float(TOPK), ALU.mult, ALU.add))
                        sv.did(nc.vector.tensor_tensor_scan(tB[:, lo:hi], tA[:, lo:hi], tA[:, lo:hi], 0.0, ALU.add, ALU.max))
                        sv.wait()
                        sv.did(nc.vector.scalar_tensor_tensor(tB[:, lo:hi], tB[:, lo:hi], cnt, tA[:, lo:hi], ALU.is_le, ALU.mult))
                        sv.wait()
                        sv.did(nc.vector.tensor_tensor(tC[:, lo:hi], tC[:, lo:hi], tB[:, lo:hi], ALU.add))
                        sv.wait()
                        sv.did(nc.vector.tensor_scalar(tC[:, lo:hi], tC[:, lo:hi], 1.0, BIG, ALU.subtract, ALU.mult))
                    sv.wait()
                    sv.did(nc.vector.tensor_tensor(tC[:, :], tC[:, :], ahead, ALU.add))
                    sv.wait()
                h = t - B_DSA
                if 0 <= h < HEADS:
                    dve.wait_ge(s_e, 2 * h + 2)
                    sv.did(nc.vector.reciprocal(small[:, 6:8], small[:, 4:6]))
                    sv.wait()
                    for b, (lo, hi) in enumerate(BLK):
                        ins = nc.vector.tensor_scalar(tE[:, lo:hi], tE[:, lo:hi], small[:, 6 + b:7 + b], None, ALU.mult)
                        ins.then_inc(s_p, 1)
                if 1 <= h <= HEADS:
                    dve.wait_ge(s_pt, h)
                    if h > 1:
                        dve.wait_ge(s_ob, h - 1)
                    nc.vector.tensor_copy(tA[:, 0:384], bank_f[:, 0:384]).then_inc(s_ptc, 1)

            half_piece(0, 8 * QKV_LOOP)
            background(4 * QKV_LOOP)
            for t in range(4 * QKV_LOOP + 1, T_WAB + 1):
                background_first(t)
                if t < B_IDX + 8:
                    half_piece(0, t + 4 * QKV_LOOP)
                split_lo(0, t + 1)
                background(t)
            done(0, T_WAB)
            for c, first in enumerate((0, 24)):
                dve.wait_ge(s_cathi, c + 1)
                ins = nc.vector.tensor_tensor(xl[:, 8 * c:8 * c + 8, :], att[:, first:first + 8, :], xh[:, 8 * c:8 * c + 8, :].bitcast(F32), ALU.subtract)
                ins.then_inc(s_h, 8)
            with dve.Fori(0, 4) as g:
                for q in range(2, 6):
                    split_lo(g * 4, T_WAB + q)
                    if q % 2:
                        k = q // 2 - 1
                        gk = att[:, bass.ds(g * 4 + (8 + 40 * k), 4), :]
                        par = (G_WAB + k) % 2
                        done(g * 4, T_WAB + 2 * (k + 1))
                        dve.wait_ge(s_sig, g * 2 + (k + 1))
                        nc.vector.tensor_tensor(gk, gk, ps[par][:, :, :], ALU.mult).then_inc(s_free[par], 1)
                ga = att[:, bass.ds(g * 4 + 8, 4), :]
                for k in range(2):
                    dve.wait_ge(s_free[(G_WAB + k) % 2], g + free_at(G_WAB + k))
                nc.vector.tensor_tensor(ga, ga, gk, ALU.add).then_inc(s_mrg, 1)
            done(0, T_WO)
            for j in range(4):
                dve.wait_ge(s_cathi, 2 + j + 1)
                nc.vector.tensor_tensor(xl[:, 4 * j:4 * j + 4, :], att[:, 8 + 4 * j:12 + 4 * j, :], xh[:, 4 * j:4 * j + 4, :].bitcast(F32),
                                        ALU.subtract).then_inc(s_h, 4)

            for j in range(4):
                for q in range(2, 6):
                    for i in range(2):
                        half_piece(0, M_LATE + 8 * j + 2 * (q - 2) + i, ada_late)
                    split_lo(0, T_WO + 4 * j + q)
                done(0, T_WO + 4 * (j + 1))
                for m in range(4):
                    c = 4 * j + m
                    ins = nc.vector.scalar_tensor_tensor(res[:, c, :], ps[(G_WO + j) % 2][:, m, :], gate[:, 0, c:c + 1], res[:, c, :], ALU.mult, ALU.add)
                ins.then_inc(s_free[(G_WO + j) % 2], 1)
            read_modulation(ADA_START + M_LATE // 8, ADA_GROUPS)
            dve.wait_ge(s_mod, 4)
            sv.did(nc.vector.tensor_scalar(gate[:, 1, :], mod[:, 5 * DC:6 * DC], 1.0, None, ALU.add))
            root(1, EPS1)
            norm_split(1, 1, H_UP, lambda c: gmod[:, 1, c:c + 1], lambda c: mod[:, 3 * DC + c:3 * DC + c + 1])

            for u in range(2):
                b0 = UPN[0] * u
                with dve.Fori(0, UPN[u]) as i:
                    for k in range(2):
                        for q in range(2, 6):
                            split_lo(i * 8, T_UP[u] + 4 * k + q)
                        cx, par = (ca, cb)[k], (G_UP[u] + k) % 2
                        for m in range(4):
                            dve.wait_ge(s_cA, i * 8 + (8 * b0 + 4 * k + m - m % 2 + 2))
                            nc.vector.scalar_tensor_tensor(cx[:, m, 1:T], ps[par][:, m, 0:T - 1], dcol("conv_w", i * 4, 2 * FC + k * FC + 4 * b0 + m),
                                                           cx[:, m, 1:T], ALU.mult, ALU.add).then_inc(s_cS, 1)
                        for m in range(4):
                            dve.wait_ge(s_cS, i * 8 + (8 * b0 + 4 * k + m + 1))
                            ins = nc.vector.scalar_tensor_tensor(cx[:, m, 2:T], ps[par][:, m, 0:T - 2], dcol("conv_w", i * 4, k * FC + 4 * b0 + m),
                                                                 cx[:, m, 2:T], ALU.mult, ALU.add)
                        ins.then_inc(s_free[par], 1)
                    dve.wait_ge(s_silu, i + (b0 + 1))
                    dve.wait_ge(s_free[(G_UP[u] + 1) % 2], i + free_at(G_UP[u] + 1))
                    nc.vector.tensor_tensor(ca[:, :, :], ca[:, :, :], cb[:, :, :], ALU.mult).then_inc(s_hid, 1)
                    dve.wait_ge(s_hidh, i + (b0 + 1))
                    nc.vector.tensor_tensor(fl[:, bass.ds(i * 4, 4), :], ca[:, :, :], fh[:, bass.ds(i * 4, 4), :].bitcast(F32),
                                            ALU.subtract).then_inc(s_hidl, 1)
                with dve.Fori(0, UPN[u]) as r:
                    for q in range(2, 6):
                        split_lo(r * 4, T_DOWN[u] + q)
                done(0, T_DOWN[u] + 4 * UPN[u])
                for j in range(4):
                    for m in range(4):
                        c = 4 * j + m
                        ins = nc.vector.scalar_tensor_tensor(res[:, c, :], down_psum[j][:, m, :], gate[:, 1, c:c + 1], res[:, c, :], ALU.mult, ALU.add)
                    ins.then_inc(s_free[(G_DOWN[u] + j) % 2] if j < 2 else s_dn, 1)
            root(2, EPS1, bank_d)
            for c in range(DC):
                nc.vector.scalar_tensor_tensor(res[:, c, :], res[:, c, :], col("g_final", c), rstd[:, :], ALU.mult, ALU.mult).then_inc(s_res, 1)
            root(3, EPS2)
            norm_split(2, 2, H_PW1, lambda c: col("norm_mix_g_2", c), lambda c: zero_c[:, 0:1])

            def glu(j):
                par = (G_PW1 + 1) % 2
                dve.wait_ge(s_free[par], free_at(G_PW1 + 1 + 2 * j))
                dve.wait_ge(s_free[1 - par], free_at(G_PW1 + 2 * j))
                for m in range(4):
                    c = 4 * j + m
                    nc.vector.scalar_tensor_tensor(upad[:, c, PAD:PAD + T], pa[:, m, :], col("conv_b_pw1_2", c), pg[:, m, :],
                                                   ALU.add, ALU.mult).then_inc(s_u, 1)

            def taps(j, lo, hi):
                for n in range(lo, hi):
                    tap, k = n // 2, n % 2
                    c = 4 * j + 2 * k
                    src = upad[:, c, tap:tap + T]
                    w = col("conv_w_dw_2", DC * tap + c)
                    if tap == 0:
                        dve.wait_ge(s_u, 4 * j + 4)
                        dve.wait_ge(s_edge, 2)
                        nc.vector.tensor_scalar(ucv[:, c, :], src, w, col("conv_b_dw_2", c), ALU.mult, ALU.add).then_inc(s_dwd, 1)
                    else:
                        dve.wait_ge(s_dwd, 2 * TAPS * j + n - 1)
                        nc.vector.scalar_tensor_tensor(ucv[:, c, :], src, w, ucv[:, c, :], ALU.mult, ALU.add).then_inc(s_dwd, 1)

            per = -(-2 * TAPS // 8)
            for j in range(5):
                for q in range(2, 10):
                    if j < 4:
                        split_lo(0, T_PW1 + 8 * j + q)
                    if j:
                        taps(j - 1, min(2 * TAPS, (q - 2) * per), min(2 * TAPS, (q - 1) * per))
                    if q == 5 and j < 4:
                        done(0, T_PW1 + 8 * j + 4)
                        nc.vector.tensor_copy(pa[:, :, :], ps[G_PW1 % 2][:, :, :]).then_inc(s_free[G_PW1 % 2], 1)
                if j < 4:
                    glu(j)
            dve.wait_ge(s_mean, 1)
            sv.did(nc.vector.tensor_copy(nwt[:, :], bank_o[:, 0:T]))
            sv.wait()
            for j in range(4):
                nc.vector.tensor_tensor(ucv[:, 4 * j:4 * j + 4, :], ucv[:, 4 * j:4 * j + 4, :], nwt[:, :].unsqueeze(1).to_broadcast([P, 4, T]),
                                        ALU.subtract).then_inc(s_xc, 1)
            root(4, EPS2)

            def scaled(c):
                nc.vector.scalar_tensor_tensor(sq[:, c % 4, :], ucv[:, c, :], col("conv_ln_g_2", c), rstd[:, :], ALU.mult, ALU.mult).then_inc(s_nt, 1)
            for c in range(3):
                scaled(c)
            for c in range(DC):
                dve.wait_ge(s_y, c + 1)
                if c + 3 < DC:
                    scaled(c + 3)
                nc.vector.tensor_copy(xh[:, c, :], ucv[:, c, :]).then_inc(s_yh, 1)
                dve.wait_ge(s_yh, c + 1)
                nc.vector.tensor_tensor(xl[:, c, :], ucv[:, c, :], xh[:, c, :].bitcast(F32), ALU.subtract).then_inc(s_h, 1)
            for j in range(4):
                for q in range(2, 6):
                    split_lo(0, T_PW2 + 4 * j + q)
                done(0, T_PW2 + 4 * (j + 1))
                for m in range(4):
                    c = 4 * j + m
                    ins = nc.vector.scalar_tensor_tensor(res[:, c, :], ps[(G_PW2 + j) % 2][:, m, :], col("conv_b_pw2_2", c), res[:, c, :], ALU.add, ALU.add)
                ins.then_inc(s_free[(G_PW2 + j) % 2], 1)
            root(5, EPS2)
            norm_split(4, 3, H_UP2, lambda c: col("norm_ffn_g_2", c), lambda c: zero_c[:, 0:1])
            for half in range(2):
                h0 = FC // 4 + 8 * half
                with dve.Fori(0, 4) as i:
                    for k in range(2):
                        for q in range(2, 6):
                            split_lo(i * 8, T_UP2[half] + 4 * k + q)
                        par = (G_UP2[half] + k) % 2
                        dve.wait_ge(s_free[par], i + free_at(G_UP2[half] + k))
                        nc.vector.tensor_tensor(tmp2[:, :, :], tmp[:, :, :], tmp[:, :, :], ALU.mult).then_inc(s_hid, 1)
                        dve.wait_ge(s_hidh, i * 2 + (h0 + k + 1))
                        nc.vector.tensor_tensor(gl[:, bass.ds(i * 8 + 4 * k, 4), :], tmp2[:, :, :], gh[:, bass.ds(i * 8 + 4 * k, 4), :].bitcast(F32),
                                                ALU.subtract).then_inc(s_hidl, 1)
                for j in range(4):
                    for q in range(2, 10):
                        if T_DN2[half] + 8 * j + q < T_END:
                            split_lo(0, T_DN2[half] + 8 * j + q)
                    par = (G_DN2[half] + j) % 2
                    done(0, T_DN2[half] + 8 * (j + 1))
                    nc.vector.tensor_tensor(res[:, 4 * j:4 * j + 4, :], res[:, 4 * j:4 * j + 4, :], ps[par][:, :, :], ALU.add).then_inc(s_free[par], 1)
            root(6, EPS2)
            for c in range(DC):
                nc.vector.scalar_tensor_tensor(res[:, c, :], res[:, c, :], col("final_norm_g_2", c), rstd[:, :], ALU.mult, ALU.mult).then_inc(s_fin, 1)

        @block.tensor
        def _(pe):
            mm = nc.tensor.matmul
            pe.sem_inc(s_used, SPL)
            pe.sem_inc(s_gemv, 2)

            def three(o, h, l, rh, rl, start, stop):
                mm(o, h, rh, start=start, stop=False, skip_group_check=True)
                mm(o, h, rl, start=False, stop=False, skip_group_check=True)
                return mm(o, l, rh, start=False, stop=stop, skip_group_check=True)

            def piece(g, t, o, rhs, first, last):
                pe.wait_ge(s_lo, g + (RAW + t + 1))
                for c in range(KC):
                    rh, rl = rhs(c)
                    for m in range(4):
                        w = slice(m * P, (m + 1) * P)
                        ins = three(o[:, m, :], whi[t % SPL][:, c, w], wlo[t % SPL][:, c, w], rh, rl,
                                    first and c == 0 and m % 2 == 0, last and c == KC - 1)
                ins.then_inc(s_used, 1)

            def from_x(k):
                return xh[:, k, :], xl[:, k, :]

            def group(g, i, t, G, H, n=4, k0=0, rhs=from_x, each=None):
                pe.wait_ge(s_free[G % 2], i + (G // 2 + 1))
                for q in range(n):
                    if H is not None:
                        pe.wait_ge(s_h, H + k0 + 4 * (q + 1))
                    piece(g, t + q, ps[G % 2], lambda c: rhs(k0 + 4 * q + c), q == 0, q == n - 1)
                    if each:
                        each(q)

            def statistic(k, steps=range(DC // 2), o=bank_o[:, 0:T]):
                for i in steps:
                    pe.wait_ge(s_sq, 8 * k + i + 1)
                    for m in range(2):
                        ins = mm(o, mean_w[:, :], sq[:, 2 * (i % 2) + m, :], start=i == 0 and m == 0, stop=i == 7 and m == 1)
                    ins.then_inc(s_acc, 1)

            def modulation(g, group):
                pe.wait_ge(s_chain, g * DC + DC * (group + 2))
                for m in range(4):
                    ins = mm(bank_m[:, bass.ds(g * 4 + (4 * group + m), 1)], mod_sum[group % 2][:, P * m:P * (m + 1)], ones[:, 0:1],
                             start=True, stop=True)
                ins.then_inc(s_gemv, 1)

            pe.wait_ge(s_in[0], 16)
            pe.wait_ge(s_vin, 16 * len(vec_parts))
            for b in range(3 + DC // 2):
                bank = (bank_z, bank_f)[b % 2]
                if b == 3:
                    pe.wait_ge(s_in[2], 32)
                if b >= 2:
                    pe.wait_ge(s_trc, b - 1)
                for i in range(min(4, VB - 4 * b) if b < 3 else 4):
                    if b < 3:
                        src = att[:, 16 + 4 * b + i, 0:P]
                    else:
                        m, c = 2 * (b - 3) + i // 2, i % 2
                        src = att[:, 8 * c + m // 2, (m % 2) * P:(m % 2 + 1) * P]
                    ins = nc.tensor.transpose(bank[:, P * i:P * (i + 1)], src, ident)
                ins.then_inc(s_tr, 1)
            pe.wait_ge(s_const, 4)
            pe.wait_ge(s_posf, 1)
            mm(bank_o[:, 0:T], ones[0:1, :], posf, start=True, stop=True).then_inc(s_posb, 1)
            pe.wait_ge(s_ang, 1)
            statistic(0)
            with pe.Fori(0, ADA_START // 2) as i:
                for par in range(2):
                    modulation(i * 2, par)
            pe.wait_ge(s_mod, 1)

            with pe.Fori(0, QKV_LOOP // 2) as i:
                for k in range(2):
                    group(i * 8, i, 4 * k, k, H_QKV)
                    modulation(i * 2, ADA_START + k)

            BLK = ((0, P), (P, 384))

            def background(t):
                if B_VTA <= t < B_VTA + 4 or B_VTB <= t < B_VTB + 4:
                    j = t - B_VTA if t < B_VTB else t - B_VTB + 4
                    first = 16 + 2 * j if j < 4 else 40 + 2 * (j - 4)
                    G = first // 4
                    pe.wait_ge(s_free[G % 2], free_at(G))
                    if j == 4:
                        pe.wait_ge(s_oc, HEADS)
                    elif j:
                        pe.wait_ge(s_vtc, j)
                    for i in range(4):
                        ins = nc.tensor.transpose(bank_o[:, P * i:P * (i + 1)], att[:, first + i // 2, (i % 2) * P:(i % 2 + 1) * P], ident)
                    ins.then_inc(s_vt, 1)
                h = (t - B_STICK) // 2
                if (t - B_STICK) % 2 == 0 and 0 <= h < HEADS:
                    if h:
                        pe.wait_ge(s_lm, h)
                    mm(bank_z[:, 0:T], att[:, 8 + h, 0:P], att[:, h, :], start=True, stop=True)
                    mm(bank_z[:, T:384], att[:, 8 + h, P:T], att[:, h, P:T], start=True, stop=True).then_inc(s_z, 1)
                if (t - B_STICK) % 2 == 0 and 1 <= h <= HEADS:
                    pe.wait_ge(s_lm, h)
                    if h > 1:
                        pe.wait_ge(s_w, h - 1)
                    mm(bank_f[:, 0:P], tri, tB[:, 0:P], start=True, stop=True)
                    mm(bank_f[:, P:T], tri, tB[:, P:T], start=True, stop=False)
                    mm(bank_f[:, P:T], ones[:, :], tB[:, T:384], start=False, stop=True)
                    mm(bank_f[:, T:384], tri, tB[:, T:384], start=True, stop=True).then_inc(s_af, 1)
                if (t - B_STICK) % 2 == 0 and 2 <= h < HEADS + 2:
                    n = h - 2
                    pe.wait_ge(s_wm, n + 1)
                    pe.wait_ge(s_vtc, 4)
                    if n:
                        pe.wait_ge(s_oc, n)
                    attend(16 + n, tC)
                    last_mm[0].then_inc(s_o, 1)
                if B_ROPE <= t < B_ROPE + 8 or B_ROPEI <= t < B_ROPEI + 5:
                    r = t - B_ROPE if t < B_ROPE + 8 else t - B_ROPEI + 8
                    if r == 0:
                        pe.wait_ge(s_lm, HEADS)
                        pe.wait_ge(s_free[0], free_at(8))
                        pe.wait_ge(s_free[1], free_at(9))
                    else:
                        pe.wait_ge(s_rd, r)
                    if r == 8:
                        pe.wait_ge(s_free[0], free_at(12))
                        pe.wait_ge(s_free[1], free_at(13))
                    if r == 12:
                        pe.wait_ge(s_ki, 2)
                        mm(bank_z[:, 0:T], cons[:, C_SW64:C_SW64 + P], kidx[:, :], start=True, stop=True).then_inc(s_rp, 1)
                    else:
                        first = 24 + 2 * r if r < 8 else 48 + 2 * (r - 8)
                        at = C_SW128 if r < 8 else C_SW64
                        mm(bank_z[:, :], cons[:, at:at + P], ch(first, first + 2), start=True, stop=True).then_inc(s_rp, 1)
                if t == B_ROPEI + 4:
                    pe.wait_ge(s_free[0], free_at(G_SMALL))
                    pe.wait_ge(s_w, HEADS)
                    for b in range(2):
                        ins = nc.tensor.transpose(bank_f[:, IDX_HEADS * b:IDX_HEADS * (b + 1)], wi_t[:, P * b:P * (b + 1)], cons[0:16, C_ID:C_ID + 16])
                    ins.then_inc(s_wt, 1)
                c = t - B_IDX
                if 0 <= c < 8:
                    if c == 0:
                        pe.wait_ge(s_rd, 13)
                        pe.wait_ge(s_wtc, 1)
                    else:
                        pe.wait_ge(s_relu, 2 * c)
                    for k in range(2):
                        half = slice(64 * k, 64 * k + 64)
                        bank = (bank_z, bank_f)[k]
                        mm(bank[:, 0:P], att[half, 48 + c, 0:P], kidx[half, 0:P], start=True, stop=True)
                        ins = mm(bank[:, P:384], att[half, 48 + c, P:T], kidx[half, :], start=True, stop=True)
                    ins.then_inc(s_dots, 1)
                h = t - B_DSA
                if 0 <= h < HEADS:
                    if h:
                        pe.wait_ge(s_lg, 2 * h)
                    else:
                        pe.wait_ge(s_relu, 16)
                    mm(bank_z[:, 0:P], att[:, 24 + h, 0:P], att[:, 32 + h, 0:P], start=True, stop=True)
                    mm(bank_z[:, P:384], att[:, 24 + h, P:T], att[:, 32 + h, :], start=True, stop=True).then_inc(s_L, 1)
                if 1 <= h <= HEADS:
                    pe.wait_ge(s_p, 2 * h)
                    if h > 1:
                        pe.wait_ge(s_ptc, h - 1)
                    for i in range(3):
                        ins = nc.tensor.transpose(bank_f[:, P * i:P * (i + 1)], tE[:, P * i:P * (i + 1)], ident)
                    ins.then_inc(s_pt, 1)
                if 2 <= h < HEADS + 2:
                    n = h - 2
                    pe.wait_ge(s_ptc, n + 1)
                    if n:
                        pe.wait_ge(s_obc, n)
                    else:
                        pe.wait_ge(s_vtc, 8)
                    attend(40 + n, tA)
                    last_mm[0].then_inc(s_ob, 1)

            last_mm = [None]

            def attend(v, w):
                mm(bank_o[:, 0:P], att[:, v, 0:P], w[:, 0:P], start=True, stop=True)
                mm(bank_o[:, P:T], att[:, v, 0:P], w[:, P:T], start=True, stop=False)
                last_mm[0] = mm(bank_o[:, P:T], att[:, v, P:T], w[:, T:384], start=False, stop=True)

            for t in range(4 * QKV_LOOP, T_WAB):
                if t == 4 * QKV_LOOP:
                    for par in range(2):
                        pe.wait_ge(s_free[par], QKV_LOOP // 2 + 1)
                background(t)
                if t == T_SMALL:
                    pe.wait_ge(s_free[G_SMALL % 2], G_SMALL // 2 + 1)
                    pe.wait_ge(s_lo, RAW + t + 1)
                    wh, wl = (x[t % SPL][:, :, :].rearrange("p c n -> p (c n)") for x in (whi, wlo))
                    for c in range(DC):
                        w = slice(NSMALL * c, NSMALL * (c + 1))
                        ins = three(ps[G_SMALL % 2][0:NSMALL, 0, :], wh[:, w], wl[:, w], xh[:, c, :], xl[:, c, :], c == 0, c == DC - 1)
                    ins.then_inc(s_used, 1)
                else:
                    G, q = (t // 4, t % 4) if t < T_SMALL else (G_GATE + (t - T_GATE) // 4, (t - T_GATE) % 4)
                    if q == 0:
                        pe.wait_ge(s_free[G % 2], G // 2 + 1)
                    piece(0, t, ps[G % 2], lambda c: from_x(4 * q + c), q == 0, q == 3)
                if t % 8 == 1 and 4 * QKV_LOOP + 8 < t < B_IDX + 10:
                    if t == 4 * QKV_LOOP + 9:
                        pe.wait_ge(s_mod, 2)
                    modulation(0, ADA_START + QKV_LOOP + (t - 4 * QKV_LOOP) // 8 - 1)
            with pe.Fori(0, 4) as g:
                for k in range(2):
                    group(g * 4, g, T_WAB + 2 * k, G_WAB + k, H_CAT, n=2, k0=8 * k)
            pe.wait_ge(s_mod, 3)

            def wo_each(j):
                late = ADA_START + M_LATE // 8
                return lambda q: modulation(0, late + j - 1) if q == 0 and j else None
            for j in range(4):
                group(0, 0, T_WO + 4 * j, G_WO + j, H_MRG, each=wo_each(j))
                if j:
                    statistic(1, (2 * j - 2, 2 * j - 1))
            modulation(0, ADA_GROUPS - 1)
            statistic(1, (6, 7))
            for u in range(2):
                with pe.Fori(0, UPN[u]) as i:
                    for k in range(2):
                        group(i * 8, i, T_UP[u] + 4 * k, G_UP[u] + k, H_UP)

                for j in range(2):
                    pe.wait_ge(s_free[(G_DOWN[u] + j) % 2], (G_DOWN[u] + j) // 2 + 1)
                if u:
                    pe.wait_ge(s_dn, 2)

                def hidden(r, first):
                    pe.wait_ge(s_hidl, r + (UPN[0] * u + 2))
                    for q in range(4):
                        piece(r * 4, T_DOWN[u] + q, down_psum[q],
                              lambda c: (fh[:, bass.ds(r * 4 + c, 1), :], fl[:, bass.ds(r * 4 + c, 1), :]), first, True)

                hidden(0, True)
                with pe.Fori(1, UPN[u]) as r:
                    hidden(r, False)
            statistic(2, o=bank_d)
            statistic(3)
            for j in range(4):
                for k in range(2):
                    group(0, 0, T_PW1 + 8 * j + 4 * k, G_PW1 + 2 * j + k, H_PW1)
            for c in range(DC):
                if c % 4 == 0:
                    pe.wait_ge(s_dwd, 2 * TAPS * (c // 4 + 1))
                    pe.wait_ge(s_padd, 2 * TAPS * (c // 4 + 1))
                ins = mm(bank_o[:, 0:T], mean_w[:, :], ucv[:, c, :], start=c == 0, stop=c == DC - 1)
            ins.then_inc(s_mean, 1)
            statistic(4)
            for j in range(4):
                group(0, 0, T_PW2 + 4 * j, G_PW2 + j, H_PW2)
                if j:
                    statistic(5, (2 * j - 2, 2 * j - 1))
            statistic(5, (6, 7))
            for half in range(2):
                with pe.Fori(0, 4) as i:
                    for k in range(2):
                        group(i * 8, i, T_UP2[half] + 4 * k, G_UP2[half] + k, H_UP2)
                pe.wait_ge(s_hidl, FC // 4 + 8 * (half + 1) + 1)
                for j in range(4):
                    group(0, 0, T_DN2[half] + 8 * j, G_DN2[half] + j, None, n=8, rhs=lambda c: (gh[:, c, :], gl[:, c, :]))
                    if half and j:
                        statistic(6, (2 * j - 2, 2 * j - 1))
            statistic(6, (6, 7))
            for b in range(8):
                c, j = b // 4, b % 4
                pe.wait_ge(s_fin, DC if c else 4 * (j + 1))
                if b >= 2:
                    pe.wait_ge(s_fc, b - 1)
                for m in range(4):
                    ins = nc.tensor.transpose((bank_z, bank_f)[b % 2][:, P * m:P * (m + 1)], res[:, 4 * j + m, P * c:P * (c + 1)], ident)
                ins.then_inc(s_ft, 1)
    return nc


INPUTS = ["x", "c", "positions", "w_in", "w_a", "w_b", "w_o", "w_ada", "b_ada", "g_mix", "g_ffn", "w_up", "conv_w", "conv_b",
          "w_down", "g_final", "norm_mix_g_2", "norm_ffn_g_2", "final_norm_g_2", "conv_w_pw1_2", "conv_b_pw1_2", "conv_w_dw_2",
          "conv_b_dw_2", "conv_ln_g_2", "conv_ln_b_2", "conv_w_pw2_2", "conv_b_pw2_2", "ffn_w_up_2", "ffn_w_down_2"]


def kernel(**inputs):
    import concourse.bacc as bacc
    from concourse.bass_utils import run_bass_kernel_spmd

    nc = bacc.Bacc("TRN2", target_bir_lowering=False, num_devices=1)
    arrays = {name: np.ascontiguousarray(inputs[name]) for name in INPUTS}
    arrays["consts"] = shape_constants()
    aps = {name: nc.dram_tensor(f"in_{name}", a.shape, mybir.dt.from_np(a.dtype), kind="ExternalInput").ap() for name, a in arrays.items()}
    out = nc.dram_tensor("out", (1, T, D), F32, kind="ExternalOutput").ap()
    build(nc, aps, out)
    r = run_bass_kernel_spmd(nc, [{f"in_{name}": a for name, a in arrays.items()}], core_ids=[0])
    return r.results[0]["out"]
```

```python
from contextlib import ExitStack

import numpy as np
import concourse.bass as bass
from concourse import mybir

F32 = mybir.dt.float32
F32R = mybir.dt.float32r
I32 = mybir.dt.int32
ALU = mybir.AluOpType
ACT = mybir.ActivationFunctionType
AX_X = mybir.AxisListType.X

P = 128
T = 256
D = 2048
DC = D // P
HEADS = 8
IDX_HEADS = 16
TOPK = 64
TOP_ROUNDS = TOPK // 8
FF = 5632
FC = FF // P
FF2 = 8192
TAPS = 31
PAD = TAPS // 2
TP = T + 2 * PAD
SCALE = float(P) ** -0.5
EPS1, EPS2 = 1e-6, 1e-5
BIG = 1.0e30

KC = 4
NCOL = 512
RAW = 4
SPL = 2
ADA_START = 8
ADA_GROUPS = 6 * D // NCOL
ATT = 3 * HEADS * 2

T_SMALL = 14 * KC
T_GATE = T_SMALL + 1
T_WAB = T_GATE + 8 * KC
T_WO = T_WAB + 4 * KC
T_UP = T_WO + 4 * KC
UPN = [6, 5]
T_UP, T_DOWN = [T_WO + 4 * KC, 0], [T_WO + 4 * KC + 8 * UPN[0], 0]
T_UP[1] = T_DOWN[0] + 4 * UPN[0]
T_DOWN[1] = T_UP[1] + 8 * UPN[1]
T_PW1 = T_DOWN[1] + 4 * UPN[1]
T_PW2 = T_PW1 + 8 * KC
T_UP2 = [T_PW2 + 4 * KC, 0]
T_DN2 = [T_UP2[0] + 8 * KC, 0]
T_UP2[1] = T_DN2[0] + 4 * 8
T_DN2[1] = T_UP2[1] + 8 * KC
T_END = T_DN2[1] + 4 * 8
G_SMALL = 14
G_GATE = 15
G_WAB = 23
G_WO = 31
G_UP, G_DOWN = [35, 49], [47, 59]
G_PW1 = 61
G_PW2 = 69
G_UP2 = [73, 85]
G_DN2 = [81, 93]
PAIRED = (2, 3, 5, 6)
NPROD = 4
NDIAG = 32
COL_KI, COL_GATE = 7168, 7248
NSMALL = COL_GATE - COL_KI
IDX_SCALE = 0.125 * 0.25
ROUND = 1.5 * 2.0 ** 23
TWO_PI = 6.283185307179586
TWO_PI_PARTS = (6.28125, 0.0019340515136718750, 1.2556659146e-06)
PI_IN, HALF_PI = 3.1415925, 1.5707963267948966


def free_at(group):
    return group // 2 + 2


B_VTA = 24
B_STICK = 24
B_ROPE = 44
B_VTB = 52
B_ROPEI = 59
B_IDX = 64
B_DSA = 77
M_LATE = 88
M_WO = M_LATE + 4 * KC

def beside(t):
    def before(t):
        if t < 24:
            return 3 * t // 2
        if t < B_IDX + 8:
            return 36 + (t - 24) * 13 // 12
        return M_LATE if t < T_WO else M_WO + 3 * (t - T_WO) // 2
    return range(before(t), before(t + 1))


def sum_of(group):
    return group % 2 if group <= ADA_START + M_LATE // 8 else (group + 1) % 2


VECS = [("b_ada", 96), ("g_mix", 16), ("g_ffn", 16), ("conv_b", 88), ("conv_w", 264), ("g_final", 16),
        ("norm_mix_g_2", 16), ("norm_ffn_g_2", 16), ("final_norm_g_2", 16), ("conv_b_pw1_2", 32),
        ("conv_w_dw_2", 16 * TAPS), ("conv_b_dw_2", 16), ("conv_ln_g_2", 16), ("conv_ln_b_2", 16),
        ("conv_b_pw2_2", 16), ("c", 16)]
AT, _n = {}, 0
for _name, _rows in VECS:
    AT[_name] = _n
    _n += _rows
NV = _n
VB = NV // P
assert NV % P == 0

C_ID, C_SW128, C_SW64, C_TRI, C_PAST, C_NEG, C_FREQ, C_SIGN = 0, 128, 256, 384, 512, 896, 1280, 1282
NCONST = 1284


def shape_constants():
    c = np.zeros((P, NCONST), np.float32)
    i = np.arange(P)
    c[i, C_ID + i] = 1
    c[i, C_SW128 + (i + 64) % 128] = 1
    c[i, C_SW64 + (i // 64) * 64 + (i % 64 + 32) % 64] = 1
    c[:, C_TRI:C_TRI + P] = i[:, None] > i[None, :]
    past = (i[:, None] < i[None, :]).astype(np.float32)
    c[:, C_PAST:C_PAST + 384] = np.concatenate([past, np.ones_like(past), past], 1)
    ahead = np.where(i[None, :] <= i[:, None], 0, -BIG).astype(np.float32)
    c[:, C_NEG:C_NEG + 384] = np.concatenate([ahead, np.zeros_like(ahead), ahead], 1)
    for n, d in enumerate((128, 64)):
        f = 1.0 / (np.float32(10000.0) ** (np.arange(0, d, 2, dtype=np.float32) / np.float32(d)))
        c[:, C_FREQ + n] = f.astype(np.float32)[i % (d // 2)]
        c[:, C_SIGN + n] = np.where(i % d < d // 2, -1, 1)
    return c


def build(nc, A, out):
    ctx = ExitStack()
    with ctx:
        def sem(name):
            return ctx.enter_context(nc.semaphore(name))

        def sb(name, shape, dt=F32, scope=ctx):
            return scope.enter_context(nc.sbuf_tensor(name, shape, dt))

        raw = [sb(f"raw{s}", [P, KC, NCOL]) for s in range(RAW)]
        whi = [sb(f"whi{s}", [P, KC, NCOL], F32R) for s in range(SPL)]
        wlo = [sb(f"wlo{s}", [P, KC, NCOL], F32R) for s in range(SPL)]
        res = sb("res", [P, DC, T])
        xh = sb("xh", [P, DC, T], F32R)
        xl = sb("xl", [P, DC, T], F32R)
        cons = sb("cons", [P, NCONST])
        cols = sb("cols", [P, NV])
        ones = sb("ones", [P, P])
        mean_w = sb("mean_w", [P, P])
        mod = sb("mod", [P, ADA_GROUPS * 4])
        gmod = sb("gmod", [P, 2, DC])
        one_c = sb("one_c", [P, 1])
        zero_c = sb("zero_c", [P, 1])
        norm_rows = sb("norm_rows", [P, 4, T])
        varr, rstd, nwt, rstd_first = (norm_rows[:, i, :] for i in range(4))
        mod_sum = [norm_rows[:, 2 * i:2 * i + 2, :].rearrange("p a t -> p (a t)") for i in range(2)]
        warm = sb("warm", [P, 8])
        cact = sb("cact", [P, DC])
        gain2 = sb("gain2", [P, DC])
        gate = sb("gate", [P, 2, DC])
        sq = sb("sq", [P, 4, T])
        mixer = ExitStack()
        att = sb("att", [P, 64, T], F32, mixer)
        def ch(a, b=None):
            b = a + 1 if b is None else b
            return att[:, a:b, :].rearrange("p c t -> p (c t)")

        ada_first = [att[:, 32 + 8 * q:40 + 8 * q, :].rearrange("p (c m) t -> p c (m t)", c=KC) for q in range(KC)]
        ada, ada_late = ([att[:, a + 4 * s:a + 4 * s + 4, :].rearrange("p (c m) t -> p c (m t)", c=2) for s in range(2)]
                         for a in (56, 32))
        rope = sb("rope", [P, 4, T], F32, mixer)
        kidx = sb("kidx", [P, T], F32, mixer)
        wi = sb("wi", [P, 2, IDX_HEADS], F32, mixer)
        tA3, tB3 = sq[:, 0:2, :], sq[:, 2:4, :]
        tA, tB = (x.rearrange("p a t -> p (a t)") for x in (tA3, tB3))
        tCDE = sb("tCDE", [P, 3 * 384], F32, mixer)
        tC, tD, tE = (tCDE[:, 384 * i:384 * (i + 1)] for i in range(3))
        first_sum = [mod_sum, [tCDE[:, 0:NCOL], tCDE[:, NCOL:2 * NCOL]]]
        small = sb("small", [P, 32], F32, mixer)
        wi_t = tC[0:16, 0:T]
        rA, rB = ch(26, 28), ch(28, 30)
        posi, posf = att[0:1, 30, :].bitcast(I32), att[0:1, 31, :]
        mixer.close()
        ffn = ExitStack()
        fh = sb("fh", [P, 4 * UPN[0], T], F32R, ffn)
        fl = sb("fl", [P, 4 * UPN[0], T], F32R, ffn)
        ca = sb("ca", [P, 4, T], F32, ffn)
        cb = sb("cb", [P, 4, T], F32, ffn)
        ffn.close()
        blk2 = ExitStack()
        gh = sb("gh", [P, 32, T], F32R, blk2)
        gl = sb("gl", [P, 32, T], F32R, blk2)
        tmp = sb("tmp", [P, 4, T], F32, blk2)
        tmp2 = sb("tmp2", [P, 4, T], F32, blk2)
        blk2.close()
        conv = ExitStack()
        upad = sb("upad", [P, DC, TP], F32, conv)
        ucv = sb("ucv", [P, DC, T], F32, conv)
        pa = sb("pa", [P, 4, T], F32, conv)
        pg = sb("pg", [P, 4, T], F32, conv)
        prod = sb("prod", [P, NPROD, T], F32, conv)
        diag = sb("diag", [P, NDIAG, P], F32, conv)
        conv.close()

        ps = [ctx.enter_context(nc.psum_tensor(f"ps{i}", [P, 4, T], F32)) for i in range(2)]
        ms = [ctx.enter_context(nc.psum_tensor(f"ms{i}", [P, 4, T], F32)) for i in range(2)]
        bank_z, bank_f = ms[0][:, 0:2, :].rearrange("p a t -> p (a t)"), ms[0][:, 2:4, :].rearrange("p a t -> p (a t)")
        bank_o, bank_m = ms[1][:, 0:2, :].rearrange("p a t -> p (a t)"), ms[1][:, 2:4, :].rearrange("p a t -> p (a t)")

        down_psum = [ps[G_DOWN[0] % 2], ps[1 - G_DOWN[0] % 2], ms[0], ms[1]]
        out_banks = (bank_z, bank_f, bank_m, bank_o)
        tri = cons[:, C_TRI:C_TRI + P]
        ident = cons[:, C_ID:C_ID + P]
        past = cons[:, C_PAST:C_PAST + 384]
        ahead = cons[:, C_NEG:C_NEG + 384]

        def col(name, i):
            return cols[:, AT[name] + i:AT[name] + i + 1]

        def dcol(name, reg, i):
            return cols[:, bass.ds(reg + (AT[name] + i), 1)]

        def pair_sum(k, i):
            return (tmp if k == 6 else prod)[:, i % 2, :]

        s_in = [sem(f"input_landed{i}") for i in range(3)]
        s_vin = sem("vectors_landed")
        s_const = sem("constants_made")
        s_land = [sem(f"weights_landed{s}") for s in range(RAW)]
        s_hi = sem("piece_hi_made")
        s_lo = sem("piece_lo_made")
        s_used = sem("piece_multiplied")
        s_free = [sem(f"psum{s}_read_out") for s in range(2)]
        s_tr = sem("input_transposed")
        s_trc = sem("vectors_copied")
        s_trx = sem("input_copied")
        s_cact = sem("c_activated")
        s_adaring = [sem(f"first_modulation_landed{s}") for s in range(KC)]
        s_adaland = [sem(f"modulation_landed{s}") for s in range(2)]
        s_chain = sem("modulation_chunk_added")
        s_gemv = sem("modulation_group_summed")
        s_mod = sem("modulation_read_out")
        s_gsig = sem("conformer_gate_sigmoid")
        s_sq = sem("squares_made")
        s_acc = sem("squares_used")
        s_psum = sem("pair_sum_multiplied")
        s_mean = sem("layer_norm_mean")
        s_var = sem("variance_read")
        s_std = sem("root_made")
        s_nt = sem("normed_chunk_scaled")
        s_nh = sem("normed_chunk_hi")
        s_h = sem("input_chunk_split")
        s_v = sem("vector_step")
        s_a = sem("scalar_step")
        s_posf = sem("positions_converted")
        s_posb = sem("positions_spread")
        s_ang = sem("angles_reduced")
        s_sin = sem("sines_made")
        s_vt = sem("v_transposed")
        s_vtc = sem("v_copied")
        s_z = sem("stick_logits")
        s_soft = sem("stick_softplus_tail")
        s_lm = sem("stick_log_left")
        s_af = sem("stick_suffix_sum")
        s_w = sem("stick_exponent")
        s_we = sem("stick_weights")
        s_wm = sem("stick_weights_masked")
        s_o = sem("stick_output")
        s_oc = sem("stick_output_copied")
        s_rp = sem("rotary_swapped")
        s_rd = sem("rotary_done")
        s_ki = sem("index_key_copied")
        s_wt = sem("head_weights_turned")
        s_wtc = sem("head_weights_copied")
        s_dots = sem("index_dots")
        s_relu = sem("index_relu")
        s_score = sem("index_scored")
        s_L = sem("logits")
        s_lg = sem("logits_shifted")
        s_e = sem("exponentials")
        s_p = sem("probabilities")
        s_pt = sem("probabilities_turned")
        s_ptc = sem("probabilities_copied")
        s_ob = sem("selected_output")
        s_obc = sem("selected_output_copied")
        s_cathi = sem("attention_output_hi")
        s_sig = sem("gate_sigmoid")
        s_mrg = sem("branches_merged")
        s_cA = sem("conv_scaled")
        s_cS = sem("conv_summed")
        s_silu = sem("conv_gate")
        s_hid = sem("hidden_made")
        s_hidh = sem("hidden_hi")
        s_hidl = sem("hidden_split")
        s_u = sem("glu_chunk")
        s_prod = sem("tap_product")
        s_padd = sem("tap_added")
        s_dwd = sem("depthwise_chunk_by_vector")
        s_edge = sem("padding_cleared")
        s_diag = sem("tap_diagonal_made")
        s_diagu = sem("tap_diagonal_used")
        s_dwt = sem("depthwise_chunk_by_tensor")
        s_dwtc = sem("depthwise_chunk_copied")
        s_xc = sem("centred")
        s_y = sem("layer_norm_silu")
        s_dn = sem("down_read_out")
        s_fin = sem("final_scaled")
        s_ft = sem("final_transposed")
        s_fc = sem("final_copied")
        s_out = sem("output_stored")

        H_QKV, H_CAT, H_MRG, H_UP, H_PW1, H_PW2, H_UP2 = (DC * i for i in range(7))

        class Steps:

            def __init__(self, eng, sem_steps):
                self.eng, self.sem_steps, self.n = eng, sem_steps, 0

            def did(self, ins):
                ins.then_inc(self.sem_steps, 1)
                self.n += 1

            def wait(self, back=0):
                self.eng.wait_ge(self.sem_steps, self.n - back)

        vec_parts = []
        for name, rows in VECS:
            done = 0
            while done < rows:
                at = AT[name] + done
                n = min(rows - done, P - at % P)
                vec_parts.append((name, done, n, at))
                done += n

        block = ctx.enter_context(nc.Block())

        @block.sync
        def _(sp):
            for name, done, n, at in vec_parts:
                v = A[name]
                letters = "abc"[:len(v.shape)]
                flat = v.rearrange(f"{' '.join(letters)} -> ({' '.join(letters)})") if len(v.shape) > 1 else v
                sp.dma_start(att[at % P:at % P + n, 16 + at // P, 0:P],
                             flat.rearrange("(r p) -> r p", p=P)[done:done + n, :]).then_inc(s_vin, 16)
            sp.dma_start(cons[:, :], A["consts"]).then_inc(s_in[0], 16)
            sp.dma_start(posi, A["positions"]).then_inc(s_in[1], 16)
            def blocks(name, parts=KC):
                return A[name].rearrange("a (q c p) n -> (a q) p c n", p=P, c=parts)

            w_ada = blocks("w_ada")
            for q in range(KC):
                sp.dma_start(ada_first[q][:, :, :], w_ada[q][:, :, 0:NCOL]).then_inc(s_adaring[q], 16)
            x_in = A["x"].rearrange("b (c p) (h t) -> p (b c) h t", p=P, t=T)
            for c in range(2):
                sp.dma_start(att[:, 8 * c:8 * c + 8, :], x_in[:, c]).then_inc(s_in[2], 16)
            with sp.Fori(1, ADA_START) as g:
                for q in range(KC):
                    sp.wait_ge(s_chain, g * DC + KC * (q + 1))
                    sp.dma_start(ada_first[q][:, :, :], w_ada[q][:, :, bass.ds(g * NCOL, NCOL)]).then_inc(s_adaring[q], 16)

            def load(g, t, src):
                sp.wait_ge(s_lo, g + (t + 1))
                sp.dma_start(raw[t % RAW][:, :, :], src).then_inc(s_land[t % RAW], 16)

            def columns(base, n, w, first_col, nq, k0=0):
                with sp.Fori(0, n) as g:
                    for q in range(nq):
                        load(g * nq, base + q, w[k0 + q][:, :, bass.ds(g * NCOL + first_col, NCOL)])

            def pairs(base, n, w, half, col0=0):
                with sp.Fori(0, n) as g:
                    for k in range(2):
                        for q in range(KC):
                            load(g * (2 * KC), base + KC * k + q, w[q][:, :, bass.ds(g * NCOL + (half * k + col0), NCOL)])

            w_in = blocks("w_in")
            columns(0, 14, w_in, 0, KC)
            sp.wait_ge(s_lo, T_SMALL + 1)
            sp.dma_start(raw[T_SMALL % RAW][:, :, :].rearrange("p c n -> p (c n)")[:, 0:DC * NSMALL].rearrange("p (c n) -> p c n", c=DC),
                         A["w_in"].rearrange("a (c p) n -> p (a c) n", p=P)[:, :, COL_KI:COL_GATE]).then_inc(s_land[T_SMALL % RAW], 16)
            columns(T_GATE, 8, w_in, COL_GATE, KC)
            w_a, w_b = blocks("w_a"), blocks("w_b")
            with sp.Fori(0, 4) as g:
                for q in range(4):
                    load(g * 4, T_WAB + q, (w_a, w_b)[q // 2][q % 2][:, :, bass.ds(g * NCOL, NCOL)])
            columns(T_WO, 4, blocks("w_o"), 0, KC)
            w_dn = A["w_down"].rearrange("a (c p) n -> p (a c) n", p=P)
            for u in range(2):
                pairs(T_UP[u], UPN[u], blocks("w_up"), FF, NCOL * UPN[0] * u)
                with sp.Fori(0, UPN[u]) as r:
                    for q in range(4):
                        load(r * 4, T_DOWN[u] + q, w_dn[:, bass.ds(r * KC + KC * UPN[0] * u, KC), NCOL * q:NCOL * (q + 1)])
            pairs(T_PW1, 4, blocks("conv_w_pw1_2"), D)
            columns(T_PW2, 4, blocks("conv_w_pw2_2"), 0, KC)
            for half in range(2):
                columns(T_UP2[half], 8, blocks("ffn_w_up_2"), half * FF2 // 2, KC)
                columns(T_DN2[half], 4, blocks("ffn_w_down_2"), 0, 8, k0=8 * half)

            o2 = out.rearrange("b (c p) d -> (b c) p d", p=P)
            for c in range(2):
                for j in range(4):
                    sp.wait_ge(s_fc, 4 * c + j + 1)
                    sp.dma_start(o2[c][:, NCOL * j:NCOL * (j + 1)],
                                 ucv[:, 8 * c + 2 * j:8 * c + 2 * j + 2, :].rearrange("p a t -> p (a t)")).then_inc(s_out, 16)
            sp.wait_ge(s_out, 8 * 16)

        @block.gpsimd
        def _(pool):
            nc.gpsimd.memset(ones[:, :], 1.0).then_inc(s_const, 1)
            nc.gpsimd.memset(mean_w[:, :], 1.0 / D).then_inc(s_const, 1)
            nc.gpsimd.memset(one_c[:, :], 1.0).then_inc(s_const, 1)
            nc.gpsimd.memset(zero_c[:, :], 0.0).then_inc(s_const, 1)

            w_ada = A["w_ada"].rearrange("a (q c p) n -> (a q) p c n", p=P, c=2)

            def half_piece(m, slots=ada):
                pool.wait_ge(s_chain, DC * (1 + ADA_START) + 2 * max(0, m - 1))
                n = (m // 8 + ADA_START) * NCOL
                pool.dma_start(slots[m % 2][:, :, :], w_ada[m % 8][:, :, n:n + NCOL]).then_inc(s_adaland[m % 2], 16)

            for t in range(B_IDX + 8):
                for m in beside(t):
                    half_piece(m)
                h = (t - B_STICK) // 2 - 1
                if (t - B_STICK) % 2 == 0 and 0 <= h < HEADS:
                    pool.wait_ge(s_we, h + 1)
                    if h:
                        pool.wait_ge(s_o, h)
                    nc.gpsimd.tensor_tensor(tC[:, :], tE[:, :], past, ALU.mult).then_inc(s_wm, 1)
            pool.wait_ge(s_L, HEADS)
            for m in range(M_LATE, 8 * (ADA_GROUPS - ADA_START)):
                half_piece(m, ada_late)

            def add_pairs(k):
                for i in range(DC // 2):
                    n = 8 * PAIRED.index(k) + i
                    pool.wait_ge(s_sq, 8 * k + i + 1)
                    if n >= 2:
                        pool.wait_ge(s_psum, n - 1)
                    nc.gpsimd.tensor_tensor(pair_sum(k, i), sq[:, 2 * (i % 2), :], sq[:, 2 * (i % 2) + 1, :], ALU.add).then_inc(s_acc, 1)

            pool.wait_ge(s_used, SPL + T_PW1)
            add_pairs(2)
            add_pairs(3)
            pool.wait_ge(s_used, SPL + T_PW1)
            nc.gpsimd.memset(upad[:, :, 0:PAD], 0.0).then_inc(s_edge, 1)
            nc.gpsimd.memset(upad[:, :, PAD + T:TP], 0.0).then_inc(s_edge, 1)
            for j in range(3):
                for n in range(2 * TAPS):
                    dst, src = ucv[:, 4 * j + 2 * (n % 2) + 1, :], prod[:, n % NPROD, :]
                    pool.wait_ge(s_prod, 2 * TAPS * j + n + 1)
                    if n < 2:
                        nc.gpsimd.tensor_copy(dst, src).then_inc(s_padd, 1)
                    else:
                        pool.wait_ge(s_padd, 2 * TAPS * j + n - 1)
                        nc.gpsimd.tensor_tensor(dst, dst, src, ALU.add).then_inc(s_padd, 1)
            add_pairs(5)
            add_pairs(6)

        @block.scalar
        def _(act):
            st = Steps(act, s_a)

            def split_hi(g, t):
                act.wait_ge(s_land[t % RAW], g * 4 + 16 * (t // RAW + 1))
                act.wait_ge(s_used, g + (t + 1))
                nc.scalar.copy(whi[t % SPL][:, :, :], raw[t % RAW][:, :, :]).then_inc(s_hi, 1)

            def done(g, t):
                act.wait_ge(s_used, g + (SPL + t))

            def square(k, i, src=res):
                n = 8 * k + i
                if n >= 2:
                    act.wait_ge(s_acc, n - 1)
                nc.scalar.activation(sq[:, 2 * (i % 2):2 * (i % 2) + 2, :], src[:, 2 * i:2 * i + 2, :], ACT.Square).then_inc(s_sq, 1)

            def squares(k, ready, src=res):
                for i in range(DC // 2):
                    ready(i)
                    square(k, i, src)

            def root(n):
                nc.scalar.activation(warm[:, n:n + 1], one_c[:, 0:1], ACT.Sqrt)
                act.wait_ge(s_var, n + 1)
                nc.scalar.activation(rstd[:, :], varr[:, :], ACT.Sqrt).then_inc(s_std, 1)

            def gained_hi(chunks, gain):
                for c in chunks:
                    nc.scalar.activation(xh[:, c, :], res[:, c, :], ACT.Copy, scale=gain(c)).then_inc(s_nh, 1)

            def norm_hi(k, shift):
                for c in range(DC):
                    act.wait_ge(s_nt, DC * k + c + 1)
                    nc.scalar.activation(xh[:, c, :], sq[:, c % 4, :], ACT.Identity, bias=shift(c)).then_inc(s_nh, 1)

            act.wait_ge(s_trc, 3)
            nc.scalar.activation(cact[:, :], cols[:, AT["c"]:AT["c"] + DC], ACT.Silu).then_inc(s_cact, 1)
            for b in range(DC // 2):
                act.wait_ge(s_tr, 3 + b + 1)
                nc.scalar.copy(res[:, 2 * b:2 * b + 2, :].rearrange("p c t -> p (c t)"), (bank_z, bank_f)[(b + 3) % 2]).then_inc(s_trx, 1)
            squares(0, lambda i: act.wait_ge(s_trx, i + 1))
            act.wait_ge(s_ang, 1)
            for n in range(2):
                nc.scalar.activation(rope[:, 2 * n, :], rB[:, T * n:T * (n + 1)], ACT.Sin).then_inc(s_sin, 1)
                nc.scalar.activation(rope[:, 2 * n + 1, :], rA[:, T * n:T * (n + 1)], ACT.Sin).then_inc(s_sin, 1)
            split_hi(0, 0)
            split_hi(0, 1)
            root(0)
            norm_hi(0, lambda c: mod[:, c:c + 1])

            def read_out(g, group, t, dst):
                done(g, t)
                nc.scalar.copy(dst, ps[group % 2][:, :, :]).then_inc(s_free[group % 2], 1)

            def background(t):
                if B_VTA <= t < B_VTA + 4 or B_VTB <= t < B_VTB + 4:
                    j = t - B_VTA if t < B_VTB else t - B_VTB + 4
                    first = 16 + 2 * j if j < 4 else 40 + 2 * (j - 4)
                    act.wait_ge(s_vt, j + 1)
                    nc.scalar.copy(ch(first, first + 2), bank_o).then_inc(s_vtc, 1)
                h = (t - B_STICK) // 2
                if (t - B_STICK) % 2 == 0 and 1 <= h <= HEADS:
                    act.wait_ge(s_w, h)
                    if h > 1:
                        act.wait_ge(s_wm, h - 1)
                    nc.scalar.activation(tE[:, :], tD[:, :], ACT.Exp).then_inc(s_we, 1)
                if (t - B_STICK) % 2 == 0 and 0 <= h < HEADS:
                    act.wait_ge(s_z, h + 1)
                    if h:
                        act.wait_ge(s_lm, h)
                    st.did(nc.scalar.activation(tA[:, 0:384], bank_z[:, 0:384], ACT.Abs, scale=SCALE))
                    st.wait()
                    st.did(nc.scalar.activation(tA[:, 0:384], tA[:, 0:384], ACT.Exp, scale=-1.0))
                    st.wait()
                    nc.scalar.activation(tA[:, 0:384], tA[:, 0:384], ACT.Ln, bias=one_c[:, 0:1]).then_inc(s_soft, 1)
                if (t - B_STICK) % 2 == 0 and 2 <= h < HEADS + 2:
                    act.wait_ge(s_o, h - 1)
                    nc.scalar.copy(att[:, h - 2, :], bank_o[:, 0:T]).then_inc(s_oc, 1)
                if t == T_SMALL + 1:
                    done(0, T_SMALL + 1)
                    nc.scalar.copy(kidx[0:64, :], ps[0][0:64, 0, :]).then_inc(s_ki, 1)
                    nc.scalar.copy(kidx[64:128, :], ps[0][0:64, 0, :]).then_inc(s_ki, 1)
                    nc.scalar.copy(wi_t[:, :], ps[0][64:80, 0, :]).then_inc(s_free[0], 1)
                c = t - B_IDX
                if 0 <= c < 8:
                    act.wait_ge(s_dots, c + 1)
                    if c:
                        act.wait_ge(s_score, 4 * c)
                    nc.scalar.activation(tA[:, 0:384], bank_z[:, 0:384], ACT.Relu, scale=IDX_SCALE).then_inc(s_relu, 1)
                    nc.scalar.activation(tB[:, 0:384], bank_f[:, 0:384], ACT.Relu, scale=IDX_SCALE).then_inc(s_relu, 1)
                h = t - B_DSA
                if 0 <= h < HEADS:
                    act.wait_ge(s_lg, 2 * h + 2)
                    if h:
                        act.wait_ge(s_pt, h)
                    for b, (lo, hi) in enumerate(((0, P), (P, 384))):
                        nc.scalar.activation(tE[:, lo:hi], tD[:, lo:hi], ACT.Exp, bias=small[:, b:b + 1],
                                             accum_out=small[:, 4 + b:5 + b]).then_inc(s_e, 1)
                if 2 <= h < HEADS + 2:
                    act.wait_ge(s_ob, h - 1)
                    nc.scalar.copy(att[:, 24 + h - 2, :], bank_o[:, 0:T]).then_inc(s_obc, 1)

            for t in range(1, T_WAB + 1):
                split_hi(0, t + 1)
                if t <= T_SMALL and t % 4 == 0:
                    g = t // 4 - 1
                    read_out(0, g, t, att[:, 4 * g:4 * g + 4, :])
                if t > T_GATE and (t - T_GATE) % 4 == 0:
                    g = (t - T_GATE) // 4 - 1
                    first = 8 + 4 * g if g < 4 else 48 + 4 * (g - 4)
                    read_out(0, G_GATE + g, t, att[:, first:first + 4, :])
                background(t)
            done(0, T_WAB)
            for c, first in enumerate((0, 24)):
                act.wait_ge((s_oc, s_obc)[c], HEADS)
                nc.scalar.copy(xh[:, 8 * c:8 * c + 8, :], att[:, first:first + 8, :]).then_inc(s_cathi, 1)
            with act.Fori(0, 4) as g:
                for k in range(2):
                    gk = att[:, bass.ds(g * 4 + (8 + 40 * k), 4), :]
                    nc.scalar.activation(gk, gk, ACT.Sigmoid).then_inc(s_sig, 1)
                for q in range(2, 6):
                    split_hi(g * 4, T_WAB + q)
            done(0, T_WO)
            for j in range(4):
                act.wait_ge(s_mrg, j + 1)
                nc.scalar.copy(xh[:, 4 * j:4 * j + 4, :], att[:, 8 + 4 * j:12 + 4 * j, :]).then_inc(s_cathi, 1)
            for j in range(4):
                for q in range(2, 6):
                    split_hi(0, T_WO + 4 * j + q)
                act.wait_ge(s_free[(G_WO + j) % 2], free_at(G_WO + j))
                for i in range(2):
                    square(1, 2 * j + i)
            root(1)

            norm_hi(1, lambda c: mod[:, 3 * DC + c:3 * DC + c + 1])

            for u in range(2):
                b0 = UPN[0] * u
                split_hi(0, T_UP[u] + 2)
                with act.Fori(0, UPN[u]) as i:
                    for k in range(2):
                        for q in range(3, 6 + k):
                            split_hi(i * 8, T_UP[u] + 3 * k + q)
                            if k == 1 and q == 3:
                                act.wait_ge(s_free[G_UP[u] % 2], i + free_at(G_UP[u]))
                                nc.scalar.activation(ca[:, :, :], ca[:, :, :], ACT.Silu).then_inc(s_silu, 1)
                        done(i * 8, T_UP[u] + 4 * (k + 1))
                        if k == 0:
                            act.wait_ge(s_hidl, i + (b0 + 1))
                        for m in range(4):
                            nc.scalar.activation((ca, cb)[k][:, m, :], ps[(G_UP[u] + k) % 2][:, m, :], ACT.Identity,
                                                 scale=dcol("conv_w", i * 4, (4 + k) * FC + 4 * b0 + m),
                                                 bias=dcol("conv_b", i * 4, k * FC + 4 * b0 + m)).then_inc(s_cA, 1)
                    split_hi(i * 8, T_UP[u] + 10)
                    act.wait_ge(s_hid, i + (b0 + 1))
                    nc.scalar.copy(fh[:, bass.ds(i * 4, 4), :], ca[:, :, :]).then_inc(s_hidh, 1)
                for q in range(3, 6):
                    split_hi(0, T_DOWN[u] + q)
                with act.Fori(1, UPN[u]) as r:
                    for q in range(2, 6):
                        split_hi(r * 4, T_DOWN[u] + q)
            for j in range(4):
                par = (G_DOWN[1] + j) % 2
                act.wait_ge(*((s_free[par], free_at(G_DOWN[1] + j)) if j < 2 else (s_dn, j + 1)))
                gained_hi(range(4 * j, 4 * j + 4), lambda c: gain2[:, c:c + 1])
            square(2, 0)
            square(2, 1)

            def square_gained(i):
                act.wait_ge(s_acc, 8 * 3 + i - 1)
                for m in range(2):
                    c = 2 * i + m
                    ins = nc.scalar.activation(sq[:, 2 * (i % 2) + m, :], res[:, c, :], ACT.Square, scale=col("g_final", c))
                ins.then_inc(s_sq, 1)

            def products(j, lo, hi):
                for n in range(lo, hi):
                    tap, k = n // 2, n % 2
                    c = 4 * j + 2 * k + 1
                    if n == 0:
                        act.wait_ge(s_u, 4 * j + 4)
                        act.wait_ge(s_edge, 2)
                    if j or n >= NPROD:
                        act.wait_ge(s_padd, 2 * TAPS * j + max(0, n - NPROD + 1))
                    dst, src, w = prod[:, n % NPROD, :], upad[:, c, tap:tap + T], col("conv_w_dw_2", DC * tap + c)
                    if tap == 0:
                        nc.scalar.activation(dst, src, ACT.Identity, scale=w, bias=col("conv_b_dw_2", c)).then_inc(s_prod, 1)
                    else:
                        nc.scalar.activation(dst, src, ACT.Copy, scale=w).then_inc(s_prod, 1)

            def diagonals(lo, hi):
                for n in range(lo, hi):
                    if n >= NDIAG:
                        act.wait_ge(s_diagu, n - NDIAG + 1)
                    nc.scalar.activation(diag[:, n % NDIAG, :], ident, ACT.Copy,
                                         scale=col("conv_w_dw_2", DC * (n % TAPS) + DC - 3 + 2 * (n // TAPS))).then_inc(s_diag, 1)

            per = -(-2 * TAPS // 8)
            act.wait_ge(s_used, SPL + T_PW1)
            for j in range(4):
                for q in range(2, 10):
                    split_hi(0, T_PW1 + 8 * j + q)
                    if j == 0 and q == 3:
                        for i in range(2, 8):
                            square(2, i)
                        root(2)
                        square_gained(0)
                        square_gained(1)
                    if j == 0 and q == 5:
                        for i in range(2, 8):
                            square_gained(i)
                        root(3)
                    if j == 0:
                        diagonals(NDIAG // 8 * (q - 2), NDIAG // 8 * (q - 1))
                    else:
                        products(j - 1, min(2 * TAPS, (q - 2) * per), min(2 * TAPS, (q - 1) * per))
                act.wait_ge(s_free[(G_PW1 + 1) % 2], free_at(G_PW1 + 1 + 2 * j))
                for m in range(4):
                    ins = nc.scalar.activation(pg[:, m, :], pg[:, m, :], ACT.Sigmoid, bias=col("conv_b_pw1_2", DC + 4 * j + m))
                ins.then_inc(s_gsig, 1)
            diagonals(NDIAG, 2 * TAPS)
            for k in range(2):
                c = DC - 3 + 2 * k
                act.wait_ge(s_dwt, k + 1)
                nc.scalar.activation(ucv[:, c, :], ms[0][:, 2 * k, :], ACT.Identity, bias=col("conv_b_dw_2", c)).then_inc(s_dwtc, 1)
            squares(4, lambda i: act.wait_ge(s_xc, i // 2 + 1), ucv)
            root(4)
            for c in range(DC):
                act.wait_ge(s_nt, DC * 2 + c + 1)
                for dst in (ucv, xh):
                    nc.scalar.activation(dst[:, c, :], sq[:, c % 4, :], ACT.Silu, bias=col("conv_ln_b_2", c)).then_inc(s_y, 1)
            for j in range(4):
                for q in range(2, 6):
                    split_hi(0, T_PW2 + 4 * j + q)
                    if j == 3 and q < 5:
                        gained_hi(range(4 * (q - 2), 4 * (q - 1)), lambda c: col("norm_ffn_g_2", c))
                act.wait_ge(s_free[(G_PW2 + j) % 2], free_at(G_PW2 + j))
                if j == 3:
                    gained_hi(range(12, 16), lambda c: col("norm_ffn_g_2", c))
                for i in range(2):
                    square(5, 2 * j + i)
            def up2(i, half):
                for k in range(2):
                    for q in range(3, 6):
                        split_hi(i * 8, T_UP2[half] + 4 * k + q)
                    split_hi(i * 8, T_UP2[half] + 4 * k + 6)
                    act.wait_ge(s_hid, i * 2 + (FC // 4 + 8 * half + k + 1))
                    nc.scalar.copy(gh[:, bass.ds(i * 8 + 4 * k, 4), :], tmp2[:, :, :]).then_inc(s_hidh, 1)

            for half in range(2):
                split_hi(0, T_UP2[half] + 2)
                if half == 0:
                    root(5)
                with act.Fori(0, 4) as i:
                    up2(i, half)
                for j in range(4):
                    for q in range(2 if j else 3, 10):
                        t = T_DN2[half] + 8 * j + q
                        if t < T_END:
                            split_hi(0, t)
                    if half == 1:
                        act.wait_ge(s_free[(G_DN2[1] + j) % 2], free_at(G_DN2[1] + j))
                        for i in range(2):
                            square(6, 2 * j + i)
            root(6)
            for b in range(8):
                act.wait_ge(s_ft, b + 1)
                nc.scalar.copy(ucv[:, 2 * b:2 * b + 2, :].rearrange("p a t -> p (a t)"), out_banks[b % 4]).then_inc(s_fc, 1)

        @block.vector
        def _(dve):
            sv = Steps(dve, s_v)
            dve.sem_inc(s_lo, RAW)
            dve.sem_inc(s_chain, DC)
            for s in (s_hidl, *s_free):
                dve.sem_inc(s, 1)

            def split_lo(g, t):
                dve.wait_ge(s_hi, g + (t + 1))
                nc.vector.tensor_tensor(wlo[t % SPL][:, :, :], raw[t % RAW][:, :, :], whi[t % SPL][:, :, :].bitcast(F32),
                                        ALU.subtract).then_inc(s_lo, 1)

            def done(g, t):
                dve.wait_ge(s_used, g + (SPL + t))

            def root(n, eps, after=None):
                if n in PAIRED:
                    dve.wait_ge(s_psum, 8 * (PAIRED.index(n) + 1))
                else:
                    dve.wait_ge(s_acc, 8 * (n + 1))
                var = bank_o[:, 0:T]
                if after is not None:
                    sv.did(nc.vector.tensor_tensor(nwt[:, :], after, after, ALU.mult))
                    sv.wait()
                    sv.did(nc.vector.tensor_tensor(nwt[:, :], var, nwt[:, :], ALU.mult))
                    sv.wait()
                    var = nwt[:, :]
                nc.vector.tensor_scalar(varr[:, :], var, eps, None, ALU.add).then_inc(s_var, 1)
                dve.wait_ge(s_std, n + 1)
                sv.did(nc.vector.reciprocal(rstd[:, :], rstd[:, :]))
                sv.wait()
                sv.did(nc.vector.tensor_tensor(nwt[:, :], rstd[:, :], rstd[:, :], ALU.mult))
                sv.wait()
                sv.did(nc.vector.scalar_tensor_tensor(nwt[:, :], nwt[:, :], -0.5, varr[:, :], ALU.mult, ALU.mult))
                sv.wait()
                sv.did(nc.vector.scalar_tensor_tensor(rstd[:, :], nwt[:, :], 1.5, rstd[:, :], ALU.add, ALU.mult))
                sv.wait()

            def gained_lo(chunks, k_hi, gain):
                for c in chunks:
                    dve.wait_ge(s_nh, DC * k_hi + c + 1)
                    nc.vector.scalar_tensor_tensor(xl[:, c, :], res[:, c, :], gain(c), xh[:, c, :].bitcast(F32), ALU.mult, ALU.subtract).then_inc(s_h, 1)

            def norm_split(k, k_hi, h0, gain, shift, src=res):
                def scaled(c):
                    nc.vector.scalar_tensor_tensor(sq[:, c % 4, :], src[:, c, :], gain(c), rstd[:, :], ALU.mult, ALU.mult).then_inc(s_nt, 1)
                for c in range(2):
                    scaled(c)
                for c in range(DC):
                    if c + 2 < DC:
                        if c >= 2:
                            dve.wait_ge(s_h, h0 + c - 1)
                        scaled(c + 2)
                    dve.wait_ge(s_nt, DC * k + c + 1)
                    dve.wait_ge(s_nh, DC * k_hi + c + 1)
                    nc.vector.scalar_tensor_tensor(xl[:, c, :], sq[:, c % 4, :], shift(c), xh[:, c, :].bitcast(F32),
                                                   ALU.add, ALU.subtract).then_inc(s_h, 1)

            for b in range(3):
                dve.wait_ge(s_tr, b + 1)
                n = min(4, VB - 4 * b) * P
                nc.vector.tensor_copy(cols[:, 4 * P * b:4 * P * b + n], (bank_z, bank_f)[b % 2][:, 0:n]).then_inc(s_trc, 1)
            dve.wait_ge(s_in[1], 16)
            nc.vector.tensor_copy(posf, posi).then_inc(s_posf, 1)
            dve.wait_ge(s_posb, 1)
            dve.wait_ge(s_in[0], 16)
            for n in range(2):
                sv.did(nc.vector.tensor_scalar(rA[:, T * n:T * (n + 1)], bank_o[:, 0:T], cons[:, C_FREQ + n:C_FREQ + n + 1], None, ALU.mult))
            sv.wait()
            sv.did(nc.vector.tensor_scalar(rB, rA, 1.0 / TWO_PI, ROUND, ALU.mult, ALU.add))
            sv.wait()
            sv.did(nc.vector.tensor_scalar(rB, rB, ROUND, None, ALU.subtract))
            for part in TWO_PI_PARTS:
                sv.wait()
                sv.did(nc.vector.scalar_tensor_tensor(rA, rB, -part, rA, ALU.mult, ALU.add))
            sv.wait()
            sv.did(nc.vector.tensor_scalar(rA, rA, PI_IN, -PI_IN, ALU.min, ALU.max))
            sv.wait()
            sv.did(nc.vector.scalar_tensor_tensor(rB, rA, -1.0, rA, ALU.mult, ALU.min))
            sv.wait()
            nc.vector.tensor_scalar(rB, rB, HALF_PI, None, ALU.add).then_inc(s_ang, 1)

            def add_product(sums, w, kc, g, n, back=1):
                cx = cact[:, kc:kc + 1]
                if kc < back:
                    ins = nc.vector.tensor_scalar(sums, w, cx, None, ALU.mult)
                else:
                    dve.wait_ge(s_chain, g + (n + 1 - back))
                    ins = nc.vector.scalar_tensor_tensor(sums, w, cx, sums, ALU.mult, ALU.add)
                ins.then_inc(s_chain, 1)

            def half_piece(m, slots=ada, g=0, apart=2):
                group = ADA_START + m // 8
                if m % 8 == 0:
                    dve.wait_ge(s_gemv, g + (group + 3 - apart))
                dve.wait_ge(s_adaland[m % 2], g * 64 + 16 * (m // 2 + 1))
                for c in range(2):
                    add_product(mod_sum[sum_of(group)], slots[m % 2][:, c, :], 2 * (m % 8) + c, g * DC, DC * (1 + ADA_START) + 2 * m + c)

            def read_modulation(a, b):
                dve.wait_ge(s_gemv, 2 + b)
                c = slice(4 * a, 4 * b)
                nc.vector.tensor_tensor(mod[:, c], bank_m[:, c], cols[:, AT["b_ada"] + 4 * a:AT["b_ada"] + 4 * b], ALU.add).then_inc(s_mod, 1)

            dve.wait_ge(s_cact, 1)
            with dve.Fori(0, ADA_START // 2) as i:
                for par in range(2):
                    dve.wait_ge(s_gemv, i * 2 + (par + 1))
                    for q in range(KC):
                        dve.wait_ge(s_adaring[q], i * 32 + (16 * par + 16))
                        for c in range(KC):
                            kc = KC * q + c
                            add_product(first_sum[par][c % 2], ada_first[q][:, c, :], kc, i * 32, DC * (1 + par) + kc, back=2)
            dve.wait_ge(s_sin, 4)
            for n in range(2):
                sv.did(nc.vector.tensor_scalar(rope[:, 2 * n + 1, :], rope[:, 2 * n + 1, :], cons[:, C_SIGN + n:C_SIGN + n + 1], None, ALU.mult))
            read_modulation(0, ADA_START)
            dve.wait_ge(s_mod, 1)
            sv.did(nc.vector.scalar_tensor_tensor(gmod[:, 0, :], mod[:, DC:2 * DC], 1.0, cols[:, AT["g_mix"]:AT["g_mix"] + DC],
                                                  ALU.add, ALU.mult))
            split_lo(0, 0)
            split_lo(0, 1)
            root(0, EPS1)
            norm_split(0, 0, H_QKV, lambda c: gmod[:, 0, c:c + 1], lambda c: mod[:, c:c + 1])

            def rotate(r):
                key = r == 12
                n = 1 if key else 2
                x = kidx[:, :].unsqueeze(1) if key else (att[:, 24 + 2 * r:26 + 2 * r, :] if r < 8 else att[:, 48 + 2 * (r - 8):50 + 2 * (r - 8), :])
                k = 0 if r < 8 else 2
                cos = rope[:, k:k + 1, :].to_broadcast([P, n, T])
                sin = rope[:, k + 1:k + 2, :].to_broadcast([P, n, T])
                dve.wait_ge(s_rp, r + 1)
                sv.did(nc.vector.tensor_tensor(tA3[:, 0:n, :], x, cos, ALU.mult))
                sv.did(nc.vector.tensor_tensor(tB3[:, 0:n, :], ms[0][:, 0:n, :], sin, ALU.mult))
                sv.wait()
                nc.vector.tensor_tensor(x, tA3[:, 0:n, :], tB3[:, 0:n, :], ALU.add).then_inc(s_rd, 1)

            BLK = ((0, P), (P, 384))

            def background_first(t):
                h = t - B_DSA
                if 0 <= h < HEADS:
                    dve.wait_ge(s_L, h + 1)
                    if h:
                        dve.wait_ge(s_e, 2 * h)
                    sv.did(nc.vector.scalar_tensor_tensor(tD[:, :], bank_z[:, 0:384], SCALE, tC[:, :], ALU.mult, ALU.add))
                    sv.wait()
                    for b, (lo, hi) in enumerate(BLK):
                        nc.vector.tensor_reduce(small[:, b:b + 1], tD[:, lo:hi], AX_X, ALU.max, negate=True).then_inc(s_lg, 1)

            def background(t):
                h = (t - B_STICK) // 2
                if (t - B_STICK) % 2 == 0 and 1 <= h <= HEADS:
                    dve.wait_ge(s_af, h)
                    nc.vector.tensor_tensor(tD[:, :], tD[:, :], bank_f[:, 0:384], ALU.add).then_inc(s_w, 1)
                if (t - B_STICK) % 2 == 0 and 0 <= h < HEADS:
                    dve.wait_ge(s_soft, h + 1)
                    sv.did(nc.vector.tensor_scalar(tB[:, 0:384], bank_z[:, 0:384], SCALE, 0.0, ALU.mult, ALU.max))
                    sv.wait()
                    sv.did(nc.vector.tensor_tensor(tB[:, 0:384], tB[:, 0:384], tA[:, 0:384], ALU.add))
                    if h:
                        dve.wait_ge(s_we, h)
                    sv.wait()
                    sv.did(nc.vector.scalar_tensor_tensor(tD[:, :], bank_z[:, 0:384], SCALE, tB[:, 0:384], ALU.mult, ALU.subtract))
                    sv.wait()
                    nc.vector.scalar_tensor_tensor(tB[:, 0:384], tB[:, 0:384], -1.0, past, ALU.mult, ALU.mult).then_inc(s_lm, 1)
                if t == B_STICK + 8:
                    read_modulation(ADA_START, ADA_START + 5)
                if t == B_DSA + 1:
                    read_modulation(ADA_START + 5, ADA_START + M_LATE // 8)
                    dve.wait_ge(s_mod, 3)
                    sv.did(nc.vector.tensor_scalar(gate[:, 0, :], mod[:, 2 * DC:3 * DC], 1.0, None, ALU.add))
                if B_ROPE <= t < B_ROPE + 8:
                    rotate(t - B_ROPE)
                if B_ROPEI <= t < B_ROPEI + 5:
                    rotate(t - B_ROPEI + 8)
                if t == B_ROPEI + 4:
                    dve.wait_ge(s_wt, 1)
                    nc.vector.tensor_copy(wi[:, :, :].rearrange("p a h -> p (a h)"), bank_f[:, 0:2 * IDX_HEADS]).then_inc(s_wtc, 1)
                c = t - B_IDX
                if 0 <= c < 8:
                    dve.wait_ge(s_relu, 2 * c + 2)
                    if c == 0:
                        dve.wait_ge(s_wtc, 1)
                    for k in range(2):
                        i = 2 * c + k
                        for b, (lo, hi) in enumerate(BLK):
                            src = (tA, tB)[k][:, lo:hi]
                            if i == 0:
                                nc.vector.tensor_scalar(tD[:, lo:hi], src, wi[:, b, i:i + 1], None, ALU.mult).then_inc(s_score, 1)
                            else:
                                dve.wait_ge(s_score, 2 * i + b - 1)
                                nc.vector.scalar_tensor_tensor(tD[:, lo:hi], src, wi[:, b, i:i + 1], tD[:, lo:hi],
                                                               ALU.mult, ALU.add).then_inc(s_score, 1)
                r = t - (B_IDX + 8)
                if r == 0:
                    dve.wait_ge(s_score, 2 * IDX_HEADS)
                    sv.did(nc.vector.tensor_tensor(tE[:, :], tD[:, :], ahead, ALU.add))
                    sv.wait()
                    sv.did(nc.vector.tensor_copy(tC[:, :], tE[:, :]))
                if 0 <= r < 4:
                    for last in range(2 * r, 2 * r + 2):
                        sv.wait()
                        for b, (lo, hi) in enumerate(BLK):
                            sv.did(nc.vector.max(small[:, 8 + 8 * b:16 + 8 * b], tC[:, lo:hi]))
                        if last < TOP_ROUNDS - 1:
                            for b, (lo, hi) in enumerate(BLK):
                                sv.wait(1)
                                sv.did(nc.vector.match_replace(tC[:, lo:hi], small[:, 8 + 8 * b:16 + 8 * b], tC[:, lo:hi], -3.0e38))
                if r == 4:
                    for b, (lo, hi) in enumerate(BLK):
                        thr, cnt = small[:, 15 + 8 * b:16 + 8 * b], small[:, 24 + b:25 + b]
                        sv.wait()
                        sv.did(nc.vector.tensor_scalar(tC[:, lo:hi], tE[:, lo:hi], thr, 0.0, ALU.is_gt, ALU.add, accum_out=cnt))
                        sv.did(nc.vector.tensor_scalar(tA[:, lo:hi], tE[:, lo:hi], thr, None, ALU.is_equal))
                        sv.wait()
                        sv.did(nc.vector.tensor_scalar(cnt, cnt, -1.0, float(TOPK), ALU.mult, ALU.add))
                        sv.did(nc.vector.tensor_tensor_scan(tB[:, lo:hi], tA[:, lo:hi], tA[:, lo:hi], 0.0, ALU.add, ALU.max))
                        sv.wait()
                        sv.did(nc.vector.scalar_tensor_tensor(tB[:, lo:hi], tB[:, lo:hi], cnt, tA[:, lo:hi], ALU.is_le, ALU.mult))
                        sv.wait()
                        sv.did(nc.vector.tensor_tensor(tC[:, lo:hi], tC[:, lo:hi], tB[:, lo:hi], ALU.add))
                        sv.wait()
                        sv.did(nc.vector.tensor_scalar(tC[:, lo:hi], tC[:, lo:hi], 1.0, BIG, ALU.subtract, ALU.mult))
                    sv.wait()
                    sv.did(nc.vector.tensor_tensor(tC[:, :], tC[:, :], ahead, ALU.add))
                    sv.wait()
                h = t - B_DSA
                if 0 <= h < HEADS:
                    dve.wait_ge(s_e, 2 * h + 2)
                    sv.did(nc.vector.reciprocal(small[:, 6:8], small[:, 4:6]))
                    sv.wait()
                    for b, (lo, hi) in enumerate(BLK):
                        ins = nc.vector.tensor_scalar(tE[:, lo:hi], tE[:, lo:hi], small[:, 6 + b:7 + b], None, ALU.mult)
                        ins.then_inc(s_p, 1)
                if 1 <= h <= HEADS:
                    dve.wait_ge(s_pt, h)
                    if h > 1:
                        dve.wait_ge(s_ob, h - 1)
                    nc.vector.tensor_copy(tA[:, 0:384], bank_f[:, 0:384]).then_inc(s_ptc, 1)

            for m in beside(0):
                half_piece(m)
            for t in range(1, T_WAB + 1):
                background_first(t)
                if t < T_WAB:
                    for m in beside(t):
                        half_piece(m)
                split_lo(0, t + 1)
                background(t)
            done(0, T_WAB)
            for c, first in enumerate((0, 24)):
                dve.wait_ge(s_cathi, c + 1)
                ins = nc.vector.tensor_tensor(xl[:, 8 * c:8 * c + 8, :], att[:, first:first + 8, :], xh[:, 8 * c:8 * c + 8, :].bitcast(F32), ALU.subtract)
                ins.then_inc(s_h, 8)
            with dve.Fori(0, 2) as g:
                for e in range(2):
                    for q in range(2, 6):
                        half_piece(M_LATE + 4 * e + q - 2, ada_late, g, apart=1)
                        split_lo(g * 8, T_WAB + 4 * e + q)
                        if q % 2:
                            k = q // 2 - 1
                            gk = att[:, bass.ds(g * 8 + (8 + 40 * k + 4 * e), 4), :]
                            par = (G_WAB + k) % 2
                            done(g * 8, T_WAB + 4 * e + 2 * (k + 1))
                            dve.wait_ge(s_sig, g * 4 + (2 * e + k + 1))
                            nc.vector.tensor_tensor(gk, gk, ps[par][:, :, :], ALU.mult).then_inc(s_free[par], 1)
                    ga = att[:, bass.ds(g * 8 + (8 + 4 * e), 4), :]
                    for k in range(2):
                        dve.wait_ge(s_free[(G_WAB + k) % 2], g * 2 + (e + free_at(G_WAB + k)))
                    nc.vector.tensor_tensor(ga, ga, gk, ALU.add).then_inc(s_mrg, 1)
            done(0, T_WO)
            for j in range(4):
                dve.wait_ge(s_cathi, 2 + j + 1)
                nc.vector.tensor_tensor(xl[:, 4 * j:4 * j + 4, :], att[:, 8 + 4 * j:12 + 4 * j, :], xh[:, 4 * j:4 * j + 4, :].bitcast(F32),
                                        ALU.subtract).then_inc(s_h, 4)

            for j in range(4):
                for q in range(2, 6):
                    for m in beside(T_WO + 4 * j + q - 2):
                        half_piece(m, ada_late)
                    split_lo(0, T_WO + 4 * j + q)
                done(0, T_WO + 4 * (j + 1))
                for m in range(4):
                    c = 4 * j + m
                    ins = nc.vector.scalar_tensor_tensor(res[:, c, :], ps[(G_WO + j) % 2][:, m, :], gate[:, 0, c:c + 1], res[:, c, :], ALU.mult, ALU.add)
                ins.then_inc(s_free[(G_WO + j) % 2], 1)
            read_modulation(ADA_START + M_LATE // 8, ADA_GROUPS)
            dve.wait_ge(s_mod, 4)
            sv.did(nc.vector.scalar_tensor_tensor(gmod[:, 1, :], mod[:, 4 * DC:5 * DC], 1.0, cols[:, AT["g_ffn"]:AT["g_ffn"] + DC],
                                                  ALU.add, ALU.mult))
            sv.did(nc.vector.tensor_scalar(gate[:, 1, :], mod[:, 5 * DC:6 * DC], 1.0, None, ALU.add))
            sv.did(nc.vector.tensor_tensor(gain2[:, :], cols[:, AT["g_final"]:AT["g_final"] + DC],
                                           cols[:, AT["norm_mix_g_2"]:AT["norm_mix_g_2"] + DC], ALU.mult))
            root(1, EPS1)
            norm_split(1, 1, H_UP, lambda c: gmod[:, 1, c:c + 1], lambda c: mod[:, 3 * DC + c:3 * DC + c + 1])

            def down_out(u, j):
                for m in range(4):
                    c = 4 * j + m
                    ins = nc.vector.scalar_tensor_tensor(res[:, c, :], down_psum[j][:, m, :], gate[:, 1, c:c + 1], res[:, c, :], ALU.mult, ALU.add)
                ins.then_inc(s_free[(G_DOWN[u] + j) % 2] if j < 2 else s_dn, 1)

            for u in range(2):
                b0 = UPN[0] * u
                split_lo(0, T_UP[u] + 2)
                with dve.Fori(0, UPN[u]) as i:
                    for k in range(2):
                        for q in range(3, 6 + k):
                            split_lo(i * 8, T_UP[u] + 3 * k + q)
                        cx, par = (ca, cb)[k], (G_UP[u] + k) % 2
                        for m in range(4):
                            dve.wait_ge(s_cA, i * 8 + (8 * b0 + 4 * k + m - m % 2 + 2))
                            nc.vector.scalar_tensor_tensor(cx[:, m, 1:T], ps[par][:, m, 0:T - 1], dcol("conv_w", i * 4, 2 * FC + k * FC + 4 * b0 + m),
                                                           cx[:, m, 1:T], ALU.mult, ALU.add).then_inc(s_cS, 1)
                        for m in range(4):
                            dve.wait_ge(s_cS, i * 8 + (8 * b0 + 4 * k + m + 1))
                            ins = nc.vector.scalar_tensor_tensor(cx[:, m, 2:T], ps[par][:, m, 0:T - 2], dcol("conv_w", i * 4, k * FC + 4 * b0 + m),
                                                                 cx[:, m, 2:T], ALU.mult, ALU.add)
                        ins.then_inc(s_free[par], 1)
                    dve.wait_ge(s_silu, i + (b0 + 1))
                    dve.wait_ge(s_free[(G_UP[u] + 1) % 2], i + free_at(G_UP[u] + 1))
                    nc.vector.tensor_tensor(ca[:, :, :], ca[:, :, :], cb[:, :, :], ALU.mult).then_inc(s_hid, 1)
                    split_lo(i * 8, T_UP[u] + 10)
                    dve.wait_ge(s_hidh, i + (b0 + 1))
                    nc.vector.tensor_tensor(fl[:, bass.ds(i * 4, 4), :], ca[:, :, :], fh[:, bass.ds(i * 4, 4), :].bitcast(F32),
                                            ALU.subtract).then_inc(s_hidl, 1)
                for q in range(3, 6):
                    split_lo(0, T_DOWN[u] + q)
                with dve.Fori(1, UPN[u]) as r:
                    for q in range(2, 6):
                        split_lo(r * 4, T_DOWN[u] + q)
                done(0, T_DOWN[u] + 4 * UPN[u])
                if u == 0:
                    for j in range(4):
                        down_out(0, j)
            down_out(1, 0)
            for j in range(4):
                if j < 3:
                    down_out(1, j + 1)
                gained_lo(range(4 * j, 4 * j + 4), 2, lambda c: gain2[:, c:c + 1])

            def glu(j):
                dve.wait_ge(s_gsig, j + 1)
                dve.wait_ge(s_free[G_PW1 % 2], free_at(G_PW1 + 2 * j))
                for m in range(4):
                    c = 4 * j + m
                    nc.vector.scalar_tensor_tensor(upad[:, c, PAD:PAD + T], pa[:, m, :], col("conv_b_pw1_2", c), pg[:, m, :],
                                                   ALU.add, ALU.mult).then_inc(s_u, 1)

            def taps(j, lo, hi):
                for n in range(lo, hi):
                    tap, k = n // 2, n % 2
                    c = 4 * j + 2 * k
                    src = upad[:, c, tap:tap + T]
                    w = col("conv_w_dw_2", DC * tap + c)
                    if tap == 0:
                        dve.wait_ge(s_u, 4 * j + 4)
                        dve.wait_ge(s_edge, 2)
                        nc.vector.tensor_scalar(ucv[:, c, :], src, w, col("conv_b_dw_2", c), ALU.mult, ALU.add).then_inc(s_dwd, 1)
                    else:
                        dve.wait_ge(s_dwd, 2 * TAPS * j + n - 1)
                        nc.vector.scalar_tensor_tensor(ucv[:, c, :], src, w, ucv[:, c, :], ALU.mult, ALU.add).then_inc(s_dwd, 1)

            def rooted(dst, G):
                nc.vector.tensor_tensor(dst[:, :, :], ps[G % 2][:, :, :], rstd.unsqueeze(1).to_broadcast([P, 4, T]), ALU.mult).then_inc(s_free[G % 2], 1)

            per = -(-2 * TAPS // 8)
            for j in range(5):
                for q in range(2, 10):
                    if j < 4:
                        split_lo(0, T_PW1 + 8 * j + q)
                    if j == 0 and q == 3:
                        root(2, EPS1)
                        sv.did(nc.vector.tensor_copy(rstd_first[:, :], rstd[:, :]))
                        sv.wait()
                    if j == 0 and q == 5:
                        root(3, EPS2, rstd_first)
                        sv.did(nc.vector.tensor_tensor(rstd[:, :], rstd[:, :], rstd_first[:, :], ALU.mult))
                        sv.wait()
                    if j == 0 and q > 5:
                        for c in range(4 * (q - 6), 4 * (q - 5)):
                            sv.did(nc.vector.scalar_tensor_tensor(res[:, c, :], res[:, c, :], col("g_final", c), rstd_first[:, :], ALU.mult, ALU.mult))
                    if j < 4 and q == 9:
                        done(0, T_PW1 + 8 * (j + 1))
                        if j:
                            dve.wait_ge(s_u, 4 * j)
                        rooted(pg, G_PW1 + 1)
                    if j == 3 and q == 9:
                        glu(j)
                    if j:
                        taps(j - 1, min(2 * TAPS, (q - 2) * per), min(2 * TAPS, (q - 1) * per))
                    if q == 5 and j < 4:
                        done(0, T_PW1 + 8 * j + 4)
                        rooted(pa, G_PW1)
                if j < 3:
                    glu(j)
            dve.wait_ge(s_mean, 1)
            sv.did(nc.vector.tensor_copy(nwt[:, :], bank_o[:, 0:T]))
            sv.wait()
            for j in range(4):
                nc.vector.tensor_tensor(ucv[:, 4 * j:4 * j + 4, :], ucv[:, 4 * j:4 * j + 4, :], nwt[:, :].unsqueeze(1).to_broadcast([P, 4, T]),
                                        ALU.subtract).then_inc(s_xc, 1)
            root(4, EPS2)

            def scaled(c):
                nc.vector.scalar_tensor_tensor(sq[:, c % 4, :], ucv[:, c, :], col("conv_ln_g_2", c), rstd[:, :], ALU.mult, ALU.mult).then_inc(s_nt, 1)
            for c in range(3):
                scaled(c)
            for c in range(DC):
                if c + 3 < DC:
                    if c:
                        dve.wait_ge(s_y, 2 * c)
                    scaled(c + 3)
                dve.wait_ge(s_y, 2 * c + 2)
                nc.vector.tensor_tensor(xl[:, c, :], ucv[:, c, :], xh[:, c, :].bitcast(F32), ALU.subtract).then_inc(s_h, 1)
            for j in range(4):
                for q in range(2, 6):
                    split_lo(0, T_PW2 + 4 * j + q)
                    if j == 3 and q < 5:
                        gained_lo(range(4 * (q - 2), 4 * (q - 1)), 3, lambda c: col("norm_ffn_g_2", c))
                done(0, T_PW2 + 4 * (j + 1))
                for m in range(4):
                    c = 4 * j + m
                    ins = nc.vector.scalar_tensor_tensor(res[:, c, :], ps[(G_PW2 + j) % 2][:, m, :], col("conv_b_pw2_2", c), res[:, c, :], ALU.add, ALU.add)
                ins.then_inc(s_free[(G_PW2 + j) % 2], 1)
            gained_lo(range(12, 16), 3, lambda c: col("norm_ffn_g_2", c))
            def up2(i, half):
                h0 = FC // 4 + 8 * half
                for k in range(2):
                    for q in range(3, 6):
                        split_lo(i * 8, T_UP2[half] + 4 * k + q)
                    par = (G_UP2[half] + k) % 2
                    done(i * 8, T_UP2[half] + 4 * (k + 1))
                    nc.vector.scalar_tensor_tensor(tmp[:, :, :], ps[par][:, :, :], 0.0, rstd.unsqueeze(1).to_broadcast([P, 4, T]),
                                                   ALU.max, ALU.mult).then_inc(s_free[par], 1)
                    dve.wait_ge(s_free[par], i + free_at(G_UP2[half] + k))
                    nc.vector.tensor_tensor(tmp2[:, :, :], tmp[:, :, :], tmp[:, :, :], ALU.mult).then_inc(s_hid, 1)
                    split_lo(i * 8, T_UP2[half] + 4 * k + 6)
                    dve.wait_ge(s_hidh, i * 2 + (h0 + k + 1))
                    nc.vector.tensor_tensor(gl[:, bass.ds(i * 8 + 4 * k, 4), :], tmp2[:, :, :], gh[:, bass.ds(i * 8 + 4 * k, 4), :].bitcast(F32),
                                            ALU.subtract).then_inc(s_hidl, 1)

            for half in range(2):
                split_lo(0, T_UP2[half] + 2)
                if half == 0:
                    root(5, EPS2)
                with dve.Fori(0, 4) as i:
                    up2(i, half)
                for j in range(4):
                    for q in range(2 if j else 3, 10):
                        if T_DN2[half] + 8 * j + q < T_END:
                            split_lo(0, T_DN2[half] + 8 * j + q)
                    par = (G_DN2[half] + j) % 2
                    done(0, T_DN2[half] + 8 * (j + 1))
                    nc.vector.tensor_tensor(res[:, 4 * j:4 * j + 4, :], res[:, 4 * j:4 * j + 4, :], ps[par][:, :, :], ALU.add).then_inc(s_free[par], 1)
            root(6, EPS2)
            for c in range(DC):
                nc.vector.scalar_tensor_tensor(res[:, c, :], res[:, c, :], col("final_norm_g_2", c), rstd[:, :], ALU.mult, ALU.mult).then_inc(s_fin, 1)

        @block.tensor
        def _(pe):
            mm = nc.tensor.matmul
            pe.sem_inc(s_used, SPL)
            pe.sem_inc(s_gemv, 2)

            def three(o, h, l, rh, rl, start, stop):
                mm(o, h, rh, start=start, stop=False, skip_group_check=True)
                mm(o, h, rl, start=False, stop=False, skip_group_check=True)
                return mm(o, l, rh, start=False, stop=stop, skip_group_check=True)

            def piece(g, t, o, rhs, first, last, chunks=None):
                pe.wait_ge(s_lo, g + (RAW + t + 1))
                for c in range(KC):
                    if chunks is not None:
                        pe.wait_ge(s_h, chunks + c + 1)
                    rh, rl = rhs(c)
                    for m in range(4):
                        w = slice(m * P, (m + 1) * P)
                        ins = three(o[:, m, :], whi[t % SPL][:, c, w], wlo[t % SPL][:, c, w], rh, rl,
                                    first and c == 0 and m % 2 == 0, last and c == KC - 1)
                ins.then_inc(s_used, 1)

            def from_x(k):
                return xh[:, k, :], xl[:, k, :]

            def group(g, i, t, G, H, n=4, k0=0, rhs=from_x, each=None, ahead_of=None):
                pe.wait_ge(s_free[G % 2], i + (G // 2 + 1))
                for q in range(n):
                    if ahead_of:
                        ahead_of(q)
                    piece(g, t + q, ps[G % 2], lambda c: rhs(k0 + 4 * q + c), q == 0, q == n - 1, None if H is None else H + k0 + 4 * q)
                    if each:
                        each(q)

            def statistic(k, steps=range(DC // 2)):
                for i in steps:
                    if k in PAIRED:
                        pe.wait_ge(s_acc, 8 * k + i + 1)
                        mm(bank_o[:, 0:T], mean_w[:, :], pair_sum(k, i), start=i == 0, stop=i == 7).then_inc(s_psum, 1)
                        continue
                    pe.wait_ge(s_sq, 8 * k + i + 1)
                    for m in range(2):
                        ins = mm(bank_o[:, 0:T], mean_w[:, :], sq[:, 2 * (i % 2) + m, :], start=i == 0 and m == 0, stop=i == 7 and m == 1)
                    ins.then_inc(s_acc, 1)

            def modulation(g, group, sums=None):
                pe.wait_ge(s_chain, g * DC + DC * (group + 2))
                sums = sums or [mod_sum[sum_of(group)]]
                for m in range(4):
                    for x in sums:
                        ins = mm(bank_m[:, bass.ds(g * 4 + (4 * group + m), 1)], x[:, P * m:P * (m + 1)], ones[:, 0:1],
                                 start=x is sums[0], stop=x is sums[-1])
                ins.then_inc(s_gemv, 1)

            pe.wait_ge(s_in[0], 16)
            pe.wait_ge(s_vin, 16 * len(vec_parts))
            for b in range(3 + DC // 2):
                bank = (bank_z, bank_f)[b % 2]
                if b == 3:
                    pe.wait_ge(s_const, 4)
                    pe.wait_ge(s_posf, 1)
                    mm(bank_o[:, 0:T], ones[0:1, :], posf, start=True, stop=True).then_inc(s_posb, 1)
                    pe.wait_ge(s_in[2], 32)
                if 2 <= b < 5:
                    pe.wait_ge(s_trc, b - 1)
                if b >= 5:
                    pe.wait_ge(s_trx, b - 4)
                for i in range(min(4, VB - 4 * b) if b < 3 else 4):
                    if b < 3:
                        src = att[:, 16 + 4 * b + i, 0:P]
                    else:
                        m, c = 2 * (b - 3) + i // 2, i % 2
                        src = att[:, 8 * c + m // 2, (m % 2) * P:(m % 2 + 1) * P]
                    ins = nc.tensor.transpose(bank[:, P * i:P * (i + 1)], src, ident)
                ins.then_inc(s_tr, 1)
            pe.wait_ge(s_ang, 1)
            statistic(0)
            with pe.Fori(0, ADA_START // 2) as i:
                for par in range(2):
                    modulation(i * 2, par, first_sum[par])
            pe.wait_ge(s_mod, 1)

            BLK = ((0, P), (P, 384))

            def background(t):
                if B_VTA <= t < B_VTA + 4 or B_VTB <= t < B_VTB + 4:
                    j = t - B_VTA if t < B_VTB else t - B_VTB + 4
                    first = 16 + 2 * j if j < 4 else 40 + 2 * (j - 4)
                    G = first // 4
                    pe.wait_ge(s_free[G % 2], free_at(G))
                    if j == 4:
                        pe.wait_ge(s_oc, HEADS)
                    elif j:
                        pe.wait_ge(s_vtc, j)
                    for i in range(4):
                        ins = nc.tensor.transpose(bank_o[:, P * i:P * (i + 1)], att[:, first + i // 2, (i % 2) * P:(i % 2 + 1) * P], ident)
                    ins.then_inc(s_vt, 1)
                h = (t - B_STICK) // 2
                if (t - B_STICK) % 2 == 0 and 0 <= h < HEADS:
                    if h:
                        pe.wait_ge(s_lm, h)
                    mm(bank_z[:, 0:T], att[:, 8 + h, 0:P], att[:, h, :], start=True, stop=True)
                    mm(bank_z[:, T:384], att[:, 8 + h, P:T], att[:, h, P:T], start=True, stop=True).then_inc(s_z, 1)
                if (t - B_STICK) % 2 == 0 and 1 <= h <= HEADS:
                    pe.wait_ge(s_lm, h)
                    if h > 1:
                        pe.wait_ge(s_w, h - 1)
                    mm(bank_f[:, 0:P], tri, tB[:, 0:P], start=True, stop=True)
                    mm(bank_f[:, P:T], tri, tB[:, P:T], start=True, stop=False)
                    mm(bank_f[:, P:T], ones[:, :], tB[:, T:384], start=False, stop=True)
                    mm(bank_f[:, T:384], tri, tB[:, T:384], start=True, stop=True).then_inc(s_af, 1)
                if (t - B_STICK) % 2 == 0 and 2 <= h < HEADS + 2:
                    n = h - 2
                    pe.wait_ge(s_wm, n + 1)
                    pe.wait_ge(s_vtc, 4)
                    if n:
                        pe.wait_ge(s_oc, n)
                    attend(16 + n, tC)
                    last_mm[0].then_inc(s_o, 1)
                if B_ROPE <= t < B_ROPE + 8 or B_ROPEI <= t < B_ROPEI + 5:
                    r = t - B_ROPE if t < B_ROPE + 8 else t - B_ROPEI + 8
                    if r == 0:
                        pe.wait_ge(s_lm, HEADS)
                        pe.wait_ge(s_free[0], free_at(8))
                        pe.wait_ge(s_free[1], free_at(9))
                    else:
                        pe.wait_ge(s_rd, r)
                    if r == 8:
                        pe.wait_ge(s_free[0], free_at(12))
                        pe.wait_ge(s_free[1], free_at(13))
                    if r == 12:
                        pe.wait_ge(s_ki, 2)
                        mm(bank_z[:, 0:T], cons[:, C_SW64:C_SW64 + P], kidx[:, :], start=True, stop=True).then_inc(s_rp, 1)
                    else:
                        first = 24 + 2 * r if r < 8 else 48 + 2 * (r - 8)
                        at = C_SW128 if r < 8 else C_SW64
                        mm(bank_z[:, :], cons[:, at:at + P], ch(first, first + 2), start=True, stop=True).then_inc(s_rp, 1)
                if t == B_ROPEI + 4:
                    pe.wait_ge(s_free[0], free_at(G_SMALL))
                    pe.wait_ge(s_w, HEADS)
                    for b in range(2):
                        ins = nc.tensor.transpose(bank_f[:, IDX_HEADS * b:IDX_HEADS * (b + 1)], wi_t[:, P * b:P * (b + 1)], cons[0:16, C_ID:C_ID + 16])
                    ins.then_inc(s_wt, 1)
                c = t - B_IDX
                if 0 <= c < 8:
                    if c == 0:
                        pe.wait_ge(s_rd, 13)
                        pe.wait_ge(s_wtc, 1)
                    else:
                        pe.wait_ge(s_relu, 2 * c)
                    for k in range(2):
                        half = slice(64 * k, 64 * k + 64)
                        bank = (bank_z, bank_f)[k]
                        mm(bank[:, 0:P], att[half, 48 + c, 0:P], kidx[half, 0:P], start=True, stop=True)
                        ins = mm(bank[:, P:384], att[half, 48 + c, P:T], kidx[half, :], start=True, stop=True)
                    ins.then_inc(s_dots, 1)
                h = t - B_DSA
                if 0 <= h < HEADS:
                    if h:
                        pe.wait_ge(s_lg, 2 * h)
                    else:
                        pe.wait_ge(s_relu, 16)
                    mm(bank_z[:, 0:P], att[:, 24 + h, 0:P], att[:, 32 + h, 0:P], start=True, stop=True)
                    mm(bank_z[:, P:384], att[:, 24 + h, P:T], att[:, 32 + h, :], start=True, stop=True).then_inc(s_L, 1)
                if 1 <= h <= HEADS:
                    pe.wait_ge(s_p, 2 * h)
                    if h > 1:
                        pe.wait_ge(s_ptc, h - 1)
                    for i in range(3):
                        ins = nc.tensor.transpose(bank_f[:, P * i:P * (i + 1)], tE[:, P * i:P * (i + 1)], ident)
                    ins.then_inc(s_pt, 1)
                if 2 <= h < HEADS + 2:
                    n = h - 2
                    pe.wait_ge(s_ptc, n + 1)
                    if n:
                        pe.wait_ge(s_obc, n)
                    else:
                        pe.wait_ge(s_vtc, 8)
                    attend(40 + n, tA)
                    last_mm[0].then_inc(s_ob, 1)

            last_mm = [None]

            def attend(v, w):
                mm(bank_o[:, 0:P], att[:, v, 0:P], w[:, 0:P], start=True, stop=True)
                mm(bank_o[:, P:T], att[:, v, 0:P], w[:, P:T], start=True, stop=False)
                last_mm[0] = mm(bank_o[:, P:T], att[:, v, P:T], w[:, T:384], start=False, stop=True)

            for t in range(T_WAB):
                if t == B_STICK:
                    for par in range(2):
                        pe.wait_ge(s_free[par], free_at(4))
                background(t)
                if t == T_SMALL:
                    pe.wait_ge(s_free[G_SMALL % 2], G_SMALL // 2 + 1)
                    pe.wait_ge(s_lo, RAW + t + 1)
                    wh, wl = (x[t % SPL][:, :, :].rearrange("p c n -> p (c n)") for x in (whi, wlo))
                    for c in range(DC):
                        w = slice(NSMALL * c, NSMALL * (c + 1))
                        ins = three(ps[G_SMALL % 2][0:NSMALL, 0, :], wh[:, w], wl[:, w], xh[:, c, :], xl[:, c, :], c == 0, c == DC - 1)
                    ins.then_inc(s_used, 1)
                else:
                    G, q = (t // 4, t % 4) if t < T_SMALL else (G_GATE + (t - T_GATE) // 4, (t - T_GATE) % 4)
                    if q == 0:
                        pe.wait_ge(s_free[G % 2], G // 2 + 1)
                    piece(0, t, ps[G % 2], lambda c: from_x(4 * q + c), q == 0, q == 3, H_QKV + 4 * q if G == 0 else None)
                for m in beside(t):
                    if m % 8 == 7:
                        if m // 8 == 5:
                            pe.wait_ge(s_mod, 2)
                        modulation(0, ADA_START + m // 8)
            pe.wait_ge(s_mod, 3)
            with pe.Fori(0, 2) as g:
                for e in range(2):
                    for k in range(2):
                        group(g * 8, g * 2 + e, T_WAB + 4 * e + 2 * k, G_WAB + k, H_CAT, n=2, k0=8 * k)
                modulation(g, ADA_START + M_LATE // 8)
            def wo_each(j):
                def each(q):
                    for m in beside(T_WO + 4 * j + q - 1) if j or q else ():
                        if m % 8 == 7:
                            modulation(0, ADA_START + m // 8)
                return each
            for j in range(4):
                group(0, 0, T_WO + 4 * j, G_WO + j, H_MRG, each=wo_each(j))
                if j:
                    statistic(1, (2 * j - 2, 2 * j - 1))
            modulation(0, ADA_GROUPS - 1)
            statistic(1, (6, 7))
            for u in range(2):
                with pe.Fori(0, UPN[u]) as i:
                    for k in range(2):
                        group(i * 8, i, T_UP[u] + 4 * k, G_UP[u] + k, H_UP)

                def hidden(r, first):
                    pe.wait_ge(s_hidl, r + (UPN[0] * u + 2))
                    for q in range(4):
                        if first and q < 2:
                            pe.wait_ge(s_free[(G_DOWN[u] + q) % 2], (G_DOWN[u] + q) // 2 + 1)
                        if first and u and q == 2:
                            pe.wait_ge(s_dn, 2)
                        piece(r * 4, T_DOWN[u] + q, down_psum[q],
                              lambda c: (fh[:, bass.ds(r * 4 + c, 1), :], fl[:, bass.ds(r * 4 + c, 1), :]), first, True)

                hidden(0, True)
                with pe.Fori(1, UPN[u]) as r:
                    hidden(r, False)

            def second_block_norms(q):
                if q == 1:
                    pe.wait_ge(s_dn, 4)
                    statistic(2)
                if q == 3:
                    statistic(3)

            for j in range(4):
                for k in range(2):
                    group(0, 0, T_PW1 + 8 * j + 4 * k, G_PW1 + 2 * j + k, H_PW1, each=None if j or k else second_block_norms)
            def mean(j):
                pe.wait_ge(s_dwd, 2 * TAPS * (j + 1))
                if j < 3:
                    pe.wait_ge(s_padd, 2 * TAPS * (j + 1))
                else:
                    pe.wait_ge(s_dwtc, 2)
                for c in range(4 * j, 4 * j + 4):
                    ins = mm(bank_o[:, 0:T], mean_w[:, :], ucv[:, c, :], start=c == 0, stop=c == DC - 1)
                return ins

            mean(0)
            mean(1)
            pe.wait_ge(s_u, DC)
            pe.wait_ge(s_edge, 2)
            for n in range(2 * TAPS):
                k, tap = n // TAPS, n % TAPS
                pe.wait_ge(s_diag, n + 1)
                mm(ms[0][:, 2 * k, :], diag[:, n % NDIAG, :], upad[:, DC - 3 + 2 * k, tap:tap + T],
                   start=tap == 0, stop=tap == TAPS - 1).then_inc(s_diagu, 1)
                if tap == TAPS - 1:
                    pe.wait_ge(s_diagu, n + 1)
                    pe.sem_inc(s_dwt, 1)
            mean(2)
            mean(3).then_inc(s_mean, 1)
            statistic(4)
            for j in range(4):
                group(0, 0, T_PW2 + 4 * j, G_PW2 + j, H_PW2)
                if j:
                    statistic(5, (2 * j - 2, 2 * j - 1))

            def up2(i, half, each=None):
                for k in range(2):
                    group(i * 8, i, T_UP2[half] + 4 * k, G_UP2[half] + k, H_UP2, each=None if k else each)
            for half in range(2):
                if half == 0:
                    up2(0, 0, lambda q: statistic(5, (6, 7)) if q == 0 else None)
                with pe.Fori(1 - half, 4) as i:
                    up2(i, half)
                def hidden_ready(q):
                    pe.wait_ge(s_hidl, FC // 4 + 8 * half + q + 2)

                for j in range(4):
                    group(0, 0, T_DN2[half] + 8 * j, G_DN2[half] + j, None, n=8, rhs=lambda c: (gh[:, c, :], gl[:, c, :]),
                          ahead_of=None if j else hidden_ready)
                    if half and j:
                        statistic(6, (2 * j - 2, 2 * j - 1))
            statistic(6, (6, 7))
            for b in range(8):
                c, j = b // 4, b % 4
                pe.wait_ge(s_fin, DC if c else 4 * (j + 1))
                if b >= 4:
                    pe.wait_ge(s_fc, b - 3)
                for m in range(4):
                    ins = nc.tensor.transpose(out_banks[b % 4][:, P * m:P * (m + 1)], res[:, 4 * j + m, P * c:P * (c + 1)], ident)
                ins.then_inc(s_ft, 1)
    return nc


INPUTS = ["x", "c", "positions", "w_in", "w_a", "w_b", "w_o", "w_ada", "b_ada", "g_mix", "g_ffn", "w_up", "conv_w", "conv_b",
          "w_down", "g_final", "norm_mix_g_2", "norm_ffn_g_2", "final_norm_g_2", "conv_w_pw1_2", "conv_b_pw1_2", "conv_w_dw_2",
          "conv_b_dw_2", "conv_ln_g_2", "conv_ln_b_2", "conv_w_pw2_2", "conv_b_pw2_2", "ffn_w_up_2", "ffn_w_down_2"]


def kernel(**inputs):
    import concourse.bacc as bacc
    from concourse.bass_utils import run_bass_kernel_spmd

    nc = bacc.Bacc("TRN2", target_bir_lowering=False, num_devices=1)
    arrays = {name: np.ascontiguousarray(inputs[name]) for name in INPUTS}
    arrays["consts"] = shape_constants()
    aps = {name: nc.dram_tensor(f"in_{name}", a.shape, mybir.dt.from_np(a.dtype), kind="ExternalInput").ap() for name, a in arrays.items()}
    out = nc.dram_tensor("out", (1, T, D), F32, kind="ExternalOutput").ap()
    build(nc, aps, out)
    r = run_bass_kernel_spmd(nc, [{f"in_{name}": a for name, a in arrays.items()}], core_ids=[0])
    return r.results[0]["out"]
```
